# Optimizing a Trainium2 kernel written in Bass

```python
import functools
import jax, jax.numpy as jnp
from jax import lax
import numpy as np

D_MODEL = 1024
BATCH = 1
SEQ = 512
DEPTH = 1
DEC_BATCH = 8
DEC_SEQ = 1
PAST_LEN = 4096
PAGE_SIZE = 128

A_GROUPS = 4
A_GROUP_W = 128
A_WIDTH = A_GROUPS * A_GROUP_W
CHUNK = 128
B_HEADS = 8
B_HEAD_DIM = 64
B_WIDTH = B_HEADS * B_HEAD_DIM
MOBA_BLOCK = 256
MOBA_TOPK = 3
Q_CHUNK = 8
MIX_WIDTH = A_WIDTH + B_WIDTH
IN_WIDTH = 3 * A_WIDTH + 4 * B_WIDTH
SPLIT_AT = (A_WIDTH, 2 * A_WIDTH, 3 * A_WIDTH, 3 * A_WIDTH + B_WIDTH,
            3 * A_WIDTH + 2 * B_WIDTH, 3 * A_WIDTH + 3 * B_WIDTH)
EPS = 1e-6
NEG = -1e30

kernel_name = "hymba_sgu_moba_alibi_step"

def _rms(x, g):
    xf = x.astype(jnp.float32)
    y = xf * lax.rsqrt(jnp.mean(xf * xf, axis=-1, keepdims=True) + EPS)
    return (y * g.astype(jnp.float32)).astype(x.dtype)

def alibi_slopes():
    return jnp.exp2(-8.0 * jnp.arange(1, B_HEADS + 1, dtype=jnp.float32) / B_HEADS)

def chunk_mlp(u, v, v_gain, w_s, b_s):
    B, T, _ = u.shape
    L = min(T, CHUNK)
    nc = T // L
    vn = _rms(jax.nn.gelu(v).reshape(B, T, A_GROUPS, A_GROUP_W), v_gain)
    w = jnp.tril(w_s[:, :L, :L])
    s = jnp.einsum('gts,bnsgc->bntgc', w, vn.reshape(B, nc, L, A_GROUPS, A_GROUP_W))
    s = s + jnp.swapaxes(b_s[:, :L], 0, 1)[None, None, :, :, None]
    out = jax.nn.gelu(u) * s.reshape(B, T, A_WIDTH)
    return out, vn.reshape(B, T, A_WIDTH)

def moba_prompt(q, k, v):
    f32 = jnp.float32
    B, S, H, D = q.shape
    nb = -(-S // MOBA_BLOCK)
    pad = nb * MOBA_BLOCK - S
    kp = jnp.pad(k, ((0, 0), (0, pad), (0, 0), (0, 0)))
    vp = jnp.pad(v, ((0, 0), (0, pad), (0, 0), (0, 0)))
    kblk = kp.reshape(B, nb, MOBA_BLOCK, H, D).transpose(0, 3, 1, 2, 4)
    vblk = vp.reshape(B, nb, MOBA_BLOCK, H, D).transpose(0, 3, 1, 2, 4)
    qf = jnp.swapaxes(q, 1, 2).astype(f32)
    pos = jnp.arange(S)
    qblk = pos // MOBA_BLOCK
    own = jnp.broadcast_to(qblk[:, None], (B, H, S, 1))
    topk = min(MOBA_TOPK, nb - 1)
    if topk > 0:
        kmean = jnp.mean(kblk.astype(f32), axis=3)
        gate = jnp.einsum('bhsd,bhnd->bhsn', qf, kmean)
        fully_past = jnp.arange(nb)[None, :] < qblk[:, None]
        gate = jnp.where(fully_past, gate, NEG)
        _, sel = lax.top_k(gate, topk)
        sel_ok = sel < qblk[:, None]
        blocks = jnp.concatenate([sel, own], axis=-1)
        ok = jnp.concatenate([sel_ok, jnp.ones((B, H, S, 1), bool)], axis=-1)
    else:
        blocks = own
        ok = jnp.ones((B, H, S, 1), bool)
    nq = S // Q_CHUNK
    slopes = alibi_slopes()[None, :, None, None, None]
    scale = D ** -0.5
    bi = jnp.arange(B)[:, None, None, None]
    hi = jnp.arange(H)[None, :, None, None]

    def to_chunks(a):
        return jnp.moveaxis(a.reshape(B, H, nq, Q_CHUNK, *a.shape[3:]), 2, 0)

    def step(args):
        qc, bc, okc, tc = args
        kg = kblk[bi, hi, bc]
        vg = vblk[bi, hi, bc]
        s = jnp.einsum('bhqd,bhqnjd->bhqnj', qc, kg.astype(f32)) * scale
        kpos = bc[..., None] * MOBA_BLOCK + jnp.arange(MOBA_BLOCK)
        dist = (tc[None, None, :, None, None] - kpos).astype(f32)
        s = jnp.where(okc[..., None] & (dist >= 0), s - slopes * dist, NEG)
        p = jax.nn.softmax(s.reshape(B, H, Q_CHUNK, -1), axis=-1).reshape(s.shape)
        return jnp.einsum('bhqnj,bhqnjd->bhqd', p.astype(vg.dtype), vg)

    o = lax.map(step, (to_chunks(qf), to_chunks(blocks), to_chunks(ok), pos.reshape(nq, Q_CHUNK)))
    o = jnp.moveaxis(o, 0, 2).reshape(B, H, S, D)
    return jnp.swapaxes(o, 1, 2).reshape(B, S, H * D).astype(q.dtype)

def moba_sample(q, k, v, cache_k, cache_v, page_table):
    f32 = jnp.float32
    Bd, T, H, D = q.shape
    n_pages = page_table.shape[1]
    past = n_pages * PAGE_SIZE
    ppb = MOBA_BLOCK // PAGE_SIZE
    n_full = past // MOBA_BLOCK
    own_first = n_full * ppb
    slopes = alibi_slopes()[None, :, None, None]
    scale = D ** -0.5
    qf = jnp.swapaxes(q, 1, 2).astype(f32)
    tpos = past + jnp.arange(T)
    scores, values = [], []
    s_new = jnp.einsum('bhtd,bjhd->bhtj', qf, k.astype(f32)) * scale
    dist = (tpos[:, None] - tpos[None, :]).astype(f32)
    scores.append(jnp.where(dist >= 0, s_new - slopes * dist, NEG))
    values.append(('bhtj,bjhd->bhtd', v))
    if own_first < n_pages:
        pages = page_table[:, own_first:]
        ko = cache_k[pages].reshape(Bd, -1, H, D)
        vo = cache_v[pages].reshape(Bd, -1, H, D)
        kpos = own_first * PAGE_SIZE + jnp.arange(ko.shape[1])
        s = jnp.einsum('bhtd,bjhd->bhtj', qf, ko.astype(f32)) * scale
        scores.append(s - slopes * (tpos[:, None] - kpos[None, :]).astype(f32))
        values.append(('bhtj,bjhd->bhtd', vo))
    topk = min(MOBA_TOPK, n_full)
    if topk > 0:
        k_full = cache_k[page_table[:, :own_first]].astype(f32).reshape(Bd, n_full, MOBA_BLOCK, H, D)
        kmean = jnp.mean(k_full, axis=2)
        gate = jnp.einsum('bhtd,bnhd->bhtn', qf, kmean)
        _, sel = lax.top_k(gate, topk)
        pidx = sel[..., None] * ppb + jnp.arange(ppb)
        pages = page_table[jnp.arange(Bd)[:, None, None, None, None], pidx]
        hidx = jnp.arange(H)[None, :, None, None, None]
        kg = cache_k[pages, :, hidx].reshape(Bd, H, T, topk * MOBA_BLOCK, D)
        vg = cache_v[pages, :, hidx].reshape(Bd, H, T, topk * MOBA_BLOCK, D)
        kpos = (sel[..., None] * MOBA_BLOCK + jnp.arange(MOBA_BLOCK)).reshape(Bd, H, T, -1)
        s = jnp.einsum('bhtd,bhtkd->bhtk', qf, kg.astype(f32)) * scale
        scores.append(s - slopes * (tpos[None, None, :, None] - kpos).astype(f32))
        values.append(('bhtk,bhtkd->bhtd', vg))
    sizes = [s.shape[-1] for s in scores]
    p = jax.nn.softmax(jnp.concatenate(scores, axis=-1), axis=-1)
    terms, off = [], 0
    for (spec, val), n in zip(values, sizes):
        terms.append(jnp.einsum(spec, p[..., off:off + n].astype(val.dtype), val))
        off += n
    out = functools.reduce(jnp.add, terms)
    return jnp.swapaxes(out, 1, 2).reshape(Bd, T, H * D).astype(q.dtype)

def _layer(x, attend, g_pre, w_in, sgu_gain, sgu_w, sgu_b, g_branch_a, g_branch_b, w_out, g_post):
    B, T, _ = x.shape
    h = _rms(x, g_pre)
    z = jnp.einsum('btd,df->btf', h, w_in)
    ua, va, ga, qb, kb, vb, gb = jnp.split(z, SPLIT_AT, axis=-1)
    ya, v_rows = chunk_mlp(ua, va, sgu_gain, sgu_w, sgu_b)
    kh = kb.reshape(B, T, B_HEADS, B_HEAD_DIM)
    vh = vb.reshape(B, T, B_HEADS, B_HEAD_DIM)
    yb = attend(qb.reshape(B, T, B_HEADS, B_HEAD_DIM), kh, vh)
    ya = _rms(ya, g_branch_a) * jax.nn.silu(ga)
    yb = _rms(yb, g_branch_b) * jax.nn.silu(gb)
    y = jnp.einsum('btf,fd->btd', jnp.concatenate([ya, yb], axis=-1), w_out)
    return x + _rms(y, g_post), kh, vh, v_rows

def setup_inputs(seed: int = 0) -> dict:
    key = jax.random.key(seed)
    ks = jax.random.split(key, 16)
    n_pages = PAST_LEN // PAGE_SIZE
    n_used = DEC_BATCH * n_pages
    n_phys = (n_used * 5 + 3) // 4
    perm = jax.random.permutation(ks[0], n_phys)
    page_table = perm[:n_used].reshape(DEC_BATCH, n_pages).astype(jnp.int32)
    nrm = jax.random.normal
    return {
        "x_prompt": nrm(ks[1], (BATCH, SEQ, D_MODEL), jnp.float32),
        "x_sample": nrm(ks[2], (DEC_BATCH, DEC_SEQ, D_MODEL), jnp.float32),
        "cache_k": nrm(ks[3], (DEPTH, n_phys, PAGE_SIZE, B_HEADS, B_HEAD_DIM), jnp.float32),
        "cache_v": nrm(ks[4], (DEPTH, n_phys, PAGE_SIZE, B_HEADS, B_HEAD_DIM), jnp.float32),
        "page_table": page_table,
        "g_pre": 1.0 + 0.05 * nrm(ks[5], (DEPTH, D_MODEL), jnp.float32),
        "w_in": nrm(ks[6], (DEPTH, D_MODEL, IN_WIDTH), jnp.float32) * D_MODEL ** -0.5,
        "sgu_gain": 1.0 + 0.05 * nrm(ks[7], (DEPTH, A_GROUPS, A_GROUP_W), jnp.float32),
        "sgu_w": nrm(ks[8], (DEPTH, A_GROUPS, CHUNK, CHUNK), jnp.float32) * CHUNK ** -0.5,
        "sgu_b": 1.0 + 0.1 * nrm(ks[9], (DEPTH, A_GROUPS, CHUNK), jnp.float32),
        "g_branch_a": 1.0 + 0.05 * nrm(ks[10], (DEPTH, A_WIDTH), jnp.float32),
        "g_branch_b": 1.0 + 0.05 * nrm(ks[11], (DEPTH, B_WIDTH), jnp.float32),
        "w_out": nrm(ks[12], (DEPTH, MIX_WIDTH, D_MODEL), jnp.float32) * MIX_WIDTH ** -0.5,
        "g_post": 1.0 + 0.05 * nrm(ks[13], (DEPTH, D_MODEL), jnp.float32),
    }

def reference(x_prompt, x_sample, cache_k, cache_v, page_table, g_pre, w_in, sgu_gain, sgu_w,
              sgu_b, g_branch_a, g_branch_b, w_out, g_post):
    yp, ys = x_prompt, x_sample
    kp_l, vp_l, ks_l, vs_l, sv_l = [], [], [], [], []
    for l in range(DEPTH):
        params = (g_pre[l], w_in[l], sgu_gain[l], sgu_w[l], sgu_b[l],
                  g_branch_a[l], g_branch_b[l], w_out[l], g_post[l])
        yp, kp, vp, _ = _layer(yp, moba_prompt, *params)
        attend_s = functools.partial(moba_sample, cache_k=cache_k[l], cache_v=cache_v[l],
                                     page_table=page_table)
        ys, kn, vn, sv = _layer(ys, attend_s, *params)
        kp_l.append(kp); vp_l.append(vp); ks_l.append(kn); vs_l.append(vn); sv_l.append(sv)
    k_prompt = jnp.stack(kp_l, 0)
    v_prompt = jnp.stack(vp_l, 0)
    k_sample = jnp.stack(ks_l, 0)
    v_sample = jnp.stack(vs_l, 0)
    sgu_v_sample = jnp.stack(sv_l, 0)
    return (yp, ys, k_prompt, v_prompt, k_sample, v_sample, sgu_v_sample)


_drawn_inputs = setup_inputs


def setup_inputs(seed=0):
    import zlib

    import numpy as np

    out = dict(_drawn_inputs(seed))
    spreads = {}
    factors = {}
    for name, (base, spread) in spreads.items():
        noise = np.random.default_rng([zlib.crc32(name.encode()), seed]).standard_normal(out[name].shape)
        drawn = base * np.exp(spread * noise) if base else spread * noise
        out[name] = __import__('jax').numpy.asarray(drawn.astype(out[name].dtype))
    for name, factor in factors.items():
        out[name] = (out[name] * factor).astype(out[name].dtype)
    return out
```

```python
import concourse.bass as bass
import concourse.mybir as mybir
from contextlib import ExitStack

F32 = mybir.dt.float32
BF16 = mybir.dt.bfloat16
I32 = mybir.dt.int32
U32 = mybir.dt.uint32
ALU = mybir.AluOpType
ACT = mybir.ActivationFunctionType
AX = mybir.AxisListType

P = 128
D = 1024
KC = D // P
SEQ = 512
NT = SEQ // P
B = 8
H, HD = 8, 64
W = 512
G = 4
PAST = 4096
PAGE = 128
NPAGE = PAST // PAGE
BLK = 256
NB = PAST // BLK
TOP = 3
ROWS = PAGE // 2
EPS = 1e-6
SCALE = HD ** -0.5
NEG = -1e30
RING = 4096
SLOPES = [2.0 ** -(h + 1) for h in range(H)]
CHUNKS = ["q", "k", "v", "u", "va", "ga", "gb"]
COL = {"u": 0, "va": 1, "ga": 2, "q": 3, "k": 4, "v": 5, "gb": 6}
SP_HEADS = 6


def make_schedule():
    att = []
    pairs = [(h, i) for h in range(H) for i in range(NT)]
    for a in range(len(pairs) + 2):
        if a < len(pairs):
            att.append(("qk",) + pairs[a])
        if 1 <= a <= len(pairs):
            att.append(("ptr",) + pairs[a - 1])
        if a >= 2:
            att.append(("pv",) + pairs[a - 2])
    pre = [("wt",)] + [("xn", t) for t in range(NT)] + [("xs",)]
    out = []

    def chunk(c):
        steps = []
        name = CHUNKS[c]
        for t in range(NT):
            steps.append(("pj", c, t))
            if name == "k" and t >= 1:
                steps.append(("kt", t - 1))
            if name == "va" and t >= 1:
                steps.append(("sg", t - 1))
            if t == 0:
                steps.append(("spj", c))
            if t == 1:
                steps.append(("sfd", c))
            if t == 2 and name == "k":
                steps.append(("sn",))
        if name == "k":
            steps.append(("kt", NT - 1))
        if name == "va":
            steps.append(("sg", NT - 1))
        return steps
    prompt = chunk(0) + chunk(1) + chunk(2)
    rest = chunk(3) + chunk(4) + chunk(5)
    n = 0
    for i, s in enumerate(rest):
        prompt.append(s)
        want = (i + 1) * len(att) // len(rest)
        prompt += att[n:want]
        n = want
    prompt += chunk(6)
    for t in range(NT):
        prompt += [("yt", t, 0), ("yt", t, 1)]
        if t >= 1:
            prompt += [("op", t - 1, 0), ("op", t - 1, 1)]
    prompt += [("op", NT - 1, 0), ("op", NT - 1, 1)]
    cost = {"pj": 7.2, "spj": 1.8, "sfd": 1.0, "kt": .3, "sg": .5, "qk": .6, "ptr": .2, "pv": .4,
            "op": 7.2, "yt": .3, "sn": 0.1}
    events = []
    T0, PERIOD = 8.0, PERIOD_US
    for b in range(B):
        t = T0 + PERIOD * b
        events.append((t, ("qb", b)))
        for n in range(NB):
            events.append((t + 17 + (PERIOD - 18) * (n + 1) / NB, ("km", b, n)))
        e = t + PERIOD
        events.append((e, ("dg", b)))
        for k, nm in enumerate(["gt", "bc"]):
            events.append((e + 2.5 + 3.0 * k, (nm, b)))
        events.append((e + 10, ("sr", b, 0)))
        for k, s in enumerate([("sr", b, 1), ("mt", b), ("mb", b), ("pvd", b)]):
            events.append((e + 15 + 3.0 * k, s))
    events = [(t if s[0] != "qb" or s[1] == 0 else t + 17, s) for t, s in events]
    events.sort(key=lambda x: x[0])
    now, res, k = 0.0, [], 0
    for s in prompt:
        while k < len(events) and events[k][0] <= now:
            res.append(events[k][1])
            k += 1
        res.append(s)
        now += cost[s[0]] + 0.0
    res += [s for _, s in events[k:]]
    first = res.index(("sfd", 0))
    early = [s for s in res[:first] if s[0] == "qb"]
    for s in early:
        res.remove(s)
    first = res.index(("sfd", 0))
    res[first + 1:first + 1] = early
    return pre + res + [("fin0",), ("fin1",), ("fin2",), ("fop", 0), ("ffd", 0), ("fop", 1), ("ffd", 1)]


PERIOD_US = 38.0


def hymba_kernel(nc, x_prompt, x_sample, cache_k, cache_v, page_table, g_pre, w_in, sgu_gain, sgu_w,
                 sgu_b, g_branch_a, g_branch_b, w_out, g_post,
                 y_prompt, y_sample, k_prompt, v_prompt, k_sample, v_sample, sgu_v_sample):
    SCHEDULE = make_schedule()

    pa_use, tp_use = {}, {}
    for s in SCHEDULE:
        if s[0] in ("pj", "sg", "qk", "op"):
            pa_use[s] = len(pa_use)
        if s[0] in ("kt", "ptr", "yt", "wt", "xs", "fin1"):
            tp_use[s] = len(tp_use)
        if s[0] == "xn":
            tp_use[s + (0,)] = len(tp_use)
            tp_use[s + (1,)] = len(tp_use)
        if s[0] == "fin2":
            tp_use[s] = len(tp_use)

    n_phys = cache_k.shape[1]
    k_rows = cache_k.rearrange("l g (p r) h d -> (l g p) (r h d)", r=2)
    v_pages = cache_v.rearrange("l g (p r) h d -> (l g) p r (h d)", r=2)
    x_rows = x_prompt.rearrange("b (t p) d -> (b t) p d", p=P)
    xs_rows = x_sample.rearrange("b t d -> (b t) d")
    y_rows = y_prompt.rearrange("b (t p) d -> (b t) p d", p=P)
    ys_rows = y_sample.rearrange("b t d -> (b t) d")
    kp_rows = k_prompt.rearrange("l b (t p) h d -> (l b t) p (h d)", p=P)
    vp_rows = v_prompt.rearrange("l b (t p) h d -> (l b t) p (h d)", p=P)
    ks_rows = k_sample.rearrange("l b t h d -> (l b t) (h d)")
    vs_rows = v_sample.rearrange("l b t h d -> (l b t) (h d)")
    sv_rows = sgu_v_sample.rearrange("l b t w -> (l b t) w")
    w_in_v = w_in.rearrange("l (k p) n -> p (l k) n", p=P)
    w_out_v = w_out.rearrange("l (k p) n -> p (l k) n", p=P)

    ctx = ExitStack()
    with ctx:
        def sb(name, shape, dt=F32):
            return ctx.enter_context(nc.sbuf_tensor(name, shape, dt))

        def pb(name):
            return ctx.enter_context(nc.psum_tensor(name, [P, 512], F32))

        def sem(name):
            return ctx.enter_context(nc.semaphore(name))

        K = sb("K", [P, NB, 2, W])
        hT = sb("hT", [P, KC, SEQ])
        wbuf = sb("wbuf", [P, 2, KC, W])
        qT = sb("qT", [P, 4, SEQ])
        kT = sb("kT", [P, 4, SEQ])
        v = sb("v", [P, NT, W])
        yb = sb("yb", [P, NT, W])
        ya = sb("ya", [P, NT, W])
        vn = sb("vn", [P, 2, W])
        V = sb("V", [P, H * TOP, 2, HD])
        prod = sb("prod", [P, 4, TOP * 2 * HD])
        qb = sb("qb", [P, W])
        pr = sb("pr", [P, 2, SEQ])
        pT = sb("pT", [P, 2, NT, P])
        junk = sb("junk", [P, D], BF16)
        ident = sb("ident", [P, P])
        alibi = sb("alibi", [P, SEQ])
        gain = sb("gain", [P, W])
        wsT = sb("wsT", [P, G, P])
        slid = sb("slid", [P, 63])
        ones = sb("ones", [P, P])
        gpre = sb("gpre", [P, KC])
        gab = sb("gab", [P, KC])
        sgub = sb("sgub", [P, G])
        hTs = sb("hTs", [P, KC, 32])
        spart = sb("spart", [P, W])
        fold = sb("fold", [P, B])
        qs = sb("qs", [B, W])
        ks = sb("ks", [B, W])
        vs = sb("vs", [B, W])
        yas = sb("yas", [B, W])
        vns = sb("vns", [B, W])
        obs = sb("obs", [B, W])
        osb = sb("osb", [P, B, 2 * HD])
        denr = sb("denr", [1, B, H])
        w00 = sb("w00", [B, G])
        b00 = sb("b00", [B, G])
        msum = sb("msum", [P, 64])
        rstd = sb("rstd", [P, 64])
        nhalf = sb("nhalf", [P, G])
        smax = sb("smax", [P, 2])
        ssum = sb("ssum", [P, H, NT])
        rinv = sb("rinv", [P, NT])
        kidx = sb("kidx", [P, B, NB], U32)
        poff = sb("poff", [P, 1])
        ptb = sb("ptb", [P, B, NB, 2], I32)
        ptbf = sb("ptbf", [P, B, NB, 2])
        iota16 = sb("iota16", [H, NB])
        gsum = sb("gsum", [P, H])
        g16 = sb("g16", [H, NB])
        top8 = sb("top8", [H, 8])
        topi = sb("topi", [H, 8], U32)
        vals = sb("vals", [H, TOP, 3])
        oneh = sb("oneh", [H, TOP, NB])
        ohp = sb("ohp", [H, TOP, 2, NB])
        spread = sb("spread", [H, H, TOP * 3])
        seln = sb("seln", [P, H, TOP])
        selni = sb("selni", [1, H * TOP], I32)
        selpi = sb("selpi", [1, H * TOP * 2], I32)
        sc = sb("sc", [P, H, TOP, 2])
        sbias = sb("sbias", [P, H, TOP])
        calibi = sb("calibi", [P, H, 2])
        dist = sb("dist", [P, 2])
        slope256 = sb("slope256", [P, H])
        mx = sb("mx", [P, H])
        mrow = sb("mrow", [H, 1])
        MT = sb("MT", [H, B])
        dgm = sb("dgm", [H, H])
        pex = sb("pex", [P, H, TOP, 2])
        psm = sb("psm", [P, H])
        sn = sb("sn", [B, H])
        snT = sb("snT", [H, B])
        pnT = sb("pnT", [H, B])
        pn = sb("pn", [B, H])
        den = sb("den", [B, H])

        PA = [pb("PA0"), pb("PA1")]
        TP = [pb("TP0"), pb("TP1")]
        PO = pb("PO")
        SM = pb("SM")
        KM = pb("KM")
        DC = pb("DC")

        s_xt = [sem(f"x_loaded{t}") for t in range(NT)]
        s_xs = sem("xs_loaded")
        s_w = [sem("w_loaded0"), sem("w_loaded1")]
        s_ws = sem("sgu_w_loaded")
        s_small = sem("small_loaded")
        s_gain = sem("gains_loaded")
        s_pt = sem("page_table_loaded")
        s_const = sem("constants_made")
        s_kidx = sem("k_index_made")
        s_k = [sem(f"k_block_loaded{n}") for n in range(NB)]
        s_km = sem("k_block_summed")
        s_v = sem("v_rows_loaded")
        s_store = sem("stored")
        s_dve = sem("dve_done")
        s_act = sem("act_done")
        s_pool = sem("pool_done")
        s_ms = sem("mean_square_ready")
        s_rs = sem("rstd_ready")
        pa_full = [sem("pa_full0"), sem("pa_full1")]
        pa_free = [sem("pa_free0"), sem("pa_free1")]
        tp_full = [sem("tp_full0"), sem("tp_full1")]
        tp_free = [sem("tp_free0"), sem("tp_free1")]
        sm_full, sm_free = sem("sm_full"), sem("sm_free")
        km_full, km_free = sem("km_full"), sem("km_free")
        dc_full, dc_free = sem("dc_full"), sem("dc_free")
        po_free = sem("po_free")
        s_ptused = sem("p_transposed_used")
        s_vns_stored = sem("vns_stored")
        s_sq = sem("out_squared")
        s_xn = sem("x_scaled")
        s_vn = sem("vn_ready")
        s_pmax = sem("prompt_max_ready")
        s_pexp = sem("prompt_exp_ready")
        s_ydone = sem("y_gated")
        s_vrow_stored = sem("v_rows_stored")
        s_krow_stored = sem("k_rows_stored")
        s_snr = sem("sn_ready")
        s_gs = sem("gsum_ready")
        s_spr = sem("spread_ready")
        s_sel = sem("selection_ready")
        s_mul = sem("k_times_q_ready")
        s_red = sem("k_times_q_reduced")
        s_mxr = sem("decode_max_ready")
        s_dgm = sem("max_diag_ready")
        s_pex = sem("decode_exp_ready")
        s_psm = sem("decode_sum_ready")
        s_obs = sem("decode_rows_gathered")
        s_yas = sem("yas_ready")
        s_fin0 = sem("new_token_steps")
        s_sout = sem("sample_out_ready")
        s_vns = sem("vns_ready")
        s_xres = sem("x_residual_loaded")
        s_yo = sem("y_tile_ready")
        s_fin = sem("fin_ready")
        s_pnT = sem("pnT_ready")

        block = ctx.enter_context(nc.Block())

        x_tile = [ya[:, 0:2, :], ya[:, 2:4, :], yb[:, 0:2, :], yb[:, 2:4, :]]
        xs_sb = prod[0:B, :, :].rearrange("p a b -> p (a b)")[:, 0:D]
        xs2_sb = prod[0:B, 0:4, 0:256]
        xres = [qT[:, 0:2, :], qT[:, 2:4, :], kT[:, 0:2, :], kT[:, 2:4, :]]
        gpost = v[:, 0:2, :].rearrange("p a b -> p (a b)")
        ws_rows = pr[:, 0, :].rearrange("p (g s) -> p g s", g=G)
        WCH = len(CHUNKS) + 2
        krow_t = [yb[:, t, :] for t in range(NT)]

        def w_src(c):
            if c < len(CHUNKS):
                o = COL[CHUNKS[c]] * W
                return w_in_v[:, :, o:o + W]
            return w_out_v[:, :, (c - len(CHUNKS)) * W:(c - len(CHUNKS) + 1) * W]

        def wait_full(eng, full, n):
            eng.wait_ge(full[n % 2], n // 2 + 1)

        def wait_evac(eng, step):
            n = pa_use[step]
            eng.wait_ge(pa_free[n % 2], n // 2 + 1)

        def wait_tp_evac(eng, key):
            n = tp_use[key]
            eng.wait_ge(tp_free[n % 2], n // 2 + 1)

        def wait_free(eng, free, n):
            if n >= 2:
                eng.wait_ge(free[n % 2], n // 2)

        DCN = ["qb", "gt", "bc", "mt", "mb", "pvd"]
        dc_use, dc_order = {}, []
        for s in SCHEDULE:
            if s[0] in DCN or s[0] in ("sn", "fin0"):
                dc_use[s] = len(dc_use)

        def fetch_v(eng, b, heads, name):
            eng.wait_ge(s_sel, b + 1)
            if b > 0:
                eng.wait_ge(dc_full, dc_use[("pvd", b - 1)] + 1)
            for h in heads:
                regs = [eng.alloc_register(f"{name}{b}_{h}_{i}") for i in range(TOP * 2)]
                eng.load(regs, selpi[0:1, h * TOP * 2:(h + 1) * TOP * 2])
                for i in range(TOP * 2):
                    page = eng.snap(regs[i], min_val=0, max_val=n_phys - 1)
                    half = (i % 2) * ROWS
                    eng.dma_start(V[half:half + ROWS, h * TOP + i // 2, :, :],
                                  v_pages[bass.ds(page, 1), :, :, h * HD:(h + 1) * HD]
                                  .rearrange("a p r d -> p (a r) d")).then_inc(s_v, 16)
                for r in regs:
                    eng.free_register(r)

        @block.sync
        def _(sp):
            for t in range(NT):
                sp.dma_start(x_tile[t], x_rows[t].rearrange("p (a b) -> p a b", a=2)).then_inc(s_xt[t], 16)
            sp.dma_start(ws_rows, sgu_w.rearrange("l g t s -> t (l g) s")).then_inc(s_ws, 16)
            sp.dma_start(xs_sb, xs_rows).then_inc(s_xs, 16)
            sp.dma_start(wbuf[:, 0, :, :], w_src(0)).then_inc(s_w[0], 16)
            sp.dma_start(wbuf[:, 1, :, :], w_src(1)).then_inc(s_w[1], 16)
            for s in SCHEDULE:
                if (s[0] == "pj" and s[2] == NT - 1 and s[1] + 2 < WCH):
                    c = s[1] + 2
                    wait_full(sp, pa_full, pa_use[s])
                    sp.dma_start(wbuf[:, c % 2, :, :], w_src(c)).then_inc(s_w[c % 2], 16)
                if s[0] == "pj" and CHUNKS[s[1]] == "k":
                    t = s[2]
                    wait_evac(sp, s)
                    sp.dma_start(kp_rows[t], krow_t[t]).then_inc(s_krow_stored, 16)
                if s[0] == "pj" and CHUNKS[s[1]] == "v":
                    t = s[2]
                    wait_evac(sp, s)
                    sp.dma_start(vp_rows[t], v[:, t, :]).then_inc(s_vrow_stored, 16)
                if s[0] == "sfd" and CHUNKS[s[1]] in ("k", "v"):
                    sp.wait_ge(sm_free, 2 * s[1] + 2)
                    if CHUNKS[s[1]] == "k":
                        sp.dma_start(ks_rows, ks[:, :]).then_inc(s_krow_stored, 16)
                    else:
                        sp.dma_start(vs_rows, vs[:, :]).then_inc(s_vrow_stored, 16)
                if s[0] == "sfd" and CHUNKS[s[1]] == "va":
                    sp.wait_ge(s_vns, 1)
                    sp.dma_start(sv_rows, vns[:, :]).then_inc(s_vns_stored, 16)
                if s[0] == "bc":
                    fetch_v(sp, s[1], range(SP_HEADS), "vs")
                if s == ("pv", H - 1, NT - 1):
                    sp.wait_ge(s_ptused, H * NT)
                    for t in range(NT):
                        sp.dma_start(xres[t], x_rows[t].rearrange("p (a b) -> p a b", a=2)).then_inc(s_xres, 16)
                    sp.dma_start(gpost, g_post.broadcast_to([P, D])).then_inc(s_xres, 16)
                if s[0] == "op" and s[2] == 1:
                    t = s[1]
                    sp.wait_ge(s_yo, t + 1)
                    sp.dma_start(y_rows[t], xres[t].rearrange("p a b -> p (a b)")).then_inc(s_store, 16)
                if s == ("pvd", B - 1):
                    sp.wait_ge(dc_free, dc_use[s] + 1)
                    for j in range(4):
                        sp.dma_start(obs[:, :].rearrange("b (t j d) -> b t j d", t=2, j=4)[:, :, j, :],
                                     osb[32 * j:32 * j + 1, :, :].rearrange("a b (t d) -> a b t d", t=2)
                                     ).then_inc(s_obs, 16)
                    sp.dma_start(den[:, :], denr[:, :, :]).then_inc(s_obs, 16)
                    sp.dma_start(xs2_sb, xs_rows.rearrange("b (a c) -> b a c", a=4)).then_inc(s_obs, 16)
            sp.wait_ge(s_sout, 1)
            sp.dma_start(ys_rows.rearrange("b (a c) -> b a c", a=4), xs2_sb).then_inc(s_store, 16)
            sp.wait_ge(s_krow_stored, 16 * (NT + 1))
            sp.wait_ge(s_vns_stored, 16)
            sp.wait_ge(s_vrow_stored, 16 * (NT + 1))
            sp.wait_ge(s_store, 16 * (NT + 1))

        @block.gpsimd
        def _(pool):
            n_pool = [0]

            def link(ins):
                n_pool[0] += 1
                ins.then_inc(s_pool, 1)
                pool.wait_ge(s_pool, n_pool[0])

            pool.dma_start(ptb[:, :, :, :].rearrange("p b n j -> p (b n j)"),
                           page_table.rearrange("(a b) n -> a (b n)", a=1).broadcast_to([P, B * NPAGE])).then_inc(s_pt, 16)
            link(pool.iota(poff[:, :], [[0, 1]], base=0, channel_multiplier=1, allow_small_or_imprecise_dtypes=True))
            link(pool.tensor_scalar_add(poff[ROWS:P, :], poff[ROWS:P, :], -float(ROWS)))
            pool.wait_ge(s_pt, 16)
            link(pool.tensor_copy(ptbf[:, :, :, :], ptb[:, :, :, :]))
            for j in range(2):
                p0 = j * ROWS
                link(pool.tensor_scalar(kidx[p0:p0 + ROWS, :, :], ptbf[p0:p0 + ROWS, :, :, j], float(ROWS),
                                        poff[p0:p0 + ROWS, 0:1], ALU.mult, ALU.add))

            def load_k(b, n):
                if b > 0:
                    pool.wait_ge(s_km, NB * (b - 1) + n + 1)
                pool.indirect_dma_start(K[:, n, :, :].rearrange("p r w -> p (r w)"), None, k_rows,
                                        bass.IndirectOffsetOnAxis(ap=kidx[:, b, n:n + 1], axis=0)
                                        ).then_inc(s_k[n], 16)

            for n in range(4):
                load_k(0, n)
            link(pool.memset(ident[:, :], 0.0))
            link(pool.affine_select(out=ident[:, :], in_=ident[:, :], compare_op=ALU.not_equal, fill=1.0,
                                    base=0, pattern=[[-1, P]], channel_multiplier=1))
            link(pool.memset(ones[:, :], 1.0))
            link(pool.memset(nhalf[:, :], -0.5))
            link(pool.memset(slid[:, :], 0.0))
            link(pool.memset(slid[:, 31:32], 1.0))
            link(pool.memset(hTs[:, :, :], 0.0))
            link(pool.memset(fold[:, :], 0.0))
            for j in range(4):
                link(pool.affine_select(out=fold[:, :], in_=fold[:, :], compare_op=ALU.not_equal, fill=1.0,
                                        base=-32 * j, pattern=[[-1, B]], channel_multiplier=1))
            link(pool.iota(alibi[:, :], [[1, SEQ]], base=-(SEQ - P), channel_multiplier=-1,
                           allow_small_or_imprecise_dtypes=True))
            link(pool.affine_select(out=alibi[:, :], in_=alibi[:, :], compare_op=ALU.is_ge, fill=NEG,
                                    base=SEQ - P, pattern=[[-1, SEQ]], channel_multiplier=1))
            link(pool.iota(dist[:, :], [[1, 2]], base=-PAST, channel_multiplier=2,
                           allow_small_or_imprecise_dtypes=True))
            for h in range(H):
                link(pool.tensor_scalar(calibi[:, h, :], dist[:, :], SLOPES[h], None, ALU.mult))
                link(pool.memset(slope256[:, h:h + 1], SLOPES[h] * BLK))
            link(pool.iota(iota16[:, :], [[1, NB]], base=0, channel_multiplier=0,
                           allow_small_or_imprecise_dtypes=True))
            pool.wait_ge(s_ws, 16)
            for g in range(G):
                link(pool.affine_select(out=ws_rows[:, g, :], in_=ws_rows[:, g, :], compare_op=ALU.is_ge,
                                        fill=0.0, base=0, pattern=[[-1, P]], channel_multiplier=1))
            pool.wait_ge(s_small, 16 * 7)
            pool.memset(osb[:, :, :], 0.0).then_inc(s_const, 1)
            for n in range(4, NB):
                load_k(0, n)

            n_ms = [0]

            def make_rstd(rows, col, n=1):
                n_ms[0] += 1
                pool.wait_ge(s_ms, n_ms[0])
                at = slice(col, col + n)
                link(pool.tensor_scalar_add(rstd[0:rows, at], msum[0:rows, at], EPS))
                pool.tensor_tensor(rstd[0:rows, at], rstd[0:rows, at], nhalf[0:rows, 0:n], ALU.pow).then_inc(s_rs, 1)

            for s in SCHEDULE:
                if s[0] == "xn":
                    make_rstd(P, s[1])
                if s[0] == "xs":
                    make_rstd(B, 4)
                if s[0] == "pj" and CHUNKS[s[1]] == "va":
                    make_rstd(P, 8 + 4 * s[2], 4)
                if s[0] == "pj" and CHUNKS[s[1]] == "ga":
                    make_rstd(P, 24 + s[2])
                if s[0] == "pj" and CHUNKS[s[1]] == "gb":
                    make_rstd(P, 28 + s[2])
                if s[0] == "sfd" and CHUNKS[s[1]] == "va":
                    make_rstd(B, 32, 4)
                if s[0] == "sfd" and CHUNKS[s[1]] == "ga":
                    make_rstd(B, 36)
                if s[0] == "op" and s[2] == 1:
                    make_rstd(P, 41 + 2 * s[1])
                if s[0] == "fin2":
                    make_rstd(B, 37)
                if s == ("ffd", 1):
                    make_rstd(B, 39)
                if s[0] == "bc":
                    b = s[1]
                    pool.wait_ge(s_sel, b + 1)
                    for h in range(H):
                        regs = [pool.alloc_register(f"n{b}_{h}_{i}") for i in range(TOP)]
                        pool.load(regs, selni[0:1, h * TOP:(h + 1) * TOP])
                        if 2 * b + h // 4 >= 1 and h % 4 == 0:
                            pool.wait_ge(s_red, 2 * b + h // 4)
                        for i in range(TOP):
                            n = pool.snap(regs[i], min_val=0, max_val=NB - 1)
                            last = pool.tensor_tensor(
                                prod[:, h % 4, i * 2 * HD:(i + 1) * 2 * HD].rearrange("p (r d) -> p r d", r=2),
                                K[:, bass.ds(n, 1), :, h * HD:(h + 1) * HD].rearrange("p a r d -> p (a r) d"),
                                qb[:, h * HD:(h + 1) * HD].unsqueeze(1).broadcast_to([P, 2, HD]), ALU.mult)
                        last.then_inc(s_mul, 1)
                        for r in regs:
                            pool.free_register(r)
                    if b + 1 < B:
                        pool.wait_ge(s_mul, H * (b + 1))
                        for n in range(NB):
                            load_k(b + 1, n)

        @block.tensor
        def _(pe):
            pe.wait_ge(s_const, 1)
            n_dc = [0]

            def dc_begin(s):
                if dc_use[s] >= 1:
                    pe.wait_ge(dc_free, dc_use[s])

            n_sm = [0]

            def sm_begin():
                if n_sm[0] >= 1:
                    pe.wait_ge(sm_free, n_sm[0])
                n_sm[0] += 1

            def sample_partials(w, src):
                for kc in range(KC):
                    j = kc % 4
                    last = pe.matmul(SM[32 * j:32 * j + 32, :], src[:, kc, :], w[:, kc, :],
                                     start=(kc < 4), stop=(kc >= 4), tile_position=(0, 32 * j))
                last.then_inc(sm_full, 1)

            for s in SCHEDULE:
                kind = s[0]
                if kind == "wt":
                    n = tp_use[s]
                    for g in range(G):
                        last = pe.transpose(TP[n % 2][:, g * P:(g + 1) * P], ws_rows[:, g, :], ident[:, :])
                    last.then_inc(tp_full[n % 2], 1)
                elif kind == "xn":
                    t = s[1]
                    pe.wait_ge(s_xn, t + 1)
                    for half in range(2):
                        n = tp_use[s + (half,)]
                        wait_free(pe, tp_free, n)
                        for i in range(4):
                            last = pe.transpose(TP[n % 2][:, i * P:(i + 1) * P],
                                                x_tile[t][:, half, i * P:(i + 1) * P], ident[:, :])
                        last.then_inc(tp_full[n % 2], 1)
                elif kind == "xs":
                    pe.wait_ge(s_xn, NT + 1)
                    n = tp_use[s]
                    wait_free(pe, tp_free, n)
                    for kc in range(KC):
                        last = pe.transpose(TP[n % 2][:, kc * B:(kc + 1) * B],
                                            xs_sb[:, kc * P:(kc + 1) * P], ident[0:B, 0:B])
                    last.then_inc(tp_full[n % 2], 1)
                elif kind == "pj":
                    c, t = s[1], s[2]
                    if t == 0:
                        pe.wait_ge(s_w[c % 2], 16 * (c // 2 + 1))
                        if c == 0:
                            for par in range(2):
                                last_n = max(tp_use[k] for k in tp_use if k[0] in ("xn", "xs") and tp_use[k] % 2 == par)
                                pe.wait_ge(tp_free[par], last_n // 2 + 1)
                    n = pa_use[s]
                    wait_free(pe, pa_free, n)
                    for kc in range(KC):
                        if CHUNKS[c] == "q":
                            lhs, rhs = wbuf[:, c % 2, kc, t * P:(t + 1) * P], hT[:, kc, :]
                        else:
                            lhs, rhs = hT[:, kc, t * P:(t + 1) * P], wbuf[:, c % 2, kc, :]
                        last = pe.matmul(PA[n % 2][:, :], lhs, rhs, start=(kc == 0), stop=(kc == KC - 1))
                    last.then_inc(pa_full[n % 2], 1)
                elif kind == "spj":
                    c = s[1]
                    sm_begin()
                    sample_partials(wbuf[:, c % 2, :, :], hTs)
                elif kind == "sfd":
                    sm_begin()
                    pe.matmul(SM[0:B, :], fold[:, :], spart[:, :], start=True, stop=True).then_inc(sm_full, 1)
                elif kind == "kt":
                    t = s[1]
                    wait_evac(pe, ("pj", 1, t))
                    n = tp_use[s]
                    wait_free(pe, tp_free, n)
                    for i in range(4):
                        last = pe.transpose(TP[n % 2][:, i * P:(i + 1) * P], krow_t[t][:, i * P:(i + 1) * P], ident[:, :])
                    last.then_inc(tp_full[n % 2], 1)
                elif kind == "sg":
                    t = s[1]
                    pe.wait_ge(s_vn, t + 1)
                    n = pa_use[s]
                    wait_free(pe, pa_free, n)
                    for g in range(G):
                        last = pe.matmul(PA[n % 2][:, g * P:(g + 1) * P], wsT[:, g, :],
                                         vn[:, t % 2, g * P:(g + 1) * P], start=True, stop=True)
                    last.then_inc(pa_full[n % 2], 1)
                elif kind == "qk":
                    h, i = s[1], s[2]
                    if (h, i) == (0, 0):
                        for t in (NT - 2, NT - 1):
                            n = tp_use[("kt", t)]
                            pe.wait_ge(tp_free[n % 2], n // 2 + 1)
                    n = pa_use[s]
                    wait_free(pe, pa_free, n)
                    o = 64 * (h % 2)
                    pe.matmul(PA[n % 2][:, 0:(i + 1) * P], qT[o:o + HD, h // 2, i * P:(i + 1) * P],
                              kT[o:o + HD, h // 2, 0:(i + 1) * P], start=True, stop=True,
                              tile_position=(o, 0)).then_inc(pa_full[n % 2], 1)
                elif kind == "ptr":
                    h, i = s[1], s[2]
                    a = h * NT + i
                    pe.wait_ge(s_pexp, a + 1)
                    n = tp_use[s]
                    wait_free(pe, tp_free, n)
                    for jt in range(i + 1):
                        last = pe.transpose(TP[n % 2][:, jt * P:(jt + 1) * P], pr[:, a % 2, jt * P:(jt + 1) * P], ident[:, :])
                    last.then_inc(tp_full[n % 2], 1)
                elif kind == "pv":
                    h, i = s[1], s[2]
                    a = h * NT + i
                    n = tp_use[("ptr", h, i)]
                    pe.wait_ge(tp_free[n % 2], n // 2 + 1)
                    if a == 0:
                        for t in (NT - 2, NT - 1):
                            wait_evac(pe, ("pj", 2, t))
                    if i == 0 and h >= 1:
                        pe.wait_ge(po_free, h)
                    for jt in range(i + 1):
                        last = pe.matmul(PO[:, i * HD:(i + 1) * HD], pT[:, a % 2, jt, :],
                                         v[:, jt, h * HD:(h + 1) * HD], start=(jt == 0), stop=(jt == i))
                    last.then_inc(s_ptused, 1)
                elif kind == "yt":
                    t, half = s[1], s[2]
                    if half == 0:
                        pe.wait_ge(s_ydone, NT + t + 1)
                    n = tp_use[s]
                    wait_free(pe, tp_free, n)
                    src = (ya if half == 0 else yb)
                    for i in range(4):
                        last = pe.transpose(TP[n % 2][:, i * P:(i + 1) * P], src[:, t, i * P:(i + 1) * P], ident[:, :])
                    last.then_inc(tp_full[n % 2], 1)
                elif kind == "op":
                    t, half = s[1], s[2]
                    c = len(CHUNKS) + half
                    if t == 0:
                        pe.wait_ge(s_w[c % 2], 16 * (c // 2 + 1))
                    if half == 0:
                        for hf in range(2):
                            n = tp_use[("yt", t, hf)]
                            pe.wait_ge(tp_free[n % 2], n // 2 + 1)
                    n = pa_use[s]
                    wait_free(pe, pa_free, n)
                    for kc in range(KC):
                        last = pe.matmul(PA[n % 2][:, :], hT[:, kc, t * P:(t + 1) * P], wbuf[:, c % 2, kc, :],
                                         start=(kc == 0), stop=(kc == KC - 1))
                    last.then_inc(pa_full[n % 2], 1)
                elif kind == "sn":
                    dc_begin(s)
                    pe.wait_ge(s_snr, 1)
                    pe.transpose(DC[0:H, 0:B], sn[:, :], ident[0:B, 0:B]).then_inc(dc_full, 1)
                elif kind == "qb":
                    b = s[1]
                    dc_begin(s)
                    pe.wait_ge(sm_free, 2)
                    pe.matmul(DC[:, :], ident[0:B, b:b + 1].broadcast_to([B, P]), qs[:, :],
                              start=True, stop=True).then_inc(dc_full, 1)
                elif kind == "km":
                    b, n = s[1], s[2]
                    if n == 0 and b >= 1:
                        pe.wait_ge(km_free, b)
                    pe.wait_ge(s_k[n], 16 * (b + 1))
                    j, m = n % 4, n // 4
                    for r in range(2):
                        last = pe.matmul(KM[32 * j:32 * j + 32, :], slid[:, 31 - m:63 - m], K[:, n, r, :],
                                         start=(m == 0 and r == 0), stop=(m == 3 and r == 1),
                                         tile_position=(0, 32 * j))
                    last.then_inc(s_km, 1)
                elif kind == "gt":
                    dc_begin(s)
                    pe.wait_ge(s_gs, s[1] + 1)
                    pe.transpose(DC[0:H, 0:P], gsum[:, :], ident[:, :]).then_inc(dc_full, 1)
                elif kind == "bc":
                    dc_begin(s)
                    pe.wait_ge(s_spr, s[1] + 1)
                    pe.matmul(DC[:, 0:H * TOP * 3], ones[0:H, :], spread[:, :, :].rearrange("p a b -> p (a b)"),
                              start=True, stop=True).then_inc(dc_full, 1)
                elif kind == "mt":
                    dc_begin(s)
                    pe.wait_ge(s_mxr, s[1] + 1)
                    pe.transpose(DC[0:H, 0:P], mx[:, :], ident[:, :]).then_inc(dc_full, 1)
                elif kind == "mb":
                    dc_begin(s)
                    pe.wait_ge(s_dgm, s[1] + 1)
                    pe.matmul(DC[:, 0:H], ones[0:H, :], dgm[:, :], start=True, stop=True).then_inc(dc_full, 1)
                elif kind == "pvd":
                    b = s[1]
                    dc_begin(s)
                    pe.wait_ge(s_pex, b + 1)
                    pe.wait_ge(s_v, 16 * H * TOP * 2 * (b + 1))
                    for hh in range(2):
                        for i in range(TOP):
                            for r in range(2):
                                for j in range(4):
                                    h = 4 * hh + j
                                    pe.matmul(DC[32 * j:32 * j + 1, hh * HD:(hh + 1) * HD], pex[:, h, i, r:r + 1],
                                              V[:, h * TOP + i, r, :], start=(i == 0 and r == 0),
                                              stop=(i == TOP - 1 and r == 1), tile_position=(0, 32 * j))
                    pe.wait_ge(s_psm, b + 1)
                    pe.matmul(DC[0:1, 2 * HD:2 * HD + H], ones[:, 0:1], psm[:, :], start=True, stop=True).then_inc(dc_full, 1)
                elif kind == "fin0":
                    dc_begin(s)
                    pe.wait_ge(s_pnT, 1)
                    pe.transpose(DC[0:B, 0:H], pnT[:, :], ident[0:H, 0:H]).then_inc(dc_full, 1)
                elif kind == "fin2":
                    pe.wait_ge(s_fin, 1)
                    n = tp_use[s]
                    wait_free(pe, tp_free, n)
                    for kc in range(KC):
                        src = yas if kc < 4 else obs
                        last = pe.transpose(TP[n % 2][:, kc * B:(kc + 1) * B], src[:, (kc % 4) * P:(kc % 4 + 1) * P], ident[0:B, 0:B])
                    last.then_inc(tp_full[n % 2], 1)
                elif kind == "fop":
                    half = s[1]
                    if half == 0:
                        n = tp_use[("fin2",)]
                        pe.wait_ge(tp_free[n % 2], n // 2 + 1)
                    sm_begin()
                    sample_partials(wbuf[:, (len(CHUNKS) + half) % 2, :, :], hTs)
                elif kind == "ffd":
                    sm_begin()
                    pe.matmul(SM[0:B, :], fold[:, :], spart[:, :], start=True, stop=True).then_inc(sm_full, 1)

        @block.scalar
        def _(act):
            for dst, src in ((gpre[:, :], g_pre.rearrange("l (k p) -> p (l k)", p=P)),
                             (gab[:, 0:4], g_branch_a.rearrange("l (k p) -> p (l k)", p=P)),
                             (gab[:, 4:8], g_branch_b.rearrange("l (k p) -> p (l k)", p=P)),
                             (sgub[:, :], sgu_b.rearrange("l g t -> t (l g)")),
                             (w00[:, :], sgu_w[:, :, 0, 0].broadcast_to([B, G])),
                             (b00[:, :], sgu_b[:, :, 0].broadcast_to([B, G])),
                             (gain[:, :], sgu_gain.rearrange("l g c -> l (g c)").broadcast_to([P, W]))):
                act.dma_start(dst, src, allow_slow_non_contiguous=True).then_inc(s_small, 16)
            n_act = [0]

            def link(ins):
                n_act[0] += 1
                ins.then_inc(s_act, 1)
                act.wait_ge(s_act, n_act[0])

            squared = []

            def mean_square(src, rows, col, width, n, done, at=0):
                if squared and at == 0:
                    act.wait_ge(*squared[-1])
                squared.append((done, n))
                return act.activation(junk[0:rows, at:at + src.shape[-1]], src, ACT.Square,
                                      scale=float(width) ** -0.5, accum_out=msum[0:rows, col:col + 1])

            n_ms, n_sq = [0], [0]

            def mean_squares(src, rows, col, width):
                n_ms[0] += 1
                mean_square(src, rows, col, width, n_ms[0], s_ms).then_inc(s_ms, 1)

            def group_squares(src, rows, col):
                n_ms[0] += 1
                for g in range(G):
                    last = mean_square(src[:, g * P:(g + 1) * P], rows, col + g, P, n_ms[0], s_ms, at=g * P)
                last.then_inc(s_ms, 1)

            def half_square(src, rows, col):
                n_sq[0] += 1
                mean_square(src, rows, col, D, n_sq[0], s_sq).then_inc(s_sq, 1)

            for s in SCHEDULE:
                kind = s[0]
                if kind == "xn":
                    act.wait_ge(s_xt[s[1]], 16)
                    mean_squares(x_tile[s[1]].rearrange("p a b -> p (a b)"), P, s[1], D)
                elif kind == "xs":
                    act.wait_ge(s_xs, 16)
                    mean_squares(xs_sb, B, 4, D)
                elif kind == "pj":
                    c, t = s[1], s[2]
                    name = CHUNKS[c]
                    n = pa_use[s]
                    if name == "va" and t >= 2:
                        wait_full(act, pa_full, pa_use[("sg", t - 2)])
                    if name == "ga" and t < 2:
                        wait_full(act, pa_full, pa_use[("sg", NT - 2 + t)])
                    if name in ("ga", "gb") and (name, t) not in (("ga", 0), ("ga", 1)):
                        act.wait_ge(s_ydone, (c - 5) * NT + t - 1)
                    wait_full(act, pa_full, n)
                    bank = PA[n % 2][:, :]
                    dst, fn, sc_ = {"q": (qT[:, t, :], ACT.Copy, SCALE), "k": (yb[:, t, :], ACT.Copy, 1.0),
                                    "v": (v[:, t, :], ACT.Copy, 1.0), "u": (ya[:, t, :], ACT.Gelu_apprx_tanh, 1.0),
                                    "va": (vn[:, t % 2, :], ACT.Gelu_apprx_tanh, 1.0),
                                    "ga": (vn[:, t % 2, :], ACT.Silu, 1.0),
                                    "gb": (vn[:, t % 2, :], ACT.Silu, 1.0)}[name]
                    act.activation(dst, bank, fn, scale=sc_).then_inc(pa_free[n % 2], 1)
                    if name == "va":
                        act.wait_ge(pa_free[n % 2], n // 2 + 1)
                        group_squares(vn[:, t % 2, :], P, 8 + 4 * t)
                    if name == "ga":
                        wait_evac(act, ("sg", t))
                        mean_squares(ya[:, t, :], P, 24 + t, W)
                    if name == "gb":
                        act.wait_ge(po_free, H)
                        mean_squares(yb[:, t, :], P, 28 + t, W)
                elif kind == "sfd":
                    c = s[1]
                    name = CHUNKS[c]
                    act.wait_ge(sm_full, 2 * c + 2)
                    if name == "ga":
                        act.wait_ge(s_vns_stored, 16)
                        act.wait_ge(s_yas, 1)
                    if name == "gb":
                        act.wait_ge(s_krow_stored, 16 * (NT + 1))
                        act.wait_ge(s_snr, 1)
                    dst, fn, sc_ = {"q": (qs, ACT.Copy, SCALE), "k": (ks, ACT.Copy, 1.0), "v": (vs, ACT.Copy, 1.0),
                                    "u": (yas, ACT.Gelu_apprx_tanh, 1.0), "va": (vns, ACT.Gelu_apprx_tanh, 1.0),
                                    "ga": (vns, ACT.Silu, 1.0), "gb": (ks, ACT.Silu, 1.0)}[name]
                    act.activation(dst[:, :], SM[0:B, :], fn, scale=sc_).then_inc(sm_free, 1)
                    if name == "va":
                        act.wait_ge(sm_free, 2 * c + 2)
                        group_squares(vns[:, :], B, 32)
                    if name == "ga":
                        mean_squares(yas[:, :], B, 36, W)
                elif kind == "qk":
                    h, i = s[1], s[2]
                    a = h * NT + i
                    act.wait_ge(s_pmax, a + 1)
                    act.activation(pr[:, a % 2, 0:(i + 1) * P], pr[:, a % 2, 0:(i + 1) * P], ACT.Exp,
                                   bias=smax[:, a % 2:a % 2 + 1], accum_out=ssum[:, h, i:i + 1]).then_inc(s_pexp, 1)
                elif kind == "ptr":
                    h, i = s[1], s[2]
                    a = h * NT + i
                    n = tp_use[s]
                    wait_full(act, tp_full, n)
                    if a >= 2:
                        act.wait_ge(s_ptused, a - 1)
                    act.copy(pT[:, a % 2, 0:i + 1, :], TP[n % 2][:, 0:(i + 1) * P].rearrange("p (j q) -> p j q", q=P)
                             ).then_inc(tp_free[n % 2], 1)
                elif kind == "bc":
                    fetch_v(act, s[1], range(SP_HEADS, H), "va")
                elif kind == "mb":
                    act.wait_ge(dc_free, dc_use[s] + 1)
                    act.activation(pex[:, :, :, :], sc[:, :, :, :], ACT.Exp).then_inc(s_pex, 1)
                elif kind == "op":
                    t, half = s[1], s[2]
                    n = pa_use[s]
                    wait_full(act, pa_full, n)
                    half_square(PA[n % 2][:, :], P, 40 + 2 * t + half)
                elif kind == "fin0":
                    act.wait_ge(s_fin0, 1)
                    act.activation(pnT[:, :], pnT[:, :], ACT.Exp).then_inc(s_pnT, 1)
                elif kind == "fin1":
                    act.wait_ge(s_fin0, 2)
                    n_ms[0] += NT
                    mean_squares(obs[:, :], B, 37, W)
                elif kind == "ffd":
                    half = s[1]
                    act.wait_ge(sm_full, 2 * len(CHUNKS) + 2 * half + 2)
                    dst = (yas if half == 0 else obs)
                    act.copy(dst[:, :], SM[0:B, :]).then_inc(sm_free, 1)
                    act.wait_ge(sm_free, 2 * len(CHUNKS) + 2 * half + 2)
                    half_square(dst[:, :], B, 38 + half)

        @block.vector
        def _(dve):
            n_dve = [0]

            def link(ins):
                n_dve[0] += 1
                ins.then_inc(s_dve, 1)
                dve.wait_ge(s_dve, n_dve[0])

            n_rs = [0]

            def rstd_wait():
                n_rs[0] += 1
                dve.wait_ge(s_rs, n_rs[0])

            dve.wait_ge(s_const, 1)
            for s in SCHEDULE:
                kind = s[0]
                if kind == "wt":
                    n = tp_use[s]
                    wait_full(dve, tp_full, n)
                    dve.tensor_copy(wsT[:, :, :], TP[n % 2][:, :].rearrange("p (g t) -> p g t", g=G)
                                    ).then_inc(tp_free[n % 2], 1)
                elif kind == "xn":
                    t = s[1]
                    rstd_wait()
                    dve.tensor_scalar(x_tile[t], x_tile[t], rstd[:, t:t + 1], None, ALU.mult).then_inc(s_xn, 1)
                    for half in range(2):
                        n = tp_use[s + (half,)]
                        wait_full(dve, tp_full, n)
                        dve.tensor_tensor(hT[:, 4 * half:4 * half + 4, t * P:(t + 1) * P],
                                          TP[n % 2][:, :].rearrange("p (k q) -> p k q", k=4),
                                          gpre[:, 4 * half:4 * half + 4].unsqueeze(2).broadcast_to([P, 4, P]),
                                          ALU.mult).then_inc(tp_free[n % 2], 1)
                elif kind == "xs":
                    rstd_wait()
                    dve.tensor_scalar(xs_sb, xs_sb, rstd[0:B, 4:5], None, ALU.mult).then_inc(s_xn, 1)
                    n = tp_use[s]
                    wait_full(dve, tp_full, n)
                    dve.tensor_tensor(hTs[:, :, 0:B], TP[n % 2][:, 0:KC * B].rearrange("p (k b) -> p k b", k=KC),
                                      gpre[:, :].unsqueeze(2).broadcast_to([P, KC, B]),
                                      ALU.mult).then_inc(tp_free[n % 2], 1)
                elif kind == "pj":
                    c, t = s[1], s[2]
                    name = CHUNKS[c]
                    if name == "va":
                        rstd_wait()
                        for g in range(G):
                            last = dve.scalar_tensor_tensor(
                                out=vn[:, t % 2, g * P:(g + 1) * P], in0=vn[:, t % 2, g * P:(g + 1) * P],
                                scalar=rstd[:, 8 + 4 * t + g:9 + 4 * t + g], in1=gain[:, g * P:(g + 1) * P],
                                op0=ALU.mult, op1=ALU.mult)
                        last.then_inc(s_vn, 1)
                    if name in ("ga", "gb"):
                        rstd_wait()
                        y, col = (ya, 24 + t) if name == "ga" else (yb, 28 + t)
                        dve.scalar_tensor_tensor(out=y[:, t, :], in0=y[:, t, :], scalar=rstd[:, col:col + 1],
                                                 in1=vn[:, t % 2, :], op0=ALU.mult, op1=ALU.mult).then_inc(s_ydone, 1)
                elif kind in ("spj", "fop"):
                    c = s[1] if kind == "spj" else len(CHUNKS) + s[1]
                    dve.wait_ge(sm_full, 2 * c + 1)
                    dve.tensor_copy(spart[:, :], SM[:, :]).then_inc(sm_free, 1)
                elif kind == "sfd":
                    name = CHUNKS[s[1]]
                    if name == "k":
                        dve.wait_ge(sm_free, 2 * s[1] + 2)
                        link(dve.tensor_tensor(obs[:, :], qs[:, :], ks[:, :], ALU.mult))
                        dve.tensor_reduce(sn[:, :], obs[:, :].rearrange("b (h d) -> b h d", h=H), AX.X,
                                          ALU.add).then_inc(s_snr, 1)
                    if name == "va":
                        rstd_wait()
                        for g in range(G):
                            last = dve.scalar_tensor_tensor(
                                out=vns[:, g * P:(g + 1) * P], in0=vns[:, g * P:(g + 1) * P],
                                scalar=rstd[0:B, 32 + g:33 + g], in1=gain[0:B, g * P:(g + 1) * P],
                                op0=ALU.mult, op1=ALU.mult)
                        last.then_inc(s_vns, 1)
                        dve.wait_ge(s_vns, 1)
                        for g in range(G):
                            last = dve.tensor_scalar(obs[:, g * P:(g + 1) * P], vns[:, g * P:(g + 1) * P],
                                                     w00[:, g:g + 1], b00[:, g:g + 1], ALU.mult, ALU.add)
                        link(last)
                        dve.tensor_tensor(yas[:, :], yas[:, :], obs[:, :], ALU.mult).then_inc(s_yas, 1)
                    if name == "ga":
                        rstd_wait()
                        link(dve.scalar_tensor_tensor(out=yas[:, :], in0=yas[:, :], scalar=rstd[0:B, 36:37],
                                                      in1=vns[:, :], op0=ALU.mult, op1=ALU.mult))
                elif kind == "kt":
                    t = s[1]
                    n = tp_use[s]
                    wait_full(dve, tp_full, n)
                    dve.tensor_copy(kT[:, :, t * P:(t + 1) * P], TP[n % 2][:, :].rearrange("p (f q) -> p f q", f=4)
                                    ).then_inc(tp_free[n % 2], 1)
                elif kind == "sg":
                    t = s[1]
                    n = pa_use[s]
                    wait_full(dve, pa_full, n)
                    for g in range(G):
                        last = dve.scalar_tensor_tensor(
                            out=ya[:, t, g * P:(g + 1) * P], in0=PA[n % 2][:, g * P:(g + 1) * P],
                            scalar=sgub[:, g:g + 1], in1=ya[:, t, g * P:(g + 1) * P], op0=ALU.add, op1=ALU.mult)
                    last.then_inc(pa_free[n % 2], 1)
                elif kind == "qk":
                    h, i = s[1], s[2]
                    a = h * NT + i
                    n = pa_use[s]
                    if a >= 2:
                        wait_full(dve, tp_full, tp_use[("ptr",) + divmod(a - 2, NT)])
                    wait_full(dve, pa_full, n)
                    m = (i + 1) * P
                    dve.scalar_tensor_tensor(out=pr[:, a % 2, 0:m], in0=alibi[:, SEQ - m:SEQ], scalar=SLOPES[h],
                                             in1=PA[n % 2][:, 0:m], op0=ALU.mult, op1=ALU.add).then_inc(pa_free[n % 2], 1)
                    dve.wait_ge(pa_free[n % 2], n // 2 + 1)
                    dve.tensor_reduce(smax[:, a % 2:a % 2 + 1], pr[:, a % 2, 0:m], AX.X, ALU.max,
                                      negate=True).then_inc(s_pmax, 1)
                elif kind == "pv" and s[2] == NT - 1:
                    h = s[1]
                    if h == 0:
                        dve.wait_ge(s_krow_stored, 16 * (NT + 1))
                    dve.wait_ge(s_ptused, NT * (h + 1))
                    dve.wait_ge(s_pexp, NT * (h + 1))
                    link(dve.reciprocal(rinv[:, :], ssum[:, h, :]))
                    dve.tensor_tensor(yb[:, :, h * HD:(h + 1) * HD], PO[:, 0:NT * HD].rearrange("p (t d) -> p t d", t=NT),
                                      rinv[:, :].unsqueeze(2).broadcast_to([P, NT, HD]), ALU.mult).then_inc(po_free, 1)
                elif kind == "yt":
                    t, half = s[1], s[2]
                    n = tp_use[s]
                    wait_full(dve, tp_full, n)
                    dve.tensor_tensor(hT[:, 4 * half:4 * half + 4, t * P:(t + 1) * P],
                                      TP[n % 2][:, :].rearrange("p (k q) -> p k q", k=4),
                                      gab[:, 4 * half:4 * half + 4].unsqueeze(2).broadcast_to([P, 4, P]),
                                      ALU.mult).then_inc(tp_free[n % 2], 1)
                elif kind == "op":
                    t, half = s[1], s[2]
                    n = pa_use[s]
                    stage = (pr[:, :, :] if t % 2 == 0 else pT[:, :, :, :].rearrange("p a j q -> p a (j q)"))
                    dve.wait_ge(s_sq, 2 * t + half + 1)
                    if t == 0 and half == 0:
                        dve.wait_ge(s_xres, 16 * (NT + 1))
                    dve.tensor_tensor(stage[:, half, :], PA[n % 2][:, :], gpost[:, half * W:(half + 1) * W],
                                      ALU.mult).then_inc(pa_free[n % 2], 1)
                    if half == 1:
                        dve.tensor_tensor(msum[:, 41 + 2 * t:42 + 2 * t], msum[:, 40 + 2 * t:41 + 2 * t],
                                          msum[:, 41 + 2 * t:42 + 2 * t], ALU.add).then_inc(s_ms, 1)
                        rstd_wait()
                        dve.wait_ge(pa_free[n % 2], n // 2 + 1)
                        dve.scalar_tensor_tensor(out=xres[t], in0=stage, scalar=rstd[:, 41 + 2 * t:42 + 2 * t],
                                                 in1=xres[t], op0=ALU.mult, op1=ALU.add).then_inc(s_yo, 1)
                elif kind == "sn":
                    dve.wait_ge(dc_full, dc_use[s] + 1)
                    dve.tensor_copy(snT[:, :], DC[0:H, 0:B]).then_inc(dc_free, 1)
                elif kind == "qb":
                    b = s[1]
                    if b >= 1:
                        dve.wait_ge(s_mul, H * b)
                    dve.wait_ge(dc_full, dc_use[s] + 1)
                    dve.tensor_copy(qb[:, :], DC[:, :]).then_inc(dc_free, 1)
                elif kind == "dg":
                    b = s[1]
                    dve.wait_ge(dc_free, dc_use[("qb", b)] + 1)
                    dve.wait_ge(s_km, NB * (b + 1))
                    tmp = prod[:, :, :].rearrange("p a b -> p (a b)")[:, 0:W]
                    dve.tensor_tensor(tmp, KM[:, :], qb[:, :], ALU.mult).then_inc(km_free, 1)
                    dve.wait_ge(km_free, b + 1)
                    dve.tensor_reduce(gsum[:, :], tmp.rearrange("p (h d) -> p h d", h=H), AX.X, ALU.add).then_inc(s_gs, 1)
                elif kind == "gt":
                    b = s[1]
                    dve.wait_ge(dc_full, dc_use[s] + 1)
                    dve.tensor_copy(g16[:, :].rearrange("h (m j) -> h j m", j=4),
                                    DC[0:H, 0:P].rearrange("h (j x) -> h j x", j=4)[:, :, 0:4]).then_inc(dc_free, 1)
                    dve.wait_ge(dc_free, dc_use[s] + 1)
                    link(dve.max(top8[:, :], g16[:, :]))
                    link(dve.max_index(topi[:, :], top8[:, :], g16[:, :]))
                    link(dve.tensor_copy(vals[:, :, 0], topi[:, 0:TOP]))
                    link(dve.tensor_tensor(oneh[:, :, :], iota16[:, :].unsqueeze(1).broadcast_to([H, TOP, NB]),
                                           vals[:, :, 0:1].broadcast_to([H, TOP, NB]), ALU.is_equal))
                    for j in range(2):
                        last = dve.tensor_tensor(ohp[:, :, j, :], oneh[:, :, :],
                                                 ptbf[0:H, b, :, j].unsqueeze(1).broadcast_to([H, TOP, NB]), ALU.mult)
                    link(last)
                    link(dve.tensor_reduce(vals[:, :, 1:3], ohp[:, :, :, :], AX.X, ALU.add))
                    dve.tensor_tensor(spread[:, :, :], ident[0:H, 0:H].unsqueeze(2).broadcast_to([H, H, TOP * 3]),
                                      vals[:, :, :].rearrange("h k c -> h (k c)").unsqueeze(1).broadcast_to([H, H, TOP * 3]),
                                      ALU.mult).then_inc(s_spr, 1)
                elif kind == "bc":
                    b = s[1]
                    dve.wait_ge(dc_full, dc_use[s] + 1)
                    got = DC[:, 0:H * TOP * 3].rearrange("p (x c) -> p x c", c=3)
                    if b >= 1:
                        dve.wait_ge(s_v, 16 * H * TOP * 2 * b)
                        dve.wait_ge(s_mul, H * b)
                    dve.tensor_copy(selni[0:1, :], got[0:1, :, 0])
                    dve.tensor_copy(selpi[0:1, :].rearrange("a (x j) -> a x j", j=2), got[0:1, :, 1:3]).then_inc(s_sel, 1)
                    dve.tensor_copy(seln[:, :, :].rearrange("p h k -> p (h k)"), got[:, :, 0]).then_inc(dc_free, 1)
                elif kind == "sr":
                    b = s[1]
                    half = s[2]
                    dve.wait_ge(s_mul, H * b + 4 * (half + 1))
                    dve.tensor_reduce(sc[:, 4 * half:4 * half + 4, :, :],
                                      prod[:, :, :].rearrange("p a (i r d) -> p a i r d", i=TOP, r=2),
                                      AX.X, ALU.add).then_inc(s_red, 1)
                    if half == 0:
                        continue
                    dve.wait_ge(s_red, 2 * (b + 1))
                    link(dve.tensor_tensor(sc[:, :, :, :], sc[:, :, :, :],
                                           calibi[:, :, :].unsqueeze(2).broadcast_to([P, H, TOP, 2]), ALU.add))
                    link(dve.tensor_tensor(sbias[:, :, :], seln[:, :, :],
                                           slope256[:, :].unsqueeze(2).broadcast_to([P, H, TOP]), ALU.mult))
                    link(dve.tensor_tensor(sc[:, :, :, :], sc[:, :, :, :],
                                           sbias[:, :, :].unsqueeze(3).broadcast_to([P, H, TOP, 2]), ALU.add))
                    dve.tensor_reduce(mx[:, :], sc[:, :, :, :].rearrange("p h k r -> p h (k r)"), AX.X,
                                      ALU.max).then_inc(s_mxr, 1)
                elif kind == "mt":
                    b = s[1]
                    dve.wait_ge(dc_full, dc_use[s] + 1)
                    dve.tensor_reduce(mrow[:, :], DC[0:H, 0:P], AX.X, ALU.max).then_inc(dc_free, 1)
                    dve.wait_ge(dc_free, dc_use[s] + 1)
                    link(dve.tensor_tensor(MT[:, b:b + 1], mrow[:, :], snT[:, b:b + 1], ALU.max))
                    dve.tensor_scalar(dgm[:, :], ident[0:H, 0:H], MT[:, b:b + 1], None, ALU.mult).then_inc(s_dgm, 1)
                elif kind == "mb":
                    dve.wait_ge(dc_full, dc_use[s] + 1)
                    dve.tensor_tensor(sc[:, :, :, :].rearrange("p h k r -> p h (k r)"),
                                      sc[:, :, :, :].rearrange("p h k r -> p h (k r)"),
                                      DC[:, 0:H].unsqueeze(2).broadcast_to([P, H, TOP * 2]), ALU.subtract
                                      ).then_inc(dc_free, 1)
                elif kind == "pvd":
                    b = s[1]
                    dve.wait_ge(s_pex, b + 1)
                    dve.tensor_reduce(psm[:, :], pex[:, :, :, :].rearrange("p h k r -> p h (k r)"), AX.X,
                                      ALU.add).then_inc(s_psm, 1)
                    dve.wait_ge(dc_full, dc_use[s] + 1)
                    for j in range(4):
                        dve.tensor_copy(osb[32 * j:32 * j + 1, b, :], DC[32 * j:32 * j + 1, 0:2 * HD])
                    dve.tensor_copy(denr[0:1, b, :], DC[0:1, 2 * HD:2 * HD + H]).then_inc(dc_free, 1)
                elif kind == "fin0":
                    dve.tensor_tensor(pnT[:, :], snT[:, :], MT[:, :], ALU.subtract).then_inc(s_fin0, 1)
                    dve.wait_ge(dc_full, dc_use[s] + 1)
                    dve.tensor_copy(pn[:, :], DC[0:B, 0:H]).then_inc(dc_free, 1)
                    dve.wait_ge(dc_free, dc_use[s] + 1)
                    dve.wait_ge(s_obs, 16 * 6)
                    link(dve.tensor_tensor(den[:, :], den[:, :], pn[:, :], ALU.add))
                    link(dve.reciprocal(den[:, :], den[:, :]))
                    o3, v3 = (x[:, :].rearrange("b (h d) -> b h d", h=H) for x in (obs, vs))
                    dve.wait_ge(s_vrow_stored, 16 * (NT + 1))
                    link(dve.tensor_tensor(v3, v3, pn[:, :].unsqueeze(2).broadcast_to([B, H, HD]), ALU.mult))
                    link(dve.tensor_tensor(o3, o3, v3, ALU.add))
                    dve.tensor_tensor(o3, o3, den[:, :].unsqueeze(2).broadcast_to([B, H, HD]), ALU.mult
                                      ).then_inc(s_fin0, 1)
                elif kind == "fin2":
                    rstd_wait()
                    dve.scalar_tensor_tensor(out=obs[:, :], in0=obs[:, :], scalar=rstd[0:B, 37:38], in1=ks[:, :],
                                             op0=ALU.mult, op1=ALU.mult).then_inc(s_fin, 1)
                    n = tp_use[s]
                    wait_full(dve, tp_full, n)
                    dve.tensor_tensor(hTs[:, :, 0:B], TP[n % 2][:, 0:KC * B].rearrange("p (k b) -> p k b", k=KC),
                                      gab[:, :].unsqueeze(2).broadcast_to([P, KC, B]), ALU.mult).then_inc(tp_free[n % 2], 1)
                elif kind == "ffd" and s[1] == 1:
                    dve.wait_ge(s_sq, 2 * NT + 2)
                    dve.tensor_tensor(msum[0:B, 39:40], msum[0:B, 38:39], msum[0:B, 39:40], ALU.add).then_inc(s_ms, 1)
                    rstd_wait()
                    for half, y in enumerate((yas, obs)):
                        last = dve.scalar_tensor_tensor(out=y[:, :], in0=y[:, :], scalar=rstd[0:B, 39:40],
                                                        in1=gpost[0:B, half * W:(half + 1) * W], op0=ALU.mult, op1=ALU.mult)
                    link(last)
                    for half, y in enumerate((yas, obs)):
                        x2 = xs2_sb[:, 2 * half:2 * half + 2, :]
                        last = dve.tensor_tensor(x2, x2, y[:, :].rearrange("b (a c) -> b a c", a=2), ALU.add)
                    last.then_inc(s_sout, 1)


_INS = ['x_prompt', 'x_sample', 'cache_k', 'cache_v', 'page_table', 'g_pre', 'w_in', 'sgu_gain', 'sgu_w',
        'sgu_b', 'g_branch_a', 'g_branch_b', 'w_out', 'g_post']
_OUTS = [(1, SEQ, D), (B, 1, D), (1, 1, SEQ, H, HD), (1, 1, SEQ, H, HD), (1, B, 1, H, HD), (1, B, 1, H, HD),
         (1, B, 1, W)]


def kernel(**inputs):
    import numpy as _np
    import concourse.bacc as _bacc
    from concourse import mybir as _mybir
    from concourse.bass_utils import run_bass_kernel_spmd as _run

    nc = _bacc.Bacc("TRN2", target_bir_lowering=False, num_devices=1, dynamic_dma_scratch_size=RING)
    arrays, args = {}, []
    for name in _INS:
        a = _np.ascontiguousarray(inputs[name])
        arrays[f"in_{name}"] = a
        args.append(nc.dram_tensor(f"in_{name}", a.shape, _mybir.dt.from_np(a.dtype), kind="ExternalInput").ap())
    for i, shape in enumerate(_OUTS):
        args.append(nc.dram_tensor(f"out_{i}", shape, F32, kind="ExternalOutput").ap())
    hymba_kernel(nc, *args)
    r = _run(nc, [arrays], core_ids=[0])
    return tuple(r.results[0][f"out_{i}"] for i in range(len(_OUTS)))
```

```python
import concourse.bass as bass
import concourse.mybir as mybir
from contextlib import ExitStack

F32 = mybir.dt.float32
BF16 = mybir.dt.bfloat16
I32 = mybir.dt.int32
U32 = mybir.dt.uint32
ALU = mybir.AluOpType
ACT = mybir.ActivationFunctionType
AX = mybir.AxisListType

P = 128
D = 1024
KC = D // P
SEQ = 512
NT = SEQ // P
B = 8
H, HD = 8, 64
W = 512
G = 4
PAST = 4096
PAGE = 128
NPAGE = PAST // PAGE
BLK = 256
NB = PAST // BLK
TOP = 3
ROWS = PAGE // 2
EPS = 1e-6
SCALE = HD ** -0.5
NEG = -1e30
RING = 4096
SLOPES = [2.0 ** -(h + 1) for h in range(H)]
CHUNKS = ["q", "k", "v", "u", "va", "ga", "gb"]
COL = {"u": 0, "va": 1, "ga": 2, "q": 3, "k": 4, "v": 5, "gb": 6}
POOL_HEADS = 4


def sp_heads(b):
    return SP_HEADS if b < B - 1 else SP_LAST


def make_schedule():
    att = []
    pairs = [(h, i) for h in range(H) for i in range(NT)]
    for a in range(len(pairs) + 2):
        att.append(([("qk",) + pairs[a]] if a < len(pairs) else [])
                   + ([("ptr",) + pairs[a - 1]] if 1 <= a <= len(pairs) else [])
                   + ([("pv",) + pairs[a - 2]] if a >= 2 else []))
    pre = [("xn", t) for t in range(NT)]
    out = []

    def chunk(c):
        steps = []
        name = CHUNKS[c]
        for t in range(NT):
            steps += [("pj0", c, t), ("pj", c, t)]
            if name == "k" and t >= 1:
                steps.append(("kt", t - 1))
            if name == "va" and t >= 1:
                steps.append(("sg", t - 1))
            if t == 0 and c == 0:
                steps += [("wt",), ("xs",)]
            if t == (1 if c == 0 else 0):
                steps.append(("spj", c))
            if t == (2 if c == 0 else 1):
                steps.append(("sfd", c))
            if t == 2 and name == "k":
                steps.append(("sn",))
        if name == "k":
            steps.append(("kt", NT - 1))
        if name == "va":
            steps.append(("sg", NT - 1))
        return steps

    def out_steps(t):
        return [("op0", t, 0), ("op", t, 0), ("op0", t, 1), ("op", t, 1)]
    prompt = chunk(0) + chunk(1) + chunk(2)
    rest = chunk(3) + chunk(4) + chunk(5)
    halves = [s[0] in ("pj0", "pj") for s in rest]
    n = done = 0
    for s, half in zip(rest, halves):
        prompt.append(s)
        done += half
        want = n + half if s[0] == "pj0" else done * len(att) // sum(halves)
        for group in att[n:want]:
            prompt += group
        n = max(n, want)
    prompt += chunk(6)
    for t in range(NT):
        prompt += [("yt", t, 0), ("yt", t, 1)]
        if t >= 1:
            prompt += out_steps(t - 1)
    prompt += out_steps(NT - 1)
    cost = {"pj0": 3.45, "pj": 3.45, "spj": 2.2, "sfd": 0.9, "kt": .9, "sg": 1.9, "qk": .8, "ptr": .5, "pv": .7,
            "sn": 0.1, "op0": 3.45, "op": 3.45, "yt": .9, "qb": .9, "km": .9, "dg": 0, "gt": .1, "bc": .1, "sr": 0, "mt": .1, "mb": .1,
            "pvd": 3.0, "fv": 0, "ld": 0, "fin0": .1, "fin1": 0, "fin2": .8, "fop": 2.2, "ffd": .9, "wt": .9, "xs": .8}
    events = []
    for b in range(B):
        t = START_US + PERIOD_US * b
        for g in range(NB // 4):
            events.append((t + KM0 + (PERIOD_US - KM0) * (g + 1) / (NB // 4), ("km", b, g)))
        e = t + PERIOD_US
        chain = [(0, ("dg", b)), (GT, ("gt", b)), (BC, ("bc", b)), (BC + SR2, ("sr", b, H - POOL_HEADS)),
                 (MT, ("mt", b)), (MB, ("mb", b)), (PVD, ("pvd", b))]
        events += [(e + dt, s) for dt, s in chain]
        events += [(e + BC + .1 + SR * k, ("sr", b, k)) for k in range(H - POOL_HEADS)]
        for k, h in enumerate(range(sp_heads(b), H)):
            events.append((e + BC + .1 + FV * k, ("fv", b, h)))
        if b + 1 < B:
            events += [(e + LD + LDS * part, ("ld", b + 1, part)) for part in range(4)]
        events.append((START_US if b == 0 else t + QB, ("qb", b)))
        if b == B - 1:
            events += [(e + PVD + dt, s) for dt, s in
                       ((FIN, ("fin0",)), (FIN + 4, ("fin1",)), (FIN + 8, ("fin2",)), (FIN + 12, ("fop", 0)),
                        (FIN + 15, ("ffd", 0)), (FIN + 15.1, ("fop", 1)), (FIN + 18, ("ffd", 1)))]
    events.sort(key=lambda x: x[0])
    now, res, k = 0.0, [], 0
    for s in prompt:
        while k < len(events) and events[k][0] <= now:
            res.append(events[k][1])
            now += cost[events[k][1][0]]
            k += 1
        res.append(s)
        now += cost[s[0]]
    res += [s for _, s in events[k:]]
    first = res.index(("sfd", 0))
    early = [s for s in res[:first] if s[0] == "qb"]
    for s in early:
        res.remove(s)
    first = res.index(("sfd", 0))
    res[first + 1:first + 1] = early
    return pre + res


START_US, PERIOD_US = 5.53, 42.28
GT, BC, SR, SR2, FV, MT, MB, QB, PVD = 2.73, 4.72, 2.34, 9.7, 11.23, 22.3, 34.03, 14.34, 49.82
KM0, LD, LDS, FIN = 20.6, 7.8, 4.59, 1.71
SP_HEADS, SP_LAST = 8, 5

def hymba_kernel(nc, x_prompt, x_sample, cache_k, cache_v, page_table, g_pre, w_in, sgu_gain, sgu_w,
                 sgu_b, g_branch_a, g_branch_b, w_out, g_post,
                 y_prompt, y_sample, k_prompt, v_prompt, k_sample, v_sample, sgu_v_sample):
    SCHEDULE = make_schedule()

    pa_use, tp_use = {}, {}
    for s in SCHEDULE:
        if s[0] in ("pj0", "op0"):
            pa_use[(s[0][:-1],) + s[1:]] = len(pa_use)
        if s[0] in ("sg", "qk"):
            pa_use[s] = len(pa_use)
        if s[0] in ("kt", "ptr", "yt", "wt", "xs", "fin1"):
            tp_use[s] = len(tp_use)
        if s[0] == "xn":
            tp_use[s + (0,)] = len(tp_use)
            tp_use[s + (1,)] = len(tp_use)
        if s[0] == "fin2":
            tp_use[s] = len(tp_use)

    n_phys = cache_k.shape[1]
    k_rows = cache_k.rearrange("l g (p r) h d -> (l g p) (r h d)", r=2)
    v_pages = cache_v.rearrange("l g (p r) h d -> (l g) p r (h d)", r=2)
    x_rows = x_prompt.rearrange("b (t p) d -> (b t) p d", p=P)
    xs_rows = x_sample.rearrange("b t d -> (b t) d")
    y_rows = y_prompt.rearrange("b (t p) d -> (b t) p d", p=P)
    ys_rows = y_sample.rearrange("b t d -> (b t) d")
    kp_rows = k_prompt.rearrange("l b (t p) h d -> (l b t) p (h d)", p=P)
    vp_rows = v_prompt.rearrange("l b (t p) h d -> (l b t) p (h d)", p=P)
    ks_rows = k_sample.rearrange("l b t h d -> (l b t) (h d)")
    vs_rows = v_sample.rearrange("l b t h d -> (l b t) (h d)")
    sv_rows = sgu_v_sample.rearrange("l b t w -> (l b t) w")
    w_in_v = w_in.rearrange("l (k p) n -> p (l k) n", p=P)
    w_out_v = w_out.rearrange("l (k p) n -> p (l k) n", p=P)

    ctx = ExitStack()
    with ctx:
        def sb(name, shape, dt=F32):
            return ctx.enter_context(nc.sbuf_tensor(name, shape, dt))

        def pb(name):
            return ctx.enter_context(nc.psum_tensor(name, [P, 512], F32))

        def sem(name):
            return ctx.enter_context(nc.semaphore(name))

        K = sb("K", [P, NB, 2, W])
        hT = sb("hT", [P, KC, SEQ])
        wbuf = sb("wbuf", [P, 2, KC, W])
        qT = sb("qT", [P, 4, SEQ])
        kT = sb("kT", [P, 4, SEQ])
        v = sb("v", [P, NT, W])
        yb = sb("yb", [P, NT, W])
        ya = sb("ya", [P, NT, W])
        vn = sb("vn", [P, 2, W])
        V = sb("V", [P, H * TOP, 2, HD])
        prod = sb("prod", [P, 4, TOP * 2 * HD])
        dprod = sb("dprod", [P, 2, TOP, 2, HD])
        qb = sb("qb", [P, W])
        pr = sb("pr", [P, 2, SEQ])
        pT = sb("pT", [P, 2, NT, P])
        nhalf = sb("nhalf", [P, G])
        junk = sb("junk", [P, D], BF16)
        ident = sb("ident", [P, P])
        alibi = sb("alibi", [P, SEQ])
        gain = sb("gain", [P, W])
        wsT = sb("wsT", [P, G, P])
        slid = sb("slid", [P, 63])
        gpre = sb("gpre", [P, KC])
        gab = sb("gab", [P, KC])
        sgub = sb("sgub", [P, G])
        hTs = sb("hTs", [P, KC, 32])
        spart = sb("spart", [P, W])
        fold = sb("fold", [P, B])
        qs = sb("qs", [B, W])
        ks = sb("ks", [B, W])
        vs = sb("vs", [B, W])
        yas = sb("yas", [B, W])
        vns = sb("vns", [B, W])
        obs = sb("obs", [B, W])
        osb = sb("osb", [P, B, 2 * HD])
        denr = sb("denr", [1, B, H])
        w00 = sb("w00", [B, G])
        b00 = sb("b00", [B, G])
        msum = sb("msum", [P, 48])
        rstd = sb("rstd", [P, 48])
        smax = sb("smax", [P, 2])
        ssum = sb("ssum", [P, H, NT])
        rinv = sb("rinv", [P, NT])
        kidx = sb("kidx", [P, B, NB], U32)
        poff = sb("poff", [P, 1])
        ptbf = sb("ptbf", [P, B, NB, 2])
        iota16 = sb("iota16", [H, NB])
        gsum = sb("gsum", [P, H])
        g16 = sb("g16", [H, NB])
        top8 = sb("top8", [H, 8])
        topi = sb("topi", [H, 8], U32)
        vals = sb("vals", [H, TOP, 3])
        oneh = sb("oneh", [H, TOP, NB])
        ohp = sb("ohp", [H, TOP, 2, NB])
        spread = sb("spread", [H, H, TOP * 3])
        seln = sb("seln", [P, H, TOP])
        selni = sb("selni", [1, H * TOP], I32)
        selpi = sb("selpi", [1, H * TOP * 2], I32)
        sc = sb("sc", [P, H, TOP, 2])
        sbias = sb("sbias", [P, H, TOP])
        calibi = sb("calibi", [P, H, 2])
        dist = sb("dist", [P, 2])
        slope256 = sb("slope256", [P, H])
        mx = sb("mx", [P, H])
        mrow = sb("mrow", [H, 1])
        MT = sb("MT", [H, B])
        dgm = sb("dgm", [H, H])
        pex = sb("pex", [P, H, TOP, 2])
        psm = sb("psm", [P, H])
        sn = sb("sn", [B, H])
        snT = sb("snT", [H, B])
        pnT = sb("pnT", [H, B])
        pn = sb("pn", [B, H])
        den = sb("den", [B, H])

        PA = [pb("PA0"), pb("PA1")]
        TP = [pb("TP0"), pb("TP1")]
        PO = pb("PO")
        SM = pb("SM")
        KM = pb("KM")
        DC = pb("DC")

        s_xt = [sem(f"x_loaded{t}") for t in range(NT)]
        s_xs = sem("xs_loaded")
        s_w = [sem("w_loaded0"), sem("w_loaded1")]
        s_ws = sem("sgu_w_loaded")
        s_gpre = sem("g_pre_loaded")
        s_small = sem("small_loaded")
        s_gain = sem("gains_loaded")
        s_pt = sem("page_table_loaded")
        s_ident = sem("identity_made")
        s_const = sem("constants_made")
        s_kidx = sem("k_index_made")
        s_k = [sem(f"k_block_loaded{n}") for n in range(NB)]
        s_km = sem("k_blocks_summed")
        s_v = sem("v_rows_loaded")
        s_store = sem("stored")
        s_dve = sem("dve_done")
        s_act = sem("act_done")
        s_pool = sem("pool_done")
        s_ms = sem("mean_square_ready")
        s_mso = sem("mean_square_of_y_ready")
        s_rs = sem("rstd_ready")
        pa_full = [sem("pa_full0"), sem("pa_full1")]
        pa_free = [sem("pa_free0"), sem("pa_free1")]
        tp_full = [sem("tp_full0"), sem("tp_full1")]
        tp_free = [sem("tp_free0"), sem("tp_free1")]
        sm_full, sm_free = sem("sm_full"), sem("sm_free")
        km_full, km_free = sem("km_full"), sem("km_free")
        dc_full, dc_free = sem("dc_full"), sem("dc_free")
        po_free = sem("po_free")
        s_ptused = sem("p_transposed_used")
        s_vns_stored = sem("vns_stored")
        s_sq = sem("out_squared")
        s_xn = sem("x_scaled")
        s_vn = sem("vn_ready")
        s_pmax = sem("prompt_max_ready")
        s_pexp = sem("prompt_exp_ready")
        s_ydone = sem("y_gated")
        s_vrow_stored = sem("v_rows_stored")
        s_krow_stored = sem("k_rows_stored")
        s_snr = sem("sn_ready")
        s_gs = sem("gsum_ready")
        s_spr = sem("spread_ready")
        s_sel = sem("selection_ready")
        s_mul = sem("k_times_q_of_pool")
        s_dmul = sem("k_times_q_of_dve")
        s_red = sem("k_times_q_reduced")
        s_mxr = sem("decode_max_ready")
        s_dgm = sem("max_diag_ready")
        s_pex = sem("decode_exp_ready")
        s_psm = sem("decode_sum_ready")
        s_obs = sem("decode_rows_gathered")
        s_yas = sem("yas_ready")
        s_fin0 = sem("new_token_steps")
        s_sout = sem("sample_out_ready")
        s_vns = sem("vns_ready")
        s_xres = sem("x_residual_loaded")
        s_yo = sem("y_tile_ready")
        s_fin = sem("fin_ready")
        s_pnT = sem("pnT_ready")

        block = ctx.enter_context(nc.Block())

        x_tile = [ya[:, 0:2, :], ya[:, 2:4, :], yb[:, 0:2, :], yb[:, 2:4, :]]
        def ones(rows, cols):
            return slid[0:rows, 31:32].broadcast_to([rows, cols])

        ptb = V[:, 0:2, :, :].rearrange("p a r d -> p (a r d)").bitcast(I32).rearrange("p (b n j) -> p b n j", b=B, j=2)
        xs_sb = prod[0:B, :, :].rearrange("p a b -> p (a b)")[:, 0:D]
        xs2_sb = prod[0:B, 0:4, 0:256]
        xres = [qT[:, 0:2, :], qT[:, 2:4, :], kT[:, 0:2, :], kT[:, 2:4, :]]
        gpost = v[:, 0:2, :].rearrange("p a b -> p (a b)")
        ws_rows = pr[:, 0, :].rearrange("p (g s) -> p g s", g=G)
        WCH = len(CHUNKS) + 2
        krow_t = [yb[:, t, :] for t in range(NT)]

        def w_src(c):
            if c < len(CHUNKS):
                o = COL[CHUNKS[c]] * W
                return w_in_v[:, :, o:o + W]
            return w_out_v[:, :, (c - len(CHUNKS)) * W:(c - len(CHUNKS) + 1) * W]

        def wait_full(eng, full, n):
            eng.wait_ge(full[n % 2], n // 2 + 1)

        def wait_evac(eng, step):
            n = pa_use[step]
            eng.wait_ge(pa_free[n % 2], n // 2 + 1)

        def wait_tp_evac(eng, key):
            n = tp_use[key]
            eng.wait_ge(tp_free[n % 2], n // 2 + 1)

        def wait_free(eng, free, n):
            if n >= 2:
                eng.wait_ge(free[n % 2], n // 2)

        sq_use = {}
        for s in SCHEDULE:
            if s[0] in ("op", "ffd"):
                sq_use[s] = len(sq_use)
        DCN = ["qb", "gt", "bc", "mt", "mb", "pvd"]
        dc_use, dc_order = {}, []
        for s in SCHEDULE:
            if s[0] in DCN or s[0] in ("sn", "fin0"):
                dc_use[s] = len(dc_use)

        def fetch_v(eng, b, heads, name):
            eng.wait_ge(s_sel, b + 1)
            if b > 0:
                eng.wait_ge(dc_full, dc_use[("pvd", b - 1)] + 1)
            for h in heads:
                regs = [eng.alloc_register(f"{name}{b}_{h}_{i}") for i in range(TOP * 2)]
                eng.load(regs, selpi[0:1, h * TOP * 2:(h + 1) * TOP * 2])
                for i in range(TOP * 2):
                    page = eng.snap(regs[i], min_val=0, max_val=n_phys - 1)
                    half = (i % 2) * ROWS
                    eng.dma_start(V[half:half + ROWS, h * TOP + i // 2, :, :],
                                  v_pages[bass.ds(page, 1), :, :, h * HD:(h + 1) * HD]
                                  .rearrange("a p r d -> p (a r) d")).then_inc(s_v, 16)
                for r in regs:
                    eng.free_register(r)

        @block.sync
        def _(sp):
            for t in range(NT):
                sp.dma_start(x_tile[t], x_rows[t].rearrange("p (a b) -> p a b", a=2)).then_inc(s_xt[t], 16)
            sp.dma_start(wbuf[:, 0, :, :], w_src(0)).then_inc(s_w[0], 16)
            sp.dma_start(xs_sb, xs_rows).then_inc(s_xs, 16)
            sp.dma_start(ws_rows, sgu_w.rearrange("l g t s -> t (l g) s")).then_inc(s_ws, 16)
            for dst, src in ((gab[:, 0:4], g_branch_a.rearrange("l (k p) -> p (l k)", p=P)),
                             (gab[:, 4:8], g_branch_b.rearrange("l (k p) -> p (l k)", p=P)),
                             (sgub[:, :], sgu_b.rearrange("l g t -> t (l g)")),
                             (w00[:, :], sgu_w[:, :, 0, 0].broadcast_to([B, G])),
                             (b00[:, :], sgu_b[:, :, 0].broadcast_to([B, G])),
                             (gain[:, :], sgu_gain.rearrange("l g c -> l (g c)").broadcast_to([P, W]))):
                sp.dma_start(dst, src, allow_slow_non_contiguous=True).then_inc(s_small, 16)
            sp.dma_start(wbuf[:, 1, :, :], w_src(1)).then_inc(s_w[1], 16)
            for s in SCHEDULE:
                if s[0] == "pj" and CHUNKS[s[1]] == "k":
                    t = s[2]
                    wait_evac(sp, s)
                    sp.dma_start(kp_rows[t], krow_t[t]).then_inc(s_krow_stored, 16)
                if s[0] == "pj" and CHUNKS[s[1]] == "v":
                    t = s[2]
                    wait_evac(sp, s)
                    sp.dma_start(vp_rows[t], v[:, t, :]).then_inc(s_vrow_stored, 16)
                if s[0] == "sfd" and CHUNKS[s[1]] in ("k", "v"):
                    sp.wait_ge(sm_free, 2 * s[1] + 2)
                    if CHUNKS[s[1]] == "k":
                        sp.dma_start(ks_rows, ks[:, :]).then_inc(s_krow_stored, 16)
                    else:
                        sp.dma_start(vs_rows, vs[:, :]).then_inc(s_vrow_stored, 16)
                if s[0] == "sfd" and CHUNKS[s[1]] == "va":
                    sp.wait_ge(s_vns, 1)
                    sp.dma_start(sv_rows, vns[:, :]).then_inc(s_vns_stored, 16)
                if s[0] == "bc":
                    fetch_v(sp, s[1], range(sp_heads(s[1])), "vs")
                if s[0] == "op" and s[2] == 1:
                    t = s[1]
                    sp.wait_ge(s_yo, t + 1)
                    sp.dma_start(y_rows[t], xres[t].rearrange("p a b -> p (a b)")).then_inc(s_store, 16)
                if s == ("pvd", B - 1):
                    sp.wait_ge(dc_free, dc_use[s] + 1)
                    for j in range(4):
                        sp.dma_start(obs[:, :].rearrange("b (t j d) -> b t j d", t=2, j=4)[:, :, j, :],
                                     osb[32 * j:32 * j + 1, :, :].rearrange("a b (t d) -> a b t d", t=2)
                                     ).then_inc(s_obs, 16)
                    sp.dma_start(den[:, :], denr[:, :, :]).then_inc(s_obs, 16)
                    sp.dma_start(xs2_sb, xs_rows.rearrange("b (a c) -> b a c", a=4)).then_inc(s_obs, 16)
            sp.wait_ge(s_sout, 1)
            sp.dma_start(ys_rows.rearrange("b (a c) -> b a c", a=4), xs2_sb).then_inc(s_store, 16)
            sp.wait_ge(s_krow_stored, 16 * (NT + 1))
            sp.wait_ge(s_vns_stored, 16)
            sp.wait_ge(s_vrow_stored, 16 * (NT + 1))
            sp.wait_ge(s_store, 16 * (NT + 1))

        @block.gpsimd
        def _(pool):
            n_pool = [0]

            def link(ins):
                n_pool[0] += 1
                ins.then_inc(s_pool, 1)
                pool.wait_ge(s_pool, n_pool[0])

            pool.dma_start(ptb.rearrange("p b n j -> p (b n j)"),
                           page_table.rearrange("(a b) n -> a (b n)", a=1).broadcast_to([P, B * NPAGE])).then_inc(s_pt, 16)
            link(pool.iota(poff[:, :], [[0, 1]], base=0, channel_multiplier=1, allow_small_or_imprecise_dtypes=True))
            link(pool.tensor_scalar_add(poff[ROWS:P, :], poff[ROWS:P, :], -float(ROWS)))
            link(pool.memset(ident[:, :], 0.0))
            pool.affine_select(out=ident[:, :], in_=ident[:, :], compare_op=ALU.not_equal, fill=1.0,
                               base=0, pattern=[[-1, P]], channel_multiplier=1).then_inc(s_ident, 1)
            link(pool.memset(nhalf[:, :], -0.5))
            pool.wait_ge(s_pt, 16)
            link(pool.tensor_copy(ptbf[:, :, :, :], ptb))
            for j in range(2):
                p0 = j * ROWS
                link(pool.tensor_scalar(kidx[p0:p0 + ROWS, :, :], ptbf[p0:p0 + ROWS, :, :, j], float(ROWS),
                                        poff[p0:p0 + ROWS, 0:1], ALU.mult, ALU.add))

            def load_k(b, n):
                if b > 0:
                    pool.wait_ge(s_km, NB // 4 * (b - 1) + n // 4 + 1)
                pool.indirect_dma_start(K[:, n, :, :].rearrange("p r w -> p (r w)"), None, k_rows,
                                        bass.IndirectOffsetOnAxis(ap=kidx[:, b, n:n + 1], axis=0)
                                        ).then_inc(s_k[n], 16)

            n_ms = [0]

            n_mso = [0]

            def make_rstd(rows, col, n=1, of_y=False):
                count, ready = (n_mso, s_mso) if of_y else (n_ms, s_ms)
                count[0] += 1
                pool.wait_ge(ready, count[0])
                at = slice(col, col + n)
                link(pool.tensor_scalar_add(rstd[0:rows, at], msum[0:rows, at], EPS))
                pool.tensor_tensor(rstd[0:rows, at], rstd[0:rows, at], nhalf[0:rows, 0:n], ALU.pow).then_inc(s_rs, 1)

            for t in range(NT):
                make_rstd(P, t)
            for n in range(NB // 4):
                load_k(0, n)
            link(pool.memset(slid[:, :], 0.0))
            link(pool.memset(slid[:, 31:32], 1.0))
            link(pool.memset(hTs[:, :, :], 0.0))
            link(pool.memset(fold[:, :], 0.0))
            for j in range(4):
                link(pool.affine_select(out=fold[:, :], in_=fold[:, :], compare_op=ALU.not_equal, fill=1.0,
                                        base=-32 * j, pattern=[[-1, B]], channel_multiplier=1))
            link(pool.iota(alibi[:, :], [[1, SEQ]], base=-(SEQ - P), channel_multiplier=-1,
                           allow_small_or_imprecise_dtypes=True))
            link(pool.affine_select(out=alibi[:, :], in_=alibi[:, :], compare_op=ALU.is_ge, fill=NEG,
                                    base=SEQ - P, pattern=[[-1, SEQ]], channel_multiplier=1))
            link(pool.iota(dist[:, :], [[1, 2]], base=-PAST, channel_multiplier=2,
                           allow_small_or_imprecise_dtypes=True))
            for h in range(H):
                link(pool.tensor_scalar(calibi[:, h, :], dist[:, :], SLOPES[h], None, ALU.mult))
                link(pool.memset(slope256[:, h:h + 1], SLOPES[h] * BLK))
            link(pool.iota(iota16[:, :], [[1, NB]], base=0, channel_multiplier=0,
                           allow_small_or_imprecise_dtypes=True))
            pool.wait_ge(s_ws, 16)
            for g in range(G):
                link(pool.affine_select(out=ws_rows[:, g, :], in_=ws_rows[:, g, :], compare_op=ALU.is_ge,
                                        fill=0.0, base=0, pattern=[[-1, P]], channel_multiplier=1))
            pool.wait_ge(s_small, 16 * 6)
            pool.memset(osb[:, :, :], 0.0).then_inc(s_const, 1)
            make_rstd(B, 4)
            for n in range(NB // 4, NB):
                load_k(0, n)

            for s in SCHEDULE:
                if s[0] == "pj" and CHUNKS[s[1]] == "va":
                    make_rstd(P, 8 + 4 * s[2], 4)
                if s[0] == "pj" and CHUNKS[s[1]] == "ga":
                    make_rstd(P, 24 + s[2])
                if s[0] == "pj" and CHUNKS[s[1]] == "gb":
                    make_rstd(P, 28 + s[2])
                if s[0] == "sfd" and CHUNKS[s[1]] == "va":
                    make_rstd(B, 32, 4)
                if s[0] == "sfd" and CHUNKS[s[1]] == "ga":
                    make_rstd(B, 36)
                if s[0] == "op" and s[2] == 1:
                    make_rstd(P, 41 + 2 * s[1], of_y=True)
                if s[0] == "fin2":
                    make_rstd(B, 37)
                if s == ("ffd", 1):
                    make_rstd(B, 39, of_y=True)
                if s[0] == "bc":
                    b = s[1]
                    pool.wait_ge(s_sel, b + 1)
                    if b >= 1:
                        pool.wait_ge(s_red, (H - POOL_HEADS + 1) * b)
                    for h in range(POOL_HEADS):
                        regs = [pool.alloc_register(f"n{b}_{h}_{i}") for i in range(TOP)]
                        pool.load(regs, selni[0:1, h * TOP:(h + 1) * TOP])
                        for i in range(TOP):
                            n = pool.snap(regs[i], min_val=0, max_val=NB - 1)
                            last = pool.tensor_tensor(
                                prod[:, h, i * 2 * HD:(i + 1) * 2 * HD].rearrange("p (r d) -> p r d", r=2),
                                K[:, bass.ds(n, 1), :, h * HD:(h + 1) * HD].rearrange("p a r d -> p (a r) d"),
                                qb[:, h * HD:(h + 1) * HD].unsqueeze(1).broadcast_to([P, 2, HD]), ALU.mult)
                        for r in regs:
                            pool.free_register(r)
                    last.then_inc(s_mul, 1)
                if s[0] == "ld":
                    b, part = s[1], s[2]
                    if part == 0:
                        pool.wait_ge(s_mul, b)
                        pool.wait_ge(s_dmul, (H - POOL_HEADS) * b)
                    for n in range(4 * part, 4 * part + 4):
                        load_k(b, n)

        @block.tensor
        def _(pe):
            pe.wait_ge(s_ident, 1)
            n_dc = [0]

            def dc_begin(s):
                if dc_use[s] >= 1:
                    pe.wait_ge(dc_free, dc_use[s])

            n_sm = [0]

            def sm_begin():
                if n_sm[0] >= 1:
                    pe.wait_ge(sm_free, n_sm[0])
                n_sm[0] += 1

            def sample_partials(w, src):
                for kc in range(KC):
                    j = kc % 4
                    last = pe.matmul(SM[32 * j:32 * j + 32, :], src[:, kc, :], w[:, kc, :],
                                     start=(kc < 4), stop=(kc >= 4), tile_position=(0, 32 * j))
                last.then_inc(sm_full, 1)

            for s in SCHEDULE:
                kind = s[0]
                if kind == "wt":
                    n = tp_use[s]
                    pe.wait_ge(s_const, 1)
                    wait_free(pe, tp_free, n)
                    for g in range(G):
                        last = pe.transpose(TP[n % 2][:, g * P:(g + 1) * P], ws_rows[:, g, :], ident[:, :])
                    last.then_inc(tp_full[n % 2], 1)
                elif kind == "xn":
                    t = s[1]
                    pe.wait_ge(s_xn, t + 1)
                    for half in range(2):
                        n = tp_use[s + (half,)]
                        wait_free(pe, tp_free, n)
                        for i in range(4):
                            last = pe.transpose(TP[n % 2][:, i * P:(i + 1) * P],
                                                x_tile[t][:, half, i * P:(i + 1) * P], ident[:, :])
                        last.then_inc(tp_full[n % 2], 1)
                elif kind == "xs":
                    pe.wait_ge(s_xn, NT + 1)
                    n = tp_use[s]
                    wait_free(pe, tp_free, n)
                    for kc in range(KC):
                        last = pe.transpose(TP[n % 2][:, kc * B:(kc + 1) * B],
                                            xs_sb[:, kc * P:(kc + 1) * P], ident[0:B, 0:B])
                    last.then_inc(tp_full[n % 2], 1)
                elif kind in ("pj0", "pj"):
                    c, t = s[1], s[2]
                    n = pa_use[("pj", c, t)]
                    if kind == "pj0":
                        if t == 0:
                            pe.wait_ge(s_w[c % 2], 16 * (c // 2 + 1))
                            if c == 0:
                                for par in range(2):
                                    last_n = max(tp_use[k] for k in tp_use if k[0] == "xn" and tp_use[k] % 2 == par)
                                    pe.wait_ge(tp_free[par], last_n // 2 + 1)
                        wait_free(pe, pa_free, n)
                    for kc in (range(KC // 2) if kind == "pj0" else range(KC // 2, KC)):
                        if CHUNKS[c] == "q":
                            lhs, rhs = wbuf[:, c % 2, kc, t * P:(t + 1) * P], hT[:, kc, :]
                        else:
                            lhs, rhs = hT[:, kc, t * P:(t + 1) * P], wbuf[:, c % 2, kc, :]
                        last = pe.matmul(PA[n % 2][:, :], lhs, rhs, start=(kc == 0), stop=(kc == KC - 1))
                    if kind == "pj":
                        last.then_inc(pa_full[n % 2], 1)
                elif kind == "spj":
                    c = s[1]
                    sm_begin()
                    if c == 0:
                        wait_tp_evac(pe, ("xs",))
                    sample_partials(wbuf[:, c % 2, :, :], hTs)
                elif kind == "sfd":
                    sm_begin()
                    pe.matmul(SM[0:B, :], fold[:, :], spart[:, :], start=True, stop=True).then_inc(sm_full, 1)
                elif kind == "kt":
                    t = s[1]
                    wait_evac(pe, ("pj", 1, t))
                    n = tp_use[s]
                    wait_free(pe, tp_free, n)
                    for i in range(4):
                        last = pe.transpose(TP[n % 2][:, i * P:(i + 1) * P], krow_t[t][:, i * P:(i + 1) * P], ident[:, :])
                    last.then_inc(tp_full[n % 2], 1)
                elif kind == "sg":
                    t = s[1]
                    pe.wait_ge(s_vn, t + 1)
                    n = pa_use[s]
                    wait_free(pe, pa_free, n)
                    for g in range(G):
                        last = pe.matmul(PA[n % 2][:, g * P:(g + 1) * P], wsT[:, g, :],
                                         vn[:, t % 2, g * P:(g + 1) * P], start=True, stop=True)
                    last.then_inc(pa_full[n % 2], 1)
                elif kind == "qk":
                    h, i = s[1], s[2]
                    if (h, i) == (0, 0):
                        for t in (NT - 2, NT - 1):
                            n = tp_use[("kt", t)]
                            pe.wait_ge(tp_free[n % 2], n // 2 + 1)
                    n = pa_use[s]
                    wait_free(pe, pa_free, n)
                    o = 64 * (h % 2)
                    pe.matmul(PA[n % 2][:, 0:(i + 1) * P], qT[o:o + HD, h // 2, i * P:(i + 1) * P],
                              kT[o:o + HD, h // 2, 0:(i + 1) * P], start=True, stop=True,
                              tile_position=(o, 0)).then_inc(pa_full[n % 2], 1)
                elif kind == "ptr":
                    h, i = s[1], s[2]
                    a = h * NT + i
                    pe.wait_ge(s_pexp, a + 1)
                    n = tp_use[s]
                    wait_free(pe, tp_free, n)
                    for jt in range(i + 1):
                        last = pe.transpose(TP[n % 2][:, jt * P:(jt + 1) * P], pr[:, a % 2, jt * P:(jt + 1) * P], ident[:, :])
                    last.then_inc(tp_full[n % 2], 1)
                elif kind == "pv":
                    h, i = s[1], s[2]
                    a = h * NT + i
                    n = tp_use[("ptr", h, i)]
                    pe.wait_ge(tp_free[n % 2], n // 2 + 1)
                    if a == 0:
                        for t in (NT - 2, NT - 1):
                            wait_evac(pe, ("pj", 2, t))
                    if i == 0 and h >= 1:
                        pe.wait_ge(po_free, h)
                    for jt in range(i + 1):
                        last = pe.matmul(PO[:, i * HD:(i + 1) * HD], pT[:, a % 2, jt, :],
                                         v[:, jt, h * HD:(h + 1) * HD], start=(jt == 0), stop=(jt == i))
                    last.then_inc(s_ptused, 1)
                elif kind == "yt":
                    t, half = s[1], s[2]
                    if half == 0:
                        pe.wait_ge(s_ydone, NT + t + 1)
                    n = tp_use[s]
                    wait_free(pe, tp_free, n)
                    src = (ya if half == 0 else yb)
                    for i in range(4):
                        last = pe.transpose(TP[n % 2][:, i * P:(i + 1) * P], src[:, t, i * P:(i + 1) * P], ident[:, :])
                    last.then_inc(tp_full[n % 2], 1)
                elif kind in ("op0", "op"):
                    t, half = s[1], s[2]
                    c = len(CHUNKS) + half
                    n = pa_use[("op", t, half)]
                    if kind == "op0":
                        if t == 0:
                            pe.wait_ge(s_w[c % 2], 16 * (c // 2 + 1))
                        if half == 0:
                            for hf in range(2):
                                m = tp_use[("yt", t, hf)]
                                pe.wait_ge(tp_free[m % 2], m // 2 + 1)
                        wait_free(pe, pa_free, n)
                    for kc in (range(KC // 2) if kind == "op0" else range(KC // 2, KC)):
                        last = pe.matmul(PA[n % 2][:, :], hT[:, kc, t * P:(t + 1) * P], wbuf[:, c % 2, kc, :],
                                         start=(kc == 0), stop=(kc == KC - 1))
                    if kind == "op":
                        last.then_inc(pa_full[n % 2], 1)
                elif kind == "sn":
                    dc_begin(s)
                    pe.wait_ge(s_snr, 1)
                    pe.transpose(DC[0:H, 0:B], sn[:, :], ident[0:B, 0:B]).then_inc(dc_full, 1)
                elif kind == "qb":
                    b = s[1]
                    dc_begin(s)
                    pe.wait_ge(sm_free, 2)
                    pe.matmul(DC[:, :], ident[0:B, b:b + 1].broadcast_to([B, P]), qs[:, :],
                              start=True, stop=True).then_inc(dc_full, 1)
                elif kind == "km":
                    b, g = s[1], s[2]
                    if g == 0 and b >= 1:
                        pe.wait_ge(km_free, b)
                    for j in range(4):
                        pe.wait_ge(s_k[4 * g + j], 16 * (b + 1))
                    for r in range(2):
                        for j in range(4):
                            last = pe.matmul(KM[32 * j:32 * j + 32, :], slid[:, 31 - g:63 - g], K[:, 4 * g + j, r, :],
                                             start=(g == 0 and r == 0), stop=(g == NB // 4 - 1 and r == 1),
                                             tile_position=(0, 32 * j))
                    last.then_inc(s_km, 1)
                elif kind == "gt":
                    dc_begin(s)
                    pe.wait_ge(s_gs, s[1] + 1)
                    pe.transpose(DC[0:H, 0:P], gsum[:, :], ident[:, :]).then_inc(dc_full, 1)
                elif kind == "bc":
                    dc_begin(s)
                    pe.wait_ge(s_spr, s[1] + 1)
                    pe.matmul(DC[:, 0:H * TOP * 3], ones(H, P), spread[:, :, :].rearrange("p a b -> p (a b)"),
                              start=True, stop=True).then_inc(dc_full, 1)
                elif kind == "mt":
                    dc_begin(s)
                    pe.wait_ge(s_mxr, s[1] + 1)
                    pe.transpose(DC[0:H, 0:P], mx[:, :], ident[:, :]).then_inc(dc_full, 1)
                elif kind == "mb":
                    dc_begin(s)
                    pe.wait_ge(s_dgm, s[1] + 1)
                    pe.matmul(DC[:, 0:H], ones(H, P), dgm[:, :], start=True, stop=True).then_inc(dc_full, 1)
                elif kind == "pvd":
                    b = s[1]
                    dc_begin(s)
                    pe.wait_ge(s_pex, b + 1)
                    pe.wait_ge(s_v, 16 * H * TOP * 2 * (b + 1))
                    for hh in range(2):
                        for i in range(TOP):
                            for r in range(2):
                                for j in range(4):
                                    h = 4 * hh + j
                                    pe.matmul(DC[32 * j:32 * j + 1, hh * HD:(hh + 1) * HD], pex[:, h, i, r:r + 1],
                                              V[:, h * TOP + i, r, :], start=(i == 0 and r == 0),
                                              stop=(i == TOP - 1 and r == 1), tile_position=(0, 32 * j))
                    pe.wait_ge(s_psm, b + 1)
                    pe.matmul(DC[0:1, 2 * HD:2 * HD + H], ones(P, 1), psm[:, :], start=True, stop=True).then_inc(dc_full, 1)
                elif kind == "fin0":
                    dc_begin(s)
                    pe.wait_ge(s_pnT, 1)
                    pe.transpose(DC[0:B, 0:H], pnT[:, :], ident[0:H, 0:H]).then_inc(dc_full, 1)
                elif kind == "fin2":
                    pe.wait_ge(s_fin, 1)
                    n = tp_use[s]
                    wait_free(pe, tp_free, n)
                    for kc in range(KC):
                        src = yas if kc < 4 else obs
                        last = pe.transpose(TP[n % 2][:, kc * B:(kc + 1) * B], src[:, (kc % 4) * P:(kc % 4 + 1) * P], ident[0:B, 0:B])
                    last.then_inc(tp_full[n % 2], 1)
                elif kind == "fop":
                    half = s[1]
                    if half == 0:
                        n = tp_use[("fin2",)]
                        pe.wait_ge(tp_free[n % 2], n // 2 + 1)
                    sm_begin()
                    sample_partials(wbuf[:, (len(CHUNKS) + half) % 2, :, :], hTs)
                elif kind == "ffd":
                    sm_begin()
                    pe.matmul(SM[0:B, :], fold[:, :], spart[:, :], start=True, stop=True).then_inc(sm_full, 1)

        @block.scalar
        def _(act):
            act.dma_start(gpre[:, :], g_pre.rearrange("l (k p) -> p (l k)", p=P),
                          allow_slow_non_contiguous=True).then_inc(s_gpre, 16)
            n_act = [0]

            def link(ins):
                n_act[0] += 1
                ins.then_inc(s_act, 1)
                act.wait_ge(s_act, n_act[0])

            squared = []

            def mean_square(src, rows, col, width, n, done, at=0):
                if squared and at == 0:
                    act.wait_ge(*squared[-1])
                squared.append((done, n))
                return act.activation(junk[0:rows, at:at + src.shape[-1]], src, ACT.Square,
                                      scale=float(width) ** -0.5, accum_out=msum[0:rows, col:col + 1])

            n_ms, n_sq = [0], [0]

            def mean_squares(src, rows, col, width):
                n_ms[0] += 1
                mean_square(src, rows, col, width, n_ms[0], s_ms).then_inc(s_ms, 1)

            def group_squares(src, rows, col):
                n_ms[0] += 1
                for g in range(G):
                    last = mean_square(src[:, g * P:(g + 1) * P], rows, col + g, P, n_ms[0], s_ms, at=g * P)
                last.then_inc(s_ms, 1)

            def half_square(src, rows, col):
                n_sq[0] += 1
                mean_square(src, rows, col, D, n_sq[0], s_sq).then_inc(s_sq, 1)

            for s in SCHEDULE:
                kind = s[0]
                if kind == "pj" and s[2] == NT - 1 and s[1] + 2 < WCH:
                    c = s[1] + 2
                    wait_full(act, pa_full, pa_use[s])
                    act.dma_start(wbuf[:, c % 2, :, :], w_src(c)).then_inc(s_w[c % 2], 16)
                if s == ("pv", H - 1, NT - 1):
                    act.wait_ge(s_ptused, H * NT)
                    for t in range(NT):
                        act.dma_start(xres[t], x_rows[t].rearrange("p (a b) -> p a b", a=2)).then_inc(s_xres, 16)
                    act.dma_start(gpost, g_post.broadcast_to([P, D])).then_inc(s_xres, 16)
                if kind == "xn":
                    t = s[1]
                    for i in range(NT if t == 0 else 0):
                        act.wait_ge(s_xt[i], 16)
                        mean_squares(x_tile[i].rearrange("p a b -> p (a b)"), P, i, D)
                    act.wait_ge(s_rs, t + 1)
                    act.activation(x_tile[t], x_tile[t], ACT.Copy, scale=rstd[:, t:t + 1]).then_inc(s_xn, 1)
                    if t == NT - 1:
                        act.wait_ge(s_xs, 16)
                        mean_squares(xs_sb, B, 4, D)
                elif kind == "xs":
                    act.wait_ge(s_rs, NT + 1)
                    act.activation(xs_sb, xs_sb, ACT.Copy, scale=rstd[0:B, 4:5]).then_inc(s_xn, 1)
                elif kind == "pj":
                    c, t = s[1], s[2]
                    name = CHUNKS[c]
                    n = pa_use[s]
                    if name == "va" and t >= 2:
                        wait_full(act, pa_full, pa_use[("sg", t - 2)])
                    if name == "ga" and t < 2:
                        wait_full(act, pa_full, pa_use[("sg", NT - 2 + t)])
                    if name in ("ga", "gb") and (name, t) not in (("ga", 0), ("ga", 1)):
                        act.wait_ge(s_ydone, (c - 5) * NT + t - 1)
                    wait_full(act, pa_full, n)
                    bank = PA[n % 2][:, :]
                    dst, fn, sc_ = {"q": (qT[:, t, :], ACT.Copy, SCALE), "k": (yb[:, t, :], ACT.Copy, 1.0),
                                    "v": (v[:, t, :], ACT.Copy, 1.0), "u": (ya[:, t, :], ACT.Gelu_apprx_tanh, 1.0),
                                    "va": (vn[:, t % 2, :], ACT.Gelu_apprx_tanh, 1.0),
                                    "ga": (vn[:, t % 2, :], ACT.Silu, 1.0),
                                    "gb": (vn[:, t % 2, :], ACT.Silu, 1.0)}[name]
                    act.activation(dst, bank, fn, scale=sc_).then_inc(pa_free[n % 2], 1)
                    if name == "va":
                        act.wait_ge(pa_free[n % 2], n // 2 + 1)
                        group_squares(vn[:, t % 2, :], P, 8 + 4 * t)
                    if name == "ga":
                        wait_evac(act, ("sg", t))
                        mean_squares(ya[:, t, :], P, 24 + t, W)
                    if name == "gb":
                        act.wait_ge(po_free, H)
                        mean_squares(yb[:, t, :], P, 28 + t, W)
                elif kind == "sfd":
                    c = s[1]
                    name = CHUNKS[c]
                    act.wait_ge(sm_full, 2 * c + 2)
                    if name == "ga":
                        act.wait_ge(s_vns_stored, 16)
                        act.wait_ge(s_yas, 1)
                    if name == "gb":
                        act.wait_ge(s_krow_stored, 16 * (NT + 1))
                        act.wait_ge(s_snr, 1)
                    dst, fn, sc_ = {"q": (qs, ACT.Copy, SCALE), "k": (ks, ACT.Copy, 1.0), "v": (vs, ACT.Copy, 1.0),
                                    "u": (yas, ACT.Gelu_apprx_tanh, 1.0), "va": (vns, ACT.Gelu_apprx_tanh, 1.0),
                                    "ga": (vns, ACT.Silu, 1.0), "gb": (ks, ACT.Silu, 1.0)}[name]
                    act.activation(dst[:, :], SM[0:B, :], fn, scale=sc_).then_inc(sm_free, 1)
                    if name == "va":
                        act.wait_ge(sm_free, 2 * c + 2)
                        group_squares(vns[:, :], B, 32)
                    if name == "ga":
                        mean_squares(yas[:, :], B, 36, W)
                elif kind == "qk":
                    h, i = s[1], s[2]
                    a = h * NT + i
                    act.wait_ge(s_pmax, a + 1)
                    act.activation(pr[:, a % 2, 0:(i + 1) * P], pr[:, a % 2, 0:(i + 1) * P], ACT.Exp,
                                   bias=smax[:, a % 2:a % 2 + 1], accum_out=ssum[:, h, i:i + 1]).then_inc(s_pexp, 1)
                elif kind == "ptr":
                    h, i = s[1], s[2]
                    a = h * NT + i
                    n = tp_use[s]
                    wait_full(act, tp_full, n)
                    if a >= 2:
                        act.wait_ge(s_ptused, a - 1)
                    act.copy(pT[:, a % 2, 0:i + 1, :], TP[n % 2][:, 0:(i + 1) * P].rearrange("p (j q) -> p j q", q=P)
                             ).then_inc(tp_free[n % 2], 1)
                elif kind == "fv":
                    fetch_v(act, s[1], [s[2]], "va")
                elif kind == "mb":
                    act.wait_ge(dc_free, dc_use[s] + 1)
                    act.activation(pex[:, :, :, :], sc[:, :, :, :], ACT.Exp).then_inc(s_pex, 1)
                elif kind == "op":
                    t, half = s[1], s[2]
                    n = pa_use[s]
                    wait_full(act, pa_full, n)
                    half_square(PA[n % 2][:, :], P, 40 + 2 * t + half)
                elif kind == "fin0":
                    act.wait_ge(s_fin0, 1)
                    act.activation(pnT[:, :], pnT[:, :], ACT.Exp).then_inc(s_pnT, 1)
                elif kind == "fin1":
                    act.wait_ge(s_fin0, 2)
                    mean_squares(obs[:, :], B, 37, W)
                elif kind == "ffd":
                    half = s[1]
                    act.wait_ge(sm_full, 2 * len(CHUNKS) + 2 * half + 2)
                    dst = (yas if half == 0 else obs)
                    act.copy(dst[:, :], SM[0:B, :]).then_inc(sm_free, 1)
                    act.wait_ge(sm_free, 2 * len(CHUNKS) + 2 * half + 2)
                    half_square(dst[:, :], B, 38 + half)

        @block.vector
        def _(dve):
            n_dve = [0]

            def link(ins):
                n_dve[0] += 1
                ins.then_inc(s_dve, 1)
                dve.wait_ge(s_dve, n_dve[0])

            n_rs = [0]

            def rstd_wait():
                n_rs[0] += 1
                dve.wait_ge(s_rs, n_rs[0])

            for s in SCHEDULE:
                kind = s[0]
                if kind == "wt":
                    dve.wait_ge(s_const, 1)
                    n = tp_use[s]
                    wait_full(dve, tp_full, n)
                    dve.tensor_copy(wsT[:, :, :], TP[n % 2][:, :].rearrange("p (g t) -> p g t", g=G)
                                    ).then_inc(tp_free[n % 2], 1)
                elif kind == "xn":
                    t = s[1]
                    n_rs[0] += 1
                    for half in range(2):
                        n = tp_use[s + (half,)]
                        wait_full(dve, tp_full, n)
                        if t == 0 and half == 0:
                            dve.wait_ge(s_gpre, 16)
                        dve.tensor_tensor(hT[:, 4 * half:4 * half + 4, t * P:(t + 1) * P],
                                          TP[n % 2][:, :].rearrange("p (k q) -> p k q", k=4),
                                          gpre[:, 4 * half:4 * half + 4].unsqueeze(2).broadcast_to([P, 4, P]),
                                          ALU.mult).then_inc(tp_free[n % 2], 1)
                elif kind == "xs":
                    n_rs[0] += 1
                    n = tp_use[s]
                    wait_full(dve, tp_full, n)
                    dve.tensor_tensor(hTs[:, :, 0:B], TP[n % 2][:, 0:KC * B].rearrange("p (k b) -> p k b", k=KC),
                                      gpre[:, :].unsqueeze(2).broadcast_to([P, KC, B]),
                                      ALU.mult).then_inc(tp_free[n % 2], 1)
                elif kind == "pj":
                    c, t = s[1], s[2]
                    name = CHUNKS[c]
                    if name == "va":
                        rstd_wait()
                        for g in range(G):
                            last = dve.scalar_tensor_tensor(
                                out=vn[:, t % 2, g * P:(g + 1) * P], in0=vn[:, t % 2, g * P:(g + 1) * P],
                                scalar=rstd[:, 8 + 4 * t + g:9 + 4 * t + g], in1=gain[:, g * P:(g + 1) * P],
                                op0=ALU.mult, op1=ALU.mult)
                        last.then_inc(s_vn, 1)
                    if name in ("ga", "gb"):
                        y, col = (ya, 24 + t) if name == "ga" else (yb, 28 + t)
                        rstd_wait()
                        dve.scalar_tensor_tensor(out=y[:, t, :], in0=y[:, t, :], scalar=rstd[:, col:col + 1],
                                                 in1=vn[:, t % 2, :], op0=ALU.mult, op1=ALU.mult).then_inc(s_ydone, 1)
                elif kind in ("spj", "fop"):
                    c = s[1] if kind == "spj" else len(CHUNKS) + s[1]
                    dve.wait_ge(sm_full, 2 * c + 1)
                    dve.tensor_copy(spart[:, :], SM[:, :]).then_inc(sm_free, 1)
                elif kind == "sfd":
                    name = CHUNKS[s[1]]
                    if name == "k":
                        dve.wait_ge(sm_free, 2 * s[1] + 2)
                        link(dve.tensor_tensor(obs[:, :], qs[:, :], ks[:, :], ALU.mult))
                        dve.tensor_reduce(sn[:, :], obs[:, :].rearrange("b (h d) -> b h d", h=H), AX.X,
                                          ALU.add).then_inc(s_snr, 1)
                    if name == "va":
                        rstd_wait()
                        for g in range(G):
                            last = dve.scalar_tensor_tensor(
                                out=vns[:, g * P:(g + 1) * P], in0=vns[:, g * P:(g + 1) * P],
                                scalar=rstd[0:B, 32 + g:33 + g], in1=gain[0:B, g * P:(g + 1) * P],
                                op0=ALU.mult, op1=ALU.mult)
                        last.then_inc(s_vns, 1)
                        dve.wait_ge(s_vns, 1)
                        for g in range(G):
                            last = dve.tensor_scalar(obs[:, g * P:(g + 1) * P], vns[:, g * P:(g + 1) * P],
                                                     w00[:, g:g + 1], b00[:, g:g + 1], ALU.mult, ALU.add)
                        link(last)
                        dve.tensor_tensor(yas[:, :], yas[:, :], obs[:, :], ALU.mult).then_inc(s_yas, 1)
                    if name == "ga":
                        rstd_wait()
                        link(dve.scalar_tensor_tensor(out=yas[:, :], in0=yas[:, :], scalar=rstd[0:B, 36:37],
                                                      in1=vns[:, :], op0=ALU.mult, op1=ALU.mult))
                elif kind == "kt":
                    t = s[1]
                    n = tp_use[s]
                    wait_full(dve, tp_full, n)
                    dve.tensor_copy(kT[:, :, t * P:(t + 1) * P], TP[n % 2][:, :].rearrange("p (f q) -> p f q", f=4)
                                    ).then_inc(tp_free[n % 2], 1)
                elif kind == "sg":
                    t = s[1]
                    n = pa_use[s]
                    wait_full(dve, pa_full, n)
                    for g in range(G):
                        last = dve.scalar_tensor_tensor(
                            out=ya[:, t, g * P:(g + 1) * P], in0=PA[n % 2][:, g * P:(g + 1) * P],
                            scalar=sgub[:, g:g + 1], in1=ya[:, t, g * P:(g + 1) * P], op0=ALU.add, op1=ALU.mult)
                    last.then_inc(pa_free[n % 2], 1)
                elif kind == "qk":
                    h, i = s[1], s[2]
                    a = h * NT + i
                    n = pa_use[s]
                    if a >= 2:
                        wait_full(dve, tp_full, tp_use[("ptr",) + divmod(a - 2, NT)])
                    wait_full(dve, pa_full, n)
                    m = (i + 1) * P
                    dve.scalar_tensor_tensor(out=pr[:, a % 2, 0:m], in0=alibi[:, SEQ - m:SEQ], scalar=SLOPES[h],
                                             in1=PA[n % 2][:, 0:m], op0=ALU.mult, op1=ALU.add).then_inc(pa_free[n % 2], 1)
                    dve.wait_ge(pa_free[n % 2], n // 2 + 1)
                    dve.tensor_reduce(smax[:, a % 2:a % 2 + 1], pr[:, a % 2, 0:m], AX.X, ALU.max,
                                      negate=True).then_inc(s_pmax, 1)
                elif kind == "pv" and s[2] == NT - 1:
                    h = s[1]
                    if h == 0:
                        dve.wait_ge(s_krow_stored, 16 * (NT + 1))
                    dve.wait_ge(s_ptused, NT * (h + 1))
                    dve.wait_ge(s_pexp, NT * (h + 1))
                    link(dve.reciprocal(rinv[:, :], ssum[:, h, :]))
                    dve.tensor_tensor(yb[:, :, h * HD:(h + 1) * HD], PO[:, 0:NT * HD].rearrange("p (t d) -> p t d", t=NT),
                                      rinv[:, :].unsqueeze(2).broadcast_to([P, NT, HD]), ALU.mult).then_inc(po_free, 1)
                elif kind == "yt":
                    t, half = s[1], s[2]
                    n = tp_use[s]
                    wait_full(dve, tp_full, n)
                    dve.tensor_tensor(hT[:, 4 * half:4 * half + 4, t * P:(t + 1) * P],
                                      TP[n % 2][:, :].rearrange("p (k q) -> p k q", k=4),
                                      gab[:, 4 * half:4 * half + 4].unsqueeze(2).broadcast_to([P, 4, P]),
                                      ALU.mult).then_inc(tp_free[n % 2], 1)
                elif kind == "op":
                    t, half = s[1], s[2]
                    n = pa_use[s]
                    stage = (pr[:, :, :] if t % 2 == 0 else pT[:, :, :, :].rearrange("p a j q -> p a (j q)"))
                    dve.wait_ge(s_sq, sq_use[s] + 1)
                    if t == 0 and half == 0:
                        dve.wait_ge(s_xres, 16 * (NT + 1))
                    dve.tensor_tensor(stage[:, half, :], PA[n % 2][:, :], gpost[:, half * W:(half + 1) * W],
                                      ALU.mult).then_inc(pa_free[n % 2], 1)
                    if half == 1:
                        dve.tensor_tensor(msum[:, 41 + 2 * t:42 + 2 * t], msum[:, 40 + 2 * t:41 + 2 * t],
                                          msum[:, 41 + 2 * t:42 + 2 * t], ALU.add).then_inc(s_mso, 1)
                        rstd_wait()
                        dve.wait_ge(pa_free[n % 2], n // 2 + 1)
                        dve.scalar_tensor_tensor(out=xres[t], in0=stage, scalar=rstd[:, 41 + 2 * t:42 + 2 * t],
                                                 in1=xres[t], op0=ALU.mult, op1=ALU.add).then_inc(s_yo, 1)
                elif kind == "sn":
                    dve.wait_ge(dc_full, dc_use[s] + 1)
                    dve.tensor_copy(snT[:, :], DC[0:H, 0:B]).then_inc(dc_free, 1)
                elif kind == "qb":
                    b = s[1]
                    if b >= 1:
                        dve.wait_ge(s_mul, b)
                    dve.wait_ge(dc_full, dc_use[s] + 1)
                    dve.tensor_copy(qb[:, :], DC[:, :]).then_inc(dc_free, 1)
                elif kind == "dg":
                    b = s[1]
                    dve.wait_ge(dc_free, dc_use[("qb", b)] + 1)
                    dve.wait_ge(s_km, NB // 4 * (b + 1))
                    tmp = prod[:, :, :].rearrange("p a b -> p (a b)")[:, 0:W]
                    dve.tensor_tensor(tmp, KM[:, :], qb[:, :], ALU.mult).then_inc(km_free, 1)
                    dve.wait_ge(km_free, b + 1)
                    dve.tensor_reduce(gsum[:, :], tmp.rearrange("p (h d) -> p h d", h=H), AX.X, ALU.add).then_inc(s_gs, 1)
                elif kind == "gt":
                    b = s[1]
                    dve.wait_ge(dc_full, dc_use[s] + 1)
                    dve.tensor_copy(g16[:, :].rearrange("h (m j) -> h j m", j=4),
                                    DC[0:H, 0:P].rearrange("h (j x) -> h j x", j=4)[:, :, 0:4]).then_inc(dc_free, 1)
                    dve.wait_ge(dc_free, dc_use[s] + 1)
                    link(dve.max(top8[:, :], g16[:, :]))
                    link(dve.max_index(topi[:, :], top8[:, :], g16[:, :]))
                    link(dve.tensor_copy(vals[:, :, 0], topi[:, 0:TOP]))
                    link(dve.tensor_tensor(oneh[:, :, :], iota16[:, :].unsqueeze(1).broadcast_to([H, TOP, NB]),
                                           vals[:, :, 0:1].broadcast_to([H, TOP, NB]), ALU.is_equal))
                    for j in range(2):
                        last = dve.tensor_tensor(ohp[:, :, j, :], oneh[:, :, :],
                                                 ptbf[0:H, b, :, j].unsqueeze(1).broadcast_to([H, TOP, NB]), ALU.mult)
                    link(last)
                    link(dve.tensor_reduce(vals[:, :, 1:3], ohp[:, :, :, :], AX.X, ALU.add))
                    dve.tensor_tensor(spread[:, :, :], ident[0:H, 0:H].unsqueeze(2).broadcast_to([H, H, TOP * 3]),
                                      vals[:, :, :].rearrange("h k c -> h (k c)").unsqueeze(1).broadcast_to([H, H, TOP * 3]),
                                      ALU.mult).then_inc(s_spr, 1)
                elif kind == "bc":
                    b = s[1]
                    dve.wait_ge(dc_full, dc_use[s] + 1)
                    got = DC[:, 0:H * TOP * 3].rearrange("p (x c) -> p x c", c=3)
                    if b >= 1:
                        dve.wait_ge(s_v, 16 * H * TOP * 2 * b)
                    dve.tensor_copy(selni[0:1, :], got[0:1, :, 0])
                    dve.tensor_copy(selpi[0:1, :].rearrange("a (x j) -> a x j", j=2), got[0:1, :, 1:3]).then_inc(s_sel, 1)
                    dve.tensor_copy(seln[:, :, :].rearrange("p h k -> p (h k)"), got[:, :, 0]).then_inc(dc_free, 1)
                elif kind == "sr":
                    b, part = s[1], s[2]
                    if part < H - POOL_HEADS:
                        h = POOL_HEADS + part
                        dve.wait_ge(s_sel, b + 1)
                        regs = [dve.alloc_register(f"d{b}_{h}_{i}") for i in range(TOP)]
                        dve.load(regs, selni[0:1, h * TOP:(h + 1) * TOP])
                        for i in range(TOP):
                            n = dve.snap(regs[i], min_val=0, max_val=NB - 1)
                            last = dve.tensor_tensor(
                                dprod[:, h % 2, i, :, :], K[:, bass.ds(n, 1), :, h * HD:(h + 1) * HD]
                                .rearrange("p a r d -> p (a r) d"),
                                qb[:, h * HD:(h + 1) * HD].unsqueeze(1).broadcast_to([P, 2, HD]), ALU.mult)
                        for r in regs:
                            dve.free_register(r)
                        last.then_inc(s_dmul, 1)
                        dve.wait_ge(s_dmul, (H - POOL_HEADS) * b + part + 1)
                        if b >= 1:
                            dve.wait_ge(s_pex, b)
                        dve.tensor_reduce(sc[:, h, :, :], dprod[:, h % 2, :, :, :], AX.X, ALU.add).then_inc(s_red, 1)
                        continue
                    dve.wait_ge(s_mul, b + 1)
                    dve.tensor_reduce(sc[:, 0:POOL_HEADS, :, :],
                                      prod[:, 0:POOL_HEADS, :].rearrange("p a (i r d) -> p a i r d", i=TOP, r=2),
                                      AX.X, ALU.add).then_inc(s_red, 1)
                    dve.wait_ge(s_red, (H - POOL_HEADS + 1) * (b + 1))
                    link(dve.tensor_tensor(sc[:, :, :, :], sc[:, :, :, :],
                                           calibi[:, :, :].unsqueeze(2).broadcast_to([P, H, TOP, 2]), ALU.add))
                    link(dve.tensor_tensor(sbias[:, :, :], seln[:, :, :],
                                           slope256[:, :].unsqueeze(2).broadcast_to([P, H, TOP]), ALU.mult))
                    link(dve.tensor_tensor(sc[:, :, :, :], sc[:, :, :, :],
                                           sbias[:, :, :].unsqueeze(3).broadcast_to([P, H, TOP, 2]), ALU.add))
                    dve.tensor_reduce(mx[:, :], sc[:, :, :, :].rearrange("p h k r -> p h (k r)"), AX.X,
                                      ALU.max).then_inc(s_mxr, 1)
                elif kind == "mt":
                    b = s[1]
                    dve.wait_ge(dc_full, dc_use[s] + 1)
                    dve.tensor_reduce(mrow[:, :], DC[0:H, 0:P], AX.X, ALU.max).then_inc(dc_free, 1)
                    dve.wait_ge(dc_free, dc_use[s] + 1)
                    link(dve.tensor_tensor(MT[:, b:b + 1], mrow[:, :], snT[:, b:b + 1], ALU.max))
                    dve.tensor_scalar(dgm[:, :], ident[0:H, 0:H], MT[:, b:b + 1], None, ALU.mult).then_inc(s_dgm, 1)
                elif kind == "mb":
                    dve.wait_ge(dc_full, dc_use[s] + 1)
                    dve.tensor_tensor(sc[:, :, :, :].rearrange("p h k r -> p h (k r)"),
                                      sc[:, :, :, :].rearrange("p h k r -> p h (k r)"),
                                      DC[:, 0:H].unsqueeze(2).broadcast_to([P, H, TOP * 2]), ALU.subtract
                                      ).then_inc(dc_free, 1)
                elif kind == "pvd":
                    b = s[1]
                    dve.wait_ge(s_pex, b + 1)
                    dve.tensor_reduce(psm[:, :], pex[:, :, :, :].rearrange("p h k r -> p h (k r)"), AX.X,
                                      ALU.add).then_inc(s_psm, 1)
                    dve.wait_ge(dc_full, dc_use[s] + 1)
                    for j in range(4):
                        dve.tensor_copy(osb[32 * j:32 * j + 1, b, :], DC[32 * j:32 * j + 1, 0:2 * HD])
                    dve.tensor_copy(denr[0:1, b, :], DC[0:1, 2 * HD:2 * HD + H]).then_inc(dc_free, 1)
                elif kind == "fin0":
                    dve.tensor_tensor(pnT[:, :], snT[:, :], MT[:, :], ALU.subtract).then_inc(s_fin0, 1)
                    dve.wait_ge(dc_full, dc_use[s] + 1)
                    dve.tensor_copy(pn[:, :], DC[0:B, 0:H]).then_inc(dc_free, 1)
                    dve.wait_ge(dc_free, dc_use[s] + 1)
                    dve.wait_ge(s_obs, 16 * 6)
                    link(dve.tensor_tensor(den[:, :], den[:, :], pn[:, :], ALU.add))
                    link(dve.reciprocal(den[:, :], den[:, :]))
                    o3, v3 = (x[:, :].rearrange("b (h d) -> b h d", h=H) for x in (obs, vs))
                    dve.wait_ge(s_vrow_stored, 16 * (NT + 1))
                    link(dve.tensor_tensor(v3, v3, pn[:, :].unsqueeze(2).broadcast_to([B, H, HD]), ALU.mult))
                    link(dve.tensor_tensor(o3, o3, v3, ALU.add))
                    dve.tensor_tensor(o3, o3, den[:, :].unsqueeze(2).broadcast_to([B, H, HD]), ALU.mult
                                      ).then_inc(s_fin0, 1)
                elif kind == "fin2":
                    rstd_wait()
                    dve.scalar_tensor_tensor(out=obs[:, :], in0=obs[:, :], scalar=rstd[0:B, 37:38], in1=ks[:, :],
                                             op0=ALU.mult, op1=ALU.mult).then_inc(s_fin, 1)
                    n = tp_use[s]
                    wait_full(dve, tp_full, n)
                    dve.tensor_tensor(hTs[:, :, 0:B], TP[n % 2][:, 0:KC * B].rearrange("p (k b) -> p k b", k=KC),
                                      gab[:, :].unsqueeze(2).broadcast_to([P, KC, B]), ALU.mult).then_inc(tp_free[n % 2], 1)
                elif kind == "ffd" and s[1] == 1:
                    dve.wait_ge(s_sq, sq_use[s] + 1)
                    dve.wait_ge(s_xres, 16 * (NT + 1))
                    dve.tensor_tensor(msum[0:B, 39:40], msum[0:B, 38:39], msum[0:B, 39:40], ALU.add).then_inc(s_mso, 1)
                    rstd_wait()
                    for half, y in enumerate((yas, obs)):
                        last = dve.scalar_tensor_tensor(out=y[:, :], in0=y[:, :], scalar=rstd[0:B, 39:40],
                                                        in1=gpost[0:B, half * W:(half + 1) * W], op0=ALU.mult, op1=ALU.mult)
                    link(last)
                    for half, y in enumerate((yas, obs)):
                        x2 = xs2_sb[:, 2 * half:2 * half + 2, :]
                        last = dve.tensor_tensor(x2, x2, y[:, :].rearrange("b (a c) -> b a c", a=2), ALU.add)
                    last.then_inc(s_sout, 1)


_INS = ['x_prompt', 'x_sample', 'cache_k', 'cache_v', 'page_table', 'g_pre', 'w_in', 'sgu_gain', 'sgu_w',
        'sgu_b', 'g_branch_a', 'g_branch_b', 'w_out', 'g_post']
_OUTS = [(1, SEQ, D), (B, 1, D), (1, 1, SEQ, H, HD), (1, 1, SEQ, H, HD), (1, B, 1, H, HD), (1, B, 1, H, HD),
         (1, B, 1, W)]


def kernel(**inputs):
    import numpy as _np
    import concourse.bacc as _bacc
    from concourse import mybir as _mybir
    from concourse.bass_utils import run_bass_kernel_spmd as _run

    nc = _bacc.Bacc("TRN2", target_bir_lowering=False, num_devices=1, dynamic_dma_scratch_size=RING)
    arrays, args = {}, []
    for name in _INS:
        a = _np.ascontiguousarray(inputs[name])
        arrays[f"in_{name}"] = a
        args.append(nc.dram_tensor(f"in_{name}", a.shape, _mybir.dt.from_np(a.dtype), kind="ExternalInput").ap())
    for i, shape in enumerate(_OUTS):
        args.append(nc.dram_tensor(f"out_{i}", shape, F32, kind="ExternalOutput").ap())
    hymba_kernel(nc, *args)
    r = _run(nc, [arrays], core_ids=[0])
    return tuple(r.results[0][f"out_{i}"] for i in range(len(_OUTS)))
```

```python
import concourse.bass as bass
import concourse.mybir as mybir
from contextlib import ExitStack

F32 = mybir.dt.float32
BF16 = mybir.dt.bfloat16
I32 = mybir.dt.int32
U32 = mybir.dt.uint32
ALU = mybir.AluOpType
ACT = mybir.ActivationFunctionType
AX = mybir.AxisListType

P = 128
D = 1024
KC = D // P
SEQ = 512
NT = SEQ // P
B = 8
H, HD = 8, 64
W = 512
G = 4
PAST = 4096
PAGE = 128
NPAGE = PAST // PAGE
BLK = 256
NB = PAST // BLK
TOP = 3
ROWS = PAGE // 2
EPS = 1e-6
SCALE = HD ** -0.5
NEG = -1e30
RING = 4096
SLOPES = [2.0 ** -(h + 1) for h in range(H)]
CHUNKS = ["q", "k", "v", "u", "va", "ga", "gb"]
COL = {"u": 0, "va": 1, "ga": 2, "q": 3, "k": 4, "v": 5, "gb": 6}
SLOTS = 10
POOL_SHARE = 3


def of_pool(m):
    return m % POOL_SHARE == 1


def pool_count(m):
    return sum(map(of_pool, range(m)))


def sp_heads(b):
    return SP_HEADS if b < B - 1 else SP_LAST


def make_schedule():
    att = []
    pairs = [(h, i) for h in range(H) for i in range(NT)]
    for a in range(len(pairs) + 2):
        att.append(([("qk",) + pairs[a]] if a < len(pairs) else [])
                   + ([("ptr",) + pairs[a - 1]] if 1 <= a <= len(pairs) else [])
                   + ([("pv",) + pairs[a - 2]] if a >= 2 else []))
    pre = [("xn", t) for t in range(NT)] + [("xs",), ("spj", 0), ("sfd", 0), ("qb", 0)]
    out = []

    def chunk(c):
        steps = []
        name = CHUNKS[c]
        for t in range(NT):
            steps += [("pj0", c, t), ("pj", c, t)]
            if name == "k" and t >= 1:
                steps.append(("kt", t - 1))
            if name == "va" and t >= 1:
                steps.append(("sg", t - 1))
            if t == 0 and c == 0:
                steps.append(("wt",))
            if c == 0 and t >= 1:
                steps.append([("spj", 1), ("sfd", 1), ("sn",)][t - 1])
            if t <= 1 and c >= 2:
                steps.append((("spj", "sfd")[t], c))
        if name == "k":
            steps.append(("kt", NT - 1))
        if name == "va":
            steps.append(("sg", NT - 1))
        return steps

    def out_steps(t):
        return [("op0", t, 0), ("op", t, 0), ("op0", t, 1), ("op", t, 1)]
    prompt = chunk(0) + chunk(1) + chunk(2)
    rest = chunk(3) + chunk(4) + chunk(5)
    halves = [s[0] in ("pj0", "pj") for s in rest]
    n = done = 0
    for s, half in zip(rest, halves):
        prompt.append(s)
        done += half
        want = n + half if s[0] == "pj0" else done * len(att) // sum(halves)
        for group in att[n:want]:
            prompt += group
        n = max(n, want)
    prompt += chunk(6)
    for t in range(NT):
        prompt += [("yt", t, 0), ("yt", t, 1)]
        if t >= 1:
            prompt += out_steps(t - 1)
    prompt += out_steps(NT - 1)
    cost = {"pj0": 3.45, "pj": 3.45, "spj": 2.2, "sfd": 0.9, "kt": .9, "sg": 1.9, "qk": .8, "ptr": .5, "pv": .7,
            "sn": 0.1, "op0": 3.45, "op": 3.45, "yt": .9, "qb": .9, "ks": 0, "dg": 0, "gt": .1, "bc": .1, "mt": .1, "mb": .1,
            "pvd": 3.0, "fv": 0, "ld": 0, "fin0": .1, "fin1": 0, "fin2": .8, "fop": 2.2, "ffd": .9, "wt": .9, "xs": .8}
    events = []
    for b in range(B):
        t = START_US + PERIOD_US * b
        for n in range(NB):
            events.append((t + PERIOD_US * (n + 1) / NB, ("ks", b, n)))
        e = t + PERIOD_US
        chain = [(.01, ("dg", b)), (GT, ("gt", b)), (BC, ("bc", b)), (MT, ("mt", b)), (MB, ("mb", b)),
                 (PVD, ("pvd", b))]
        events += [(e + dt, s) for dt, s in chain]
        for k, h in enumerate(range(sp_heads(b), H)):
            events.append((e + BC + .1 + FV * k, ("fv", b, h)))
        if b >= 1:
            events.append((t - QB, ("qb", b)))
        if b == B - 1:
            events += [(e + PVD + dt, s) for dt, s in
                       ((FIN, ("fin0",)), (FIN + 4, ("fin1",)), (FIN + 8, ("fin2",)), (FIN + 12, ("fop", 0)),
                        (FIN + 15, ("ffd", 0)), (FIN + 15.1, ("fop", 1)), (FIN + 18, ("ffd", 1)))]
    events.sort(key=lambda x: x[0])
    now, res, k = 0.0, [], 0
    for s in prompt:
        while k < len(events) and events[k][0] <= now:
            res.append(events[k][1])
            now += cost[events[k][1][0]]
            k += 1
        res.append(s)
        now += cost[s[0]]
    res += [s for _, s in events[k:]]
    return pre + res


START_US, PERIOD_US = 1.24, 39.0
GT, BC, FV, MT, MB, QB, PVD = 2.44, 5.68, 9.0, 17.16, 28.24, 18.41, 53.07
FIN = 3.8
SP_HEADS, SP_LAST = 8, 5

def hymba_kernel(nc, x_prompt, x_sample, cache_k, cache_v, page_table, g_pre, w_in, sgu_gain, sgu_w,
                 sgu_b, g_branch_a, g_branch_b, w_out, g_post,
                 y_prompt, y_sample, k_prompt, v_prompt, k_sample, v_sample, sgu_v_sample):
    SCHEDULE = make_schedule()

    pa_use, tp_use = {}, {}
    for s in SCHEDULE:
        if s[0] in ("pj0", "op0"):
            pa_use[(s[0][:-1],) + s[1:]] = len(pa_use)
        if s[0] in ("sg", "qk"):
            pa_use[s] = len(pa_use)
        if s[0] in ("kt", "ptr", "yt", "wt", "xs"):
            tp_use[s] = len(tp_use)
        if s[0] == "xn":
            tp_use[s + (0,)] = len(tp_use)
            tp_use[s + (1,)] = len(tp_use)
        if s[0] == "fin2":
            tp_use[s] = len(tp_use)

    n_phys = cache_k.shape[1]
    k_rows = cache_k.rearrange("l g (p r) h d -> (l g p) (r h d)", r=2)
    v_pages = cache_v.rearrange("l g (p r) h d -> (l g) p r (h d)", r=2)
    x_rows = x_prompt.rearrange("b (t p) d -> (b t) p d", p=P)
    xs_rows = x_sample.rearrange("b t d -> (b t) d")
    y_rows = y_prompt.rearrange("b (t p) d -> (b t) p d", p=P)
    ys_rows = y_sample.rearrange("b t d -> (b t) d")
    kp_rows = k_prompt.rearrange("l b (t p) h d -> (l b t) p (h d)", p=P)
    vp_rows = v_prompt.rearrange("l b (t p) h d -> (l b t) p (h d)", p=P)
    ks_rows = k_sample.rearrange("l b t h d -> (l b t) (h d)")
    vs_rows = v_sample.rearrange("l b t h d -> (l b t) (h d)")
    sv_rows = sgu_v_sample.rearrange("l b t w -> (l b t) w")
    w_in_v = w_in.rearrange("l (k p) n -> p (l k) n", p=P)
    w_out_v = w_out.rearrange("l (k p) n -> p (l k) n", p=P)

    ctx = ExitStack()
    with ctx:
        def sb(name, shape, dt=F32):
            return ctx.enter_context(nc.sbuf_tensor(name, shape, dt))

        def pb(name):
            return ctx.enter_context(nc.psum_tensor(name, [P, 512], F32))

        def sem(name):
            return ctx.enter_context(nc.semaphore(name))

        K = sb("K", [P, SLOTS, 2, W])
        hT = sb("hT", [P, KC, SEQ])
        wbuf = sb("wbuf", [P, 2, KC, W])
        qT = sb("qT", [P, 4, SEQ])
        kT = sb("kT", [P, 4, SEQ])
        v = sb("v", [P, NT, W])
        yb = sb("yb", [P, NT, W])
        ya = sb("ya", [P, NT, W])
        vn = sb("vn", [P, 2, W])
        V = sb("V", [P, 2, H * TOP, 2, HD])
        prod = sb("prod", [P, 2, 2, W])
        pprod = sb("pprod", [P, 2, W])
        sall = sb("sall", [P, 2, NB, 2, H])
        gtmp = sb("gtmp", [H, NB, 2, H])
        spreado = sb("spreado", [H, H, TOP * NB])
        qb = sb("qb", [P, 2, W])
        pr = sb("pr", [P, 2, SEQ])
        pT = sb("pT", [P, 2, NT, P])
        nhalf = sb("nhalf", [P, G])
        junk = sb("junk", [P, D], BF16)
        ident = sb("ident", [P, P])
        alibi = sb("alibi", [P, SEQ])
        gain = sb("gain", [P, W])
        wsT = sb("wsT", [P, G, P])
        one = sb("one", [P, 1])
        gpre = sb("gpre", [P, KC])
        gab = sb("gab", [P, KC])
        sgub = sb("sgub", [P, G])
        hTs = sb("hTs", [P, KC, 32])
        spart = sb("spart", [P, W])
        fold = sb("fold", [P, B])
        qs = sb("qs", [B, W])
        ks = sb("ks", [B, W])
        vs = sb("vs", [B, W])
        yas = sb("yas", [B, W])
        vns = sb("vns", [B, W])
        obs = sb("obs", [B, W])
        osb = sb("osb", [P, B, 2 * HD])
        denr = sb("denr", [1, B, H])
        w00 = sb("w00", [B, G])
        b00 = sb("b00", [B, G])
        msum = sb("msum", [P, 48])
        rstd = sb("rstd", [P, 48])
        smax = sb("smax", [P, 2])
        ssum = sb("ssum", [P, H, NT])
        rinv = sb("rinv", [P, NT])
        kidx = sb("kidx", [P, B, NB], U32)
        poff = sb("poff", [P, 1])
        ptbf = sb("ptbf", [P, B, NB, 2])
        iota16 = sb("iota16", [H, NB])
        g16 = sb("g16", [H, NB])
        top8 = sb("top8", [H, 8])
        topi = sb("topi", [H, 8], U32)
        vals = sb("vals", [H, TOP, 3])
        oneh = sb("oneh", [H, TOP, NB])
        ohp = sb("ohp", [H, TOP, 2, NB])
        spread = sb("spread", [H, H, TOP * 3])
        selpi = sb("selpi", [1, 2, H * TOP * 2], I32)
        sc = sb("sc", [P, H, TOP, 2])
        sbias = sb("sbias", [P, H, TOP])
        calibi = sb("calibi", [P, H, 2])
        dist = sb("dist", [P, 2])
        slope256 = sb("slope256", [P, H])
        mx = sb("mx", [P, H])
        mrow = sb("mrow", [H, 1])
        MT = sb("MT", [H, B])
        dgm = sb("dgm", [H, H])
        pex = sb("pex", [P, H, TOP, 2])
        psm = sb("psm", [P, H])
        sn = sb("sn", [B, H])
        snT = sb("snT", [H, B])
        pnT = sb("pnT", [H, B])
        pn = sb("pn", [B, H])
        den = sb("den", [B, H])

        PA = [pb("PA0"), pb("PA1")]
        TP = [pb("TP0"), pb("TP1")]
        PO = pb("PO")
        SM = pb("SM")
        DC = pb("DC")

        s_xt = [sem(f"x_loaded{t}") for t in range(NT)]
        s_xs = sem("xs_loaded")
        s_w = [sem("w_loaded0"), sem("w_loaded1")]
        s_ws = sem("sgu_w_loaded")
        s_gpre = sem("g_pre_loaded")
        s_small = sem("small_loaded")
        s_pt = sem("page_table_loaded")
        s_ident = sem("identity_made")
        s_fold = sem("first_constants_made")
        s_const = sem("constants_made")
        s_k = [sem(f"k_block_loaded{n}") for n in range(SLOTS)]
        s_v = [sem("v_rows_loaded0"), sem("v_rows_loaded1")]
        s_store = sem("stored")
        s_dve = sem("dve_done")
        s_act = sem("act_done")
        s_pool = sem("pool_done")
        s_ms = sem("mean_square_ready")
        s_mso = sem("mean_square_of_y_ready")
        s_rs = sem("rstd_ready")
        pa_full = [sem("pa_full0"), sem("pa_full1")]
        pa_free = [sem("pa_free0"), sem("pa_free1")]
        tp_full = [sem("tp_full0"), sem("tp_full1")]
        tp_free = [sem("tp_free0"), sem("tp_free1")]
        sm_full, sm_free = sem("sm_full"), sem("sm_free")
        dc_full, dc_free = sem("dc_full"), sem("dc_free")
        po_free = sem("po_free")
        s_ptused = sem("p_transposed_used")
        s_vns_stored = sem("vns_stored")
        s_sq = sem("out_squared")
        s_xn = sem("x_scaled")
        s_vn = sem("vn_ready")
        s_pmax = sem("prompt_max_ready")
        s_pexp = sem("prompt_exp_ready")
        s_ydone = sem("y_gated")
        s_vrow_stored = sem("v_rows_stored")
        s_krow_stored = sem("k_rows_stored")
        s_snr = sem("sn_ready")
        s_spr = sem("spread_ready")
        s_sel = sem("selection_ready")
        s_pmul = sem("k_times_q_of_pool")
        s_dmul = sem("k_times_q_of_dve")
        s_red = sem("k_block_scored")
        s_mxr = sem("decode_max_ready")
        s_dgm = sem("max_diag_ready")
        s_pex = sem("decode_exp_ready")
        s_psm = sem("decode_sum_ready")
        s_obs = sem("decode_rows_gathered")
        s_yas = sem("yas_ready")
        s_fin0 = sem("new_token_steps")
        s_sout = sem("sample_out_ready")
        s_vns = sem("vns_ready")
        s_xres = sem("x_residual_loaded")
        s_yo = sem("y_tile_ready")
        s_fin = sem("fin_ready")
        s_pnT = sem("pnT_ready")

        block = ctx.enter_context(nc.Block())

        x_tile = [ya[:, 0:2, :], ya[:, 2:4, :], yb[:, 0:2, :], yb[:, 2:4, :]]
        def ones(rows, cols):
            return one[0:rows, :].broadcast_to([rows, cols])

        ptb = V[:, 0, 0:2, :, :].rearrange("p a r d -> p (a r d)").bitcast(I32).rearrange("p (b n j) -> p b n j", b=B, j=2)
        xs_sb = prod[0:B, 0, :, :].rearrange("p a b -> p (a b)")
        xs2_sb = prod[0:B, 0, :, :].rearrange("p a (b c) -> p (a b) c", b=2)
        xres = [qT[:, 0:2, :], qT[:, 2:4, :], kT[:, 0:2, :], kT[:, 2:4, :]]
        gpost = v[:, 0:2, :].rearrange("p a b -> p (a b)")
        ws_rows = pr[:, 0, :].rearrange("p (g s) -> p g s", g=G)
        WCH = len(CHUNKS) + 2
        krow_t = [yb[:, t, :] for t in range(NT)]

        def w_src(c):
            if c < len(CHUNKS):
                o = COL[CHUNKS[c]] * W
                return w_in_v[:, :, o:o + W]
            return w_out_v[:, :, (c - len(CHUNKS)) * W:(c - len(CHUNKS) + 1) * W]

        def wait_full(eng, full, n):
            eng.wait_ge(full[n % 2], n // 2 + 1)

        def wait_evac(eng, step):
            n = pa_use[step]
            eng.wait_ge(pa_free[n % 2], n // 2 + 1)

        def wait_tp_evac(eng, key):
            n = tp_use[key]
            eng.wait_ge(tp_free[n % 2], n // 2 + 1)

        def wait_free(eng, free, n):
            if n >= 2:
                eng.wait_ge(free[n % 2], n // 2)

        scored_at, score_no, product_slot, products = {}, {}, {}, 0
        for s in SCHEDULE:
            if s[0] in ("ks", "dg"):
                m = NB * s[1] + (s[2] if s[0] == "ks" else NB)
                due = [x for x in range(m) if x not in score_no
                       and (s[0] == "dg" or not of_pool(x) or x <= m - 2)]
                scored_at[s] = due
                for x in due:
                    score_no[x] = len(score_no)
                products += s[0] == "ks" and not of_pool(m)
            if s[0] == "bc":
                product_slot[s] = products % 2, len(score_no)
        sq_use = {}
        for s in SCHEDULE:
            if s[0] in ("op", "ffd"):
                sq_use[s] = len(sq_use)
        DCN = ["qb", "gt", "bc", "mt", "mb", "pvd"]
        dc_use = {}
        for s in SCHEDULE:
            if s[0] in DCN or s[0] in ("sn", "fin0"):
                dc_use[s] = len(dc_use)

        def fetch_v(eng, b, heads, name):
            eng.wait_ge(s_sel, b + 1)
            if b > 1:
                eng.wait_ge(dc_full, dc_use[("pvd", b - 2)] + 1)
            for h in heads:
                regs = [eng.alloc_register(f"{name}{b}_{h}_{i}") for i in range(TOP * 2)]
                eng.load(regs, selpi[0:1, b % 2, h * TOP * 2:(h + 1) * TOP * 2])
                for i in range(TOP * 2):
                    page = eng.snap(regs[i], min_val=0, max_val=n_phys - 1)
                    half = (i % 2) * ROWS
                    eng.dma_start(V[half:half + ROWS, b % 2, h * TOP + i // 2, :, :],
                                  v_pages[bass.ds(page, 1), :, :, h * HD:(h + 1) * HD]
                                  .rearrange("a p r d -> p (a r) d")).then_inc(s_v[b % 2], 16)
                for r in regs:
                    eng.free_register(r)

        @block.sync
        def _(sp):
            for t in range(NT):
                sp.dma_start(x_tile[t], x_rows[t].rearrange("p (a b) -> p a b", a=2)).then_inc(s_xt[t], 16)
            sp.dma_start(wbuf[:, 0, :, :], w_src(0)).then_inc(s_w[0], 16)
            sp.dma_start(xs_sb, xs_rows).then_inc(s_xs, 16)
            sp.dma_start(ws_rows, sgu_w.rearrange("l g t s -> t (l g) s")).then_inc(s_ws, 16)
            for dst, src in ((gab[:, 0:4], g_branch_a.rearrange("l (k p) -> p (l k)", p=P)),
                             (gab[:, 4:8], g_branch_b.rearrange("l (k p) -> p (l k)", p=P)),
                             (sgub[:, :], sgu_b.rearrange("l g t -> t (l g)")),
                             (w00[:, :], sgu_w[:, :, 0, 0].broadcast_to([B, G])),
                             (b00[:, :], sgu_b[:, :, 0].broadcast_to([B, G])),
                             (gain[:, :], sgu_gain.rearrange("l g c -> l (g c)").broadcast_to([P, W]))):
                sp.dma_start(dst, src, allow_slow_non_contiguous=True).then_inc(s_small, 16)
            sp.dma_start(wbuf[:, 1, :, :], w_src(1)).then_inc(s_w[1], 16)
            for s in SCHEDULE:
                if s[0] == "pj" and CHUNKS[s[1]] == "k":
                    t = s[2]
                    wait_evac(sp, s)
                    sp.dma_start(kp_rows[t], krow_t[t]).then_inc(s_krow_stored, 16)
                if s[0] == "pj" and CHUNKS[s[1]] == "v":
                    t = s[2]
                    wait_evac(sp, s)
                    sp.dma_start(vp_rows[t], v[:, t, :]).then_inc(s_vrow_stored, 16)
                if s[0] == "sfd" and CHUNKS[s[1]] in ("k", "v"):
                    sp.wait_ge(sm_free, 2 * s[1] + 2)
                    if CHUNKS[s[1]] == "k":
                        sp.dma_start(ks_rows, ks[:, :]).then_inc(s_krow_stored, 16)
                    else:
                        sp.dma_start(vs_rows, vs[:, :]).then_inc(s_vrow_stored, 16)
                if s[0] == "sfd" and CHUNKS[s[1]] == "va":
                    sp.wait_ge(s_vns, 1)
                    sp.dma_start(sv_rows, vns[:, :]).then_inc(s_vns_stored, 16)
                if s[0] == "bc":
                    fetch_v(sp, s[1], range(sp_heads(s[1])), "vs")
                if s[0] == "op" and s[2] == 1:
                    t = s[1]
                    sp.wait_ge(s_yo, t + 1)
                    sp.dma_start(y_rows[t], xres[t].rearrange("p a b -> p (a b)")).then_inc(s_store, 16)
                if s == ("pvd", B - 1):
                    sp.wait_ge(dc_free, dc_use[s] + 1)
                    for j in range(4):
                        sp.dma_start(obs[:, :].rearrange("b (t j d) -> b t j d", t=2, j=4)[:, :, j, :],
                                     osb[32 * j:32 * j + 1, :, :].rearrange("a b (t d) -> a b t d", t=2)
                                     ).then_inc(s_obs, 16)
                    sp.dma_start(den[:, :], denr[:, :, :]).then_inc(s_obs, 16)
                    sp.dma_start(xs2_sb, xs_rows.rearrange("b (a c) -> b a c", a=4)).then_inc(s_obs, 16)
            sp.wait_ge(s_sout, 1)
            sp.dma_start(ys_rows.rearrange("b (a c) -> b a c", a=4), xs2_sb).then_inc(s_store, 16)
            sp.wait_ge(s_krow_stored, 16 * (NT + 1))
            sp.wait_ge(s_vns_stored, 16)
            sp.wait_ge(s_vrow_stored, 16 * (NT + 1))
            sp.wait_ge(s_store, 16 * (NT + 1))

        @block.gpsimd
        def _(pool):
            n_pool = [0]

            def link(ins):
                n_pool[0] += 1
                ins.then_inc(s_pool, 1)
                pool.wait_ge(s_pool, n_pool[0])

            pool.dma_start(ptb.rearrange("p b n j -> p (b n j)"),
                           page_table.rearrange("(a b) n -> a (b n)", a=1).broadcast_to([P, B * NPAGE])).then_inc(s_pt, 16)
            link(pool.iota(poff[:, :], [[0, 1]], base=0, channel_multiplier=1, allow_small_or_imprecise_dtypes=True))
            link(pool.tensor_scalar_add(poff[ROWS:P, :], poff[ROWS:P, :], -float(ROWS)))
            link(pool.memset(ident[:, :], 0.0))
            pool.affine_select(out=ident[:, :], in_=ident[:, :], compare_op=ALU.not_equal, fill=1.0,
                               base=0, pattern=[[-1, P]], channel_multiplier=1).then_inc(s_ident, 1)
            link(pool.memset(nhalf[:, :], -0.5))
            link(pool.memset(one[:, :], 1.0))
            link(pool.memset(hTs[:, :, :], 0.0))
            link(pool.memset(fold[:, :], 0.0))
            for j in range(3):
                link(pool.affine_select(out=fold[:, :], in_=fold[:, :], compare_op=ALU.not_equal, fill=1.0,
                                        base=-32 * j, pattern=[[-1, B]], channel_multiplier=1))
            pool.affine_select(out=fold[:, :], in_=fold[:, :], compare_op=ALU.not_equal, fill=1.0,
                               base=-32 * 3, pattern=[[-1, B]], channel_multiplier=1).then_inc(s_fold, 1)
            pool.wait_ge(s_pt, 16)
            link(pool.tensor_copy(ptbf[:, :, :, :], ptb))
            for j in range(2):
                p0 = j * ROWS
                link(pool.tensor_scalar(kidx[p0:p0 + ROWS, :, :], ptbf[p0:p0 + ROWS, :, :, j], float(ROWS),
                                        poff[p0:p0 + ROWS, 0:1], ALU.mult, ALU.add))

            def load_k(m):
                last = m - SLOTS
                if last >= 0 and of_pool(last):
                    pool.wait_ge(s_pmul, pool_count(last + 1))
                elif last >= 0:
                    pool.wait_ge(s_dmul, last + 1 - pool_count(last + 1))
                b, n = divmod(m, NB)
                pool.indirect_dma_start(K[:, m % SLOTS, :, :].rearrange("p r w -> p (r w)"), None, k_rows,
                                        bass.IndirectOffsetOnAxis(ap=kidx[:, b, n:n + 1], axis=0)
                                        ).then_inc(s_k[m % SLOTS], 16)

            n_ms = [0]

            n_mso = [0]

            def make_rstd(rows, col, n=1, of_y=False):
                count, ready = (n_mso, s_mso) if of_y else (n_ms, s_ms)
                count[0] += 1
                pool.wait_ge(ready, count[0])
                at = slice(col, col + n)
                link(pool.tensor_scalar_add(rstd[0:rows, at], msum[0:rows, at], EPS))
                pool.tensor_tensor(rstd[0:rows, at], rstd[0:rows, at], nhalf[0:rows, 0:n], ALU.pow).then_inc(s_rs, 1)

            for t in range(NT):
                make_rstd(P, t)
            for n in range(4):
                load_k(n)
            make_rstd(B, 4)
            link(pool.iota(alibi[:, :], [[1, SEQ]], base=-(SEQ - P), channel_multiplier=-1,
                           allow_small_or_imprecise_dtypes=True))
            link(pool.affine_select(out=alibi[:, :], in_=alibi[:, :], compare_op=ALU.is_ge, fill=NEG,
                                    base=SEQ - P, pattern=[[-1, SEQ]], channel_multiplier=1))
            link(pool.iota(dist[:, :], [[1, 2]], base=-PAST, channel_multiplier=2,
                           allow_small_or_imprecise_dtypes=True))
            for h in range(H):
                link(pool.tensor_scalar(calibi[:, h, :], dist[:, :], SLOPES[h], None, ALU.mult))
                link(pool.memset(slope256[:, h:h + 1], SLOPES[h] * BLK))
            link(pool.iota(iota16[:, :], [[1, NB]], base=0, channel_multiplier=0,
                           allow_small_or_imprecise_dtypes=True))
            pool.wait_ge(s_ws, 16)
            for g in range(G):
                link(pool.affine_select(out=ws_rows[:, g, :], in_=ws_rows[:, g, :], compare_op=ALU.is_ge,
                                        fill=0.0, base=0, pattern=[[-1, P]], channel_multiplier=1))
            pool.wait_ge(s_small, 16 * 6)
            pool.memset(osb[:, :, :], 0.0).then_inc(s_const, 1)
            for n in range(4, SLOTS - 1):
                load_k(n)

            for s in SCHEDULE:
                if s[0] == "pj" and CHUNKS[s[1]] == "va":
                    make_rstd(P, 8 + 4 * s[2], 4)
                if s[0] == "pj" and CHUNKS[s[1]] == "ga":
                    make_rstd(P, 24 + s[2])
                if s[0] == "pj" and CHUNKS[s[1]] == "gb":
                    make_rstd(P, 28 + s[2])
                if s[0] == "sfd" and CHUNKS[s[1]] == "va":
                    make_rstd(B, 32, 4)
                if s[0] == "sfd" and CHUNKS[s[1]] == "ga":
                    make_rstd(B, 36)
                if s[0] == "op" and s[2] == 1:
                    make_rstd(P, 41 + 2 * s[1], of_y=True)
                if s[0] == "fin1":
                    make_rstd(B, 37)
                if s == ("ffd", 1):
                    make_rstd(B, 39, of_y=True)
                if s[0] == "ks":
                    b, n = s[1], s[2]
                    m = NB * b + n
                    if of_pool(m):
                        pool.wait_ge(s_k[m % SLOTS], 16 * (m // SLOTS + 1))
                        pool.wait_ge(dc_free, dc_use[("qb", b)] + 1)
                        if pool_count(m) >= 1:
                            pool.wait_ge(s_red, score_no[m - POOL_SHARE] + 1)
                        pool.tensor_tensor(pprod[:, :, :], K[:, m % SLOTS, :, :],
                                           qb[:, b % 2, :].unsqueeze(1).broadcast_to([P, 2, W]), ALU.mult
                                           ).then_inc(s_pmul, 1)
                    if m + SLOTS - 1 < B * NB:
                        load_k(m + SLOTS - 1)

        @block.tensor
        def _(pe):
            pe.wait_ge(s_ident, 1)
            n_dc = [0]

            def dc_begin(s):
                if dc_use[s] >= 1:
                    pe.wait_ge(dc_free, dc_use[s])

            n_sm = [0]

            def sm_begin():
                if n_sm[0] >= 1:
                    pe.wait_ge(sm_free, n_sm[0])
                n_sm[0] += 1

            def sample_partials(w, src):
                for kc in range(KC):
                    j = kc % 4
                    last = pe.matmul(SM[32 * j:32 * j + 32, :], src[:, kc, :], w[:, kc, :],
                                     start=(kc < 4), stop=(kc >= 4), tile_position=(0, 32 * j))
                last.then_inc(sm_full, 1)

            for s in SCHEDULE:
                kind = s[0]
                if kind == "wt":
                    n = tp_use[s]
                    pe.wait_ge(s_const, 1)
                    wait_free(pe, tp_free, n)
                    for g in range(G):
                        last = pe.transpose(TP[n % 2][:, g * P:(g + 1) * P], ws_rows[:, g, :], ident[:, :])
                    last.then_inc(tp_full[n % 2], 1)
                elif kind == "xn":
                    t = s[1]
                    pe.wait_ge(s_xn, t + 1)
                    for half in range(2):
                        n = tp_use[s + (half,)]
                        wait_free(pe, tp_free, n)
                        for i in range(4):
                            last = pe.transpose(TP[n % 2][:, i * P:(i + 1) * P],
                                                x_tile[t][:, half, i * P:(i + 1) * P], ident[:, :])
                        last.then_inc(tp_full[n % 2], 1)
                elif kind == "xs":
                    pe.wait_ge(s_fold, 1)
                    pe.wait_ge(s_xn, NT + 1)
                    n = tp_use[s]
                    wait_free(pe, tp_free, n)
                    for kc in range(KC):
                        last = pe.transpose(TP[n % 2][:, kc * B:(kc + 1) * B],
                                            xs_sb[:, kc * P:(kc + 1) * P], ident[0:B, 0:B])
                    last.then_inc(tp_full[n % 2], 1)
                elif kind in ("pj0", "pj"):
                    c, t = s[1], s[2]
                    n = pa_use[("pj", c, t)]
                    if kind == "pj0":
                        if t == 0:
                            pe.wait_ge(s_w[c % 2], 16 * (c // 2 + 1))
                            if c == 0:
                                for par in range(2):
                                    last_n = max(tp_use[k] for k in tp_use if k[0] == "xn" and tp_use[k] % 2 == par)
                                    pe.wait_ge(tp_free[par], last_n // 2 + 1)
                        wait_free(pe, pa_free, n)
                    for kc in (range(KC // 2) if kind == "pj0" else range(KC // 2, KC)):
                        if CHUNKS[c] == "q":
                            lhs, rhs = wbuf[:, c % 2, kc, t * P:(t + 1) * P], hT[:, kc, :]
                        else:
                            lhs, rhs = hT[:, kc, t * P:(t + 1) * P], wbuf[:, c % 2, kc, :]
                        last = pe.matmul(PA[n % 2][:, :], lhs, rhs, start=(kc == 0), stop=(kc == KC - 1))
                    if kind == "pj":
                        last.then_inc(pa_full[n % 2], 1)
                elif kind == "spj":
                    c = s[1]
                    sm_begin()
                    if c <= 1:
                        pe.wait_ge(s_w[c], 16)
                    if c == 0:
                        wait_tp_evac(pe, ("xs",))
                    sample_partials(wbuf[:, c % 2, :, :], hTs)
                elif kind == "sfd":
                    sm_begin()
                    pe.matmul(SM[0:B, :], fold[:, :], spart[:, :], start=True, stop=True).then_inc(sm_full, 1)
                elif kind == "kt":
                    t = s[1]
                    wait_evac(pe, ("pj", 1, t))
                    n = tp_use[s]
                    wait_free(pe, tp_free, n)
                    for i in range(4):
                        last = pe.transpose(TP[n % 2][:, i * P:(i + 1) * P], krow_t[t][:, i * P:(i + 1) * P], ident[:, :])
                    last.then_inc(tp_full[n % 2], 1)
                elif kind == "sg":
                    t = s[1]
                    pe.wait_ge(s_vn, t + 1)
                    n = pa_use[s]
                    wait_free(pe, pa_free, n)
                    for g in range(G):
                        last = pe.matmul(PA[n % 2][:, g * P:(g + 1) * P], wsT[:, g, :],
                                         vn[:, t % 2, g * P:(g + 1) * P], start=True, stop=True)
                    last.then_inc(pa_full[n % 2], 1)
                elif kind == "qk":
                    h, i = s[1], s[2]
                    if (h, i) == (0, 0):
                        for t in (NT - 2, NT - 1):
                            n = tp_use[("kt", t)]
                            pe.wait_ge(tp_free[n % 2], n // 2 + 1)
                    n = pa_use[s]
                    wait_free(pe, pa_free, n)
                    o = 64 * (h % 2)
                    pe.matmul(PA[n % 2][:, 0:(i + 1) * P], qT[o:o + HD, h // 2, i * P:(i + 1) * P],
                              kT[o:o + HD, h // 2, 0:(i + 1) * P], start=True, stop=True,
                              tile_position=(o, 0)).then_inc(pa_full[n % 2], 1)
                elif kind == "ptr":
                    h, i = s[1], s[2]
                    a = h * NT + i
                    pe.wait_ge(s_pexp, a + 1)
                    n = tp_use[s]
                    wait_free(pe, tp_free, n)
                    for jt in range(i + 1):
                        last = pe.transpose(TP[n % 2][:, jt * P:(jt + 1) * P], pr[:, a % 2, jt * P:(jt + 1) * P], ident[:, :])
                    last.then_inc(tp_full[n % 2], 1)
                elif kind == "pv":
                    h, i = s[1], s[2]
                    a = h * NT + i
                    n = tp_use[("ptr", h, i)]
                    pe.wait_ge(tp_free[n % 2], n // 2 + 1)
                    if a == 0:
                        for t in (NT - 2, NT - 1):
                            wait_evac(pe, ("pj", 2, t))
                    if i == 0 and h >= 1:
                        pe.wait_ge(po_free, h)
                    for jt in range(i + 1):
                        last = pe.matmul(PO[:, i * HD:(i + 1) * HD], pT[:, a % 2, jt, :],
                                         v[:, jt, h * HD:(h + 1) * HD], start=(jt == 0), stop=(jt == i))
                    last.then_inc(s_ptused, 1)
                elif kind == "yt":
                    t, half = s[1], s[2]
                    if half == 0:
                        pe.wait_ge(s_ydone, NT + t + 1)
                    n = tp_use[s]
                    wait_free(pe, tp_free, n)
                    src = (ya if half == 0 else yb)
                    for i in range(4):
                        last = pe.transpose(TP[n % 2][:, i * P:(i + 1) * P], src[:, t, i * P:(i + 1) * P], ident[:, :])
                    last.then_inc(tp_full[n % 2], 1)
                elif kind in ("op0", "op"):
                    t, half = s[1], s[2]
                    c = len(CHUNKS) + half
                    n = pa_use[("op", t, half)]
                    if kind == "op0":
                        if t == 0:
                            pe.wait_ge(s_w[c % 2], 16 * (c // 2 + 1))
                        if half == 0:
                            for hf in range(2):
                                m = tp_use[("yt", t, hf)]
                                pe.wait_ge(tp_free[m % 2], m // 2 + 1)
                        wait_free(pe, pa_free, n)
                    for kc in (range(KC // 2) if kind == "op0" else range(KC // 2, KC)):
                        last = pe.matmul(PA[n % 2][:, :], hT[:, kc, t * P:(t + 1) * P], wbuf[:, c % 2, kc, :],
                                         start=(kc == 0), stop=(kc == KC - 1))
                    if kind == "op":
                        last.then_inc(pa_full[n % 2], 1)
                elif kind == "sn":
                    dc_begin(s)
                    pe.wait_ge(s_snr, 1)
                    pe.transpose(DC[0:H, 0:B], sn[:, :], ident[0:B, 0:B]).then_inc(dc_full, 1)
                elif kind == "qb":
                    b = s[1]
                    dc_begin(s)
                    pe.wait_ge(sm_free, 2)
                    pe.matmul(DC[:, :], ident[0:B, b:b + 1].broadcast_to([B, P]), qs[:, :],
                              start=True, stop=True).then_inc(dc_full, 1)
                elif kind == "gt":
                    dc_begin(s)
                    pe.wait_ge(s_red, NB * (s[1] + 1))
                    pe.matmul(DC[0:H, 0:NB * 2 * H], ones(P, H), sall[:, s[1] % 2, :, :, :].rearrange("p n r h -> p (n r h)"),
                              start=True, stop=True).then_inc(dc_full, 1)
                elif kind == "bc":
                    dc_begin(s)
                    pe.wait_ge(s_spr, s[1] + 1)
                    pe.matmul(DC[:, 0:H * TOP * 3], ones(H, P), spread[:, :, :].rearrange("p a b -> p (a b)"),
                              start=True, stop=True)
                    pe.matmul(DC[:, H * TOP * 3:H * TOP * (3 + NB)], ones(H, P),
                              spreado[:, :, :].rearrange("p a b -> p (a b)"), start=True, stop=True).then_inc(dc_full, 1)
                elif kind == "mt":
                    dc_begin(s)
                    pe.wait_ge(s_mxr, s[1] + 1)
                    pe.transpose(DC[0:H, 0:P], mx[:, :], ident[:, :]).then_inc(dc_full, 1)
                elif kind == "mb":
                    dc_begin(s)
                    pe.wait_ge(s_dgm, s[1] + 1)
                    pe.matmul(DC[:, 0:H], ones(H, P), dgm[:, :], start=True, stop=True).then_inc(dc_full, 1)
                elif kind == "pvd":
                    b = s[1]
                    dc_begin(s)
                    pe.wait_ge(s_pex, b + 1)
                    pe.wait_ge(s_v[b % 2], 16 * H * TOP * 2 * (b // 2 + 1))
                    for hh in range(2):
                        for i in range(TOP):
                            for r in range(2):
                                for j in range(4):
                                    h = 4 * hh + j
                                    pe.matmul(DC[32 * j:32 * j + 32, hh * HD:(hh + 1) * HD],
                                              pex[:, h, i, r:r + 1].broadcast_to([P, 32]),
                                              V[:, b % 2, h * TOP + i, r, :], start=(i == 0 and r == 0),
                                              stop=(i == TOP - 1 and r == 1), tile_position=(0, 32 * j))
                    pe.wait_ge(s_psm, b + 1)
                    pe.matmul(DC[0:1, 2 * HD:2 * HD + H], ones(P, 1), psm[:, :], start=True, stop=True).then_inc(dc_full, 1)
                elif kind == "fin0":
                    dc_begin(s)
                    pe.wait_ge(s_pnT, 1)
                    pe.transpose(DC[0:B, 0:H], pnT[:, :], ident[0:H, 0:H]).then_inc(dc_full, 1)
                elif kind == "fin2":
                    pe.wait_ge(s_fin, 1)
                    n = tp_use[s]
                    wait_free(pe, tp_free, n)
                    for kc in range(KC):
                        src = yas if kc < 4 else obs
                        last = pe.transpose(TP[n % 2][:, kc * B:(kc + 1) * B], src[:, (kc % 4) * P:(kc % 4 + 1) * P], ident[0:B, 0:B])
                    last.then_inc(tp_full[n % 2], 1)
                elif kind == "fop":
                    half = s[1]
                    if half == 0:
                        n = tp_use[("fin2",)]
                        pe.wait_ge(tp_free[n % 2], n // 2 + 1)
                    sm_begin()
                    sample_partials(wbuf[:, (len(CHUNKS) + half) % 2, :, :], hTs)
                elif kind == "ffd":
                    sm_begin()
                    pe.matmul(SM[0:B, :], fold[:, :], spart[:, :], start=True, stop=True).then_inc(sm_full, 1)

        @block.scalar
        def _(act):
            act.dma_start(gpre[:, :], g_pre.rearrange("l (k p) -> p (l k)", p=P),
                          allow_slow_non_contiguous=True).then_inc(s_gpre, 16)
            n_act = [0]

            def link(ins):
                n_act[0] += 1
                ins.then_inc(s_act, 1)
                act.wait_ge(s_act, n_act[0])

            squared = []

            def mean_square(src, rows, col, width, n, done, at=0):
                if squared and at == 0:
                    act.wait_ge(*squared[-1])
                squared.append((done, n))
                return act.activation(junk[0:rows, at:at + src.shape[-1]], src, ACT.Square,
                                      scale=float(width) ** -0.5, accum_out=msum[0:rows, col:col + 1])

            n_ms, n_sq = [0], [0]

            def mean_squares(src, rows, col, width):
                n_ms[0] += 1
                mean_square(src, rows, col, width, n_ms[0], s_ms).then_inc(s_ms, 1)

            def group_squares(src, rows, col):
                n_ms[0] += 1
                for g in range(G):
                    last = mean_square(src[:, g * P:(g + 1) * P], rows, col + g, P, n_ms[0], s_ms, at=g * P)
                last.then_inc(s_ms, 1)

            def half_square(src, rows, col):
                n_sq[0] += 1
                mean_square(src, rows, col, D, n_sq[0], s_sq).then_inc(s_sq, 1)

            for s in SCHEDULE:
                kind = s[0]
                if kind == "pj" and s[2] == NT - 1 and s[1] + 2 < WCH:
                    c = s[1] + 2
                    wait_full(act, pa_full, pa_use[s])
                    act.dma_start(wbuf[:, c % 2, :, :], w_src(c)).then_inc(s_w[c % 2], 16)
                if s == ("pv", H - 1, NT - 1):
                    act.wait_ge(s_ptused, H * NT)
                    for t in range(NT):
                        act.dma_start(xres[t], x_rows[t].rearrange("p (a b) -> p a b", a=2)).then_inc(s_xres, 16)
                    act.dma_start(gpost, g_post.broadcast_to([P, D])).then_inc(s_xres, 16)
                if kind == "xn":
                    t = s[1]
                    for i in range(NT if t == 0 else 0):
                        act.wait_ge(s_xt[i], 16)
                        mean_squares(x_tile[i].rearrange("p a b -> p (a b)"), P, i, D)
                    act.wait_ge(s_rs, t + 1)
                    act.activation(x_tile[t], x_tile[t], ACT.Copy, scale=rstd[:, t:t + 1]).then_inc(s_xn, 1)
                    if t == NT - 1:
                        act.wait_ge(s_xs, 16)
                        mean_squares(xs_sb, B, 4, D)
                elif kind == "xs":
                    act.wait_ge(s_rs, NT + 1)
                    act.activation(xs_sb, xs_sb, ACT.Copy, scale=rstd[0:B, 4:5]).then_inc(s_xn, 1)
                elif kind == "pj":
                    c, t = s[1], s[2]
                    name = CHUNKS[c]
                    n = pa_use[s]
                    if name == "va" and t >= 2:
                        wait_full(act, pa_full, pa_use[("sg", t - 2)])
                    if name == "ga" and t < 2:
                        wait_full(act, pa_full, pa_use[("sg", NT - 2 + t)])
                    if name in ("ga", "gb") and (name, t) not in (("ga", 0), ("ga", 1)):
                        act.wait_ge(s_ydone, (c - 5) * NT + t - 1)
                    wait_full(act, pa_full, n)
                    bank = PA[n % 2][:, :]
                    dst, fn, sc_ = {"q": (qT[:, t, :], ACT.Copy, SCALE), "k": (yb[:, t, :], ACT.Copy, 1.0),
                                    "v": (v[:, t, :], ACT.Copy, 1.0), "u": (ya[:, t, :], ACT.Gelu_apprx_tanh, 1.0),
                                    "va": (vn[:, t % 2, :], ACT.Gelu_apprx_tanh, 1.0),
                                    "ga": (vn[:, t % 2, :], ACT.Silu, 1.0),
                                    "gb": (vn[:, t % 2, :], ACT.Silu, 1.0)}[name]
                    act.activation(dst, bank, fn, scale=sc_).then_inc(pa_free[n % 2], 1)
                    if name == "va":
                        act.wait_ge(pa_free[n % 2], n // 2 + 1)
                        group_squares(vn[:, t % 2, :], P, 8 + 4 * t)
                    if name == "ga":
                        wait_evac(act, ("sg", t))
                        mean_squares(ya[:, t, :], P, 24 + t, W)
                    if name == "gb":
                        act.wait_ge(po_free, H)
                        mean_squares(yb[:, t, :], P, 28 + t, W)
                elif kind == "sfd":
                    c = s[1]
                    name = CHUNKS[c]
                    act.wait_ge(sm_full, 2 * c + 2)
                    if name == "ga":
                        act.wait_ge(s_vns_stored, 16)
                        act.wait_ge(s_yas, 1)
                    if name == "gb":
                        act.wait_ge(s_krow_stored, 16 * (NT + 1))
                        act.wait_ge(s_snr, 1)
                    dst, fn, sc_ = {"q": (qs, ACT.Copy, SCALE), "k": (ks, ACT.Copy, 1.0), "v": (vs, ACT.Copy, 1.0),
                                    "u": (yas, ACT.Gelu_apprx_tanh, 1.0), "va": (vns, ACT.Gelu_apprx_tanh, 1.0),
                                    "ga": (vns, ACT.Silu, 1.0), "gb": (ks, ACT.Silu, 1.0)}[name]
                    act.activation(dst[:, :], SM[0:B, :], fn, scale=sc_).then_inc(sm_free, 1)
                    if name == "va":
                        act.wait_ge(sm_free, 2 * c + 2)
                        group_squares(vns[:, :], B, 32)
                    if name == "ga":
                        mean_squares(yas[:, :], B, 36, W)
                elif kind == "qk":
                    h, i = s[1], s[2]
                    a = h * NT + i
                    act.wait_ge(s_pmax, a + 1)
                    act.activation(pr[:, a % 2, 0:(i + 1) * P], pr[:, a % 2, 0:(i + 1) * P], ACT.Exp,
                                   bias=smax[:, a % 2:a % 2 + 1], accum_out=ssum[:, h, i:i + 1]).then_inc(s_pexp, 1)
                elif kind == "ptr":
                    h, i = s[1], s[2]
                    a = h * NT + i
                    n = tp_use[s]
                    wait_full(act, tp_full, n)
                    if a >= 2:
                        act.wait_ge(s_ptused, a - 1)
                    act.copy(pT[:, a % 2, 0:i + 1, :], TP[n % 2][:, 0:(i + 1) * P].rearrange("p (j q) -> p j q", q=P)
                             ).then_inc(tp_free[n % 2], 1)
                elif kind == "fv":
                    fetch_v(act, s[1], [s[2]], "va")
                elif kind == "mb":
                    act.wait_ge(dc_free, dc_use[s] + 1)
                    act.activation(pex[:, :, :, :], sc[:, :, :, :], ACT.Exp).then_inc(s_pex, 1)
                elif kind == "op":
                    t, half = s[1], s[2]
                    n = pa_use[s]
                    wait_full(act, pa_full, n)
                    half_square(PA[n % 2][:, :], P, 40 + 2 * t + half)
                elif kind in ("spj", "fop"):
                    c = s[1] if kind == "spj" else len(CHUNKS) + s[1]
                    act.wait_ge(sm_full, 2 * c + 1)
                    act.copy(spart[:, :], SM[:, :]).then_inc(sm_free, 1)
                elif kind == "kt":
                    t = s[1]
                    n = tp_use[s]
                    wait_full(act, tp_full, n)
                    act.copy(kT[:, :, t * P:(t + 1) * P], TP[n % 2][:, :].rearrange("p (f q) -> p f q", f=4)
                             ).then_inc(tp_free[n % 2], 1)
                elif kind == "qb":
                    b = s[1]
                    if b >= 2:
                        m = NB * (b - 1)
                        act.wait_ge(s_pmul, pool_count(m))
                        act.wait_ge(s_dmul, m - pool_count(m))
                    act.wait_ge(dc_full, dc_use[s] + 1)
                    act.copy(qb[:, b % 2, :], DC[:, :]).then_inc(dc_free, 1)
                elif kind == "pvd":
                    b = s[1]
                    act.wait_ge(dc_full, dc_use[s] + 1)
                    act.copy(denr[0:1, b, :], DC[0:1, 2 * HD:2 * HD + H])
                    act.copy(osb[:, b, :], DC[:, 0:2 * HD]).then_inc(dc_free, 1)
                elif kind == "fin0":
                    act.wait_ge(s_fin0, 1)
                    act.activation(pnT[:, :], pnT[:, :], ACT.Exp).then_inc(s_pnT, 1)
                elif kind == "fin1":
                    act.wait_ge(s_fin0, 2)
                    mean_squares(obs[:, :], B, 37, W)
                elif kind == "ffd":
                    half = s[1]
                    act.wait_ge(sm_full, 2 * len(CHUNKS) + 2 * half + 2)
                    dst = (yas if half == 0 else obs)
                    act.copy(dst[:, :], SM[0:B, :]).then_inc(sm_free, 1)
                    act.wait_ge(sm_free, 2 * len(CHUNKS) + 2 * half + 2)
                    half_square(dst[:, :], B, 38 + half)

        @block.vector
        def _(dve):
            n_dve = [0]

            def link(ins):
                n_dve[0] += 1
                ins.then_inc(s_dve, 1)
                dve.wait_ge(s_dve, n_dve[0])

            n_rs = [0]

            def rstd_wait():
                n_rs[0] += 1
                dve.wait_ge(s_rs, n_rs[0])

            def score(x):
                b, n = divmod(x, NB)
                if of_pool(x):
                    dve.wait_ge(s_pmul, pool_count(x + 1))
                    src = pprod[:, :, :]
                else:
                    dve.wait_ge(s_dmul, x + 1 - pool_count(x))
                    src = prod[:, (x - pool_count(x)) % 2, :, :]
                dve.tensor_reduce(sall[:, b % 2, n, :, :], src.rearrange("p r (h d) -> p r h d", h=H),
                                  AX.X, ALU.add).then_inc(s_red, 1)

            for s in SCHEDULE:
                kind = s[0]
                if kind == "wt":
                    dve.wait_ge(s_const, 1)
                    n = tp_use[s]
                    wait_full(dve, tp_full, n)
                    dve.tensor_copy(wsT[:, :, :], TP[n % 2][:, :].rearrange("p (g t) -> p g t", g=G)
                                    ).then_inc(tp_free[n % 2], 1)
                elif kind == "xn":
                    t = s[1]
                    n_rs[0] += 1
                    for half in range(2):
                        n = tp_use[s + (half,)]
                        wait_full(dve, tp_full, n)
                        if t == 0 and half == 0:
                            dve.wait_ge(s_gpre, 16)
                        dve.tensor_tensor(hT[:, 4 * half:4 * half + 4, t * P:(t + 1) * P],
                                          TP[n % 2][:, :].rearrange("p (k q) -> p k q", k=4),
                                          gpre[:, 4 * half:4 * half + 4].unsqueeze(2).broadcast_to([P, 4, P]),
                                          ALU.mult).then_inc(tp_free[n % 2], 1)
                elif kind == "xs":
                    n_rs[0] += 1
                    dve.wait_ge(s_fold, 1)
                    n = tp_use[s]
                    wait_full(dve, tp_full, n)
                    dve.tensor_tensor(hTs[:, :, 0:B], TP[n % 2][:, 0:KC * B].rearrange("p (k b) -> p k b", k=KC),
                                      gpre[:, :].unsqueeze(2).broadcast_to([P, KC, B]),
                                      ALU.mult).then_inc(tp_free[n % 2], 1)
                elif kind == "pj":
                    c, t = s[1], s[2]
                    name = CHUNKS[c]
                    if name == "va":
                        rstd_wait()
                        for g in range(G):
                            last = dve.scalar_tensor_tensor(
                                out=vn[:, t % 2, g * P:(g + 1) * P], in0=vn[:, t % 2, g * P:(g + 1) * P],
                                scalar=rstd[:, 8 + 4 * t + g:9 + 4 * t + g], in1=gain[:, g * P:(g + 1) * P],
                                op0=ALU.mult, op1=ALU.mult)
                        last.then_inc(s_vn, 1)
                    if name in ("ga", "gb"):
                        y, col = (ya, 24 + t) if name == "ga" else (yb, 28 + t)
                        rstd_wait()
                        dve.scalar_tensor_tensor(out=y[:, t, :], in0=y[:, t, :], scalar=rstd[:, col:col + 1],
                                                 in1=vn[:, t % 2, :], op0=ALU.mult, op1=ALU.mult).then_inc(s_ydone, 1)
                elif kind == "sfd":
                    name = CHUNKS[s[1]]
                    if name == "k":
                        dve.wait_ge(sm_free, 2 * s[1] + 2)
                        link(dve.tensor_tensor(obs[:, :], qs[:, :], ks[:, :], ALU.mult))
                        dve.tensor_reduce(sn[:, :], obs[:, :].rearrange("b (h d) -> b h d", h=H), AX.X,
                                          ALU.add).then_inc(s_snr, 1)
                    if name == "va":
                        rstd_wait()
                        for g in range(G):
                            last = dve.scalar_tensor_tensor(
                                out=vns[:, g * P:(g + 1) * P], in0=vns[:, g * P:(g + 1) * P],
                                scalar=rstd[0:B, 32 + g:33 + g], in1=gain[0:B, g * P:(g + 1) * P],
                                op0=ALU.mult, op1=ALU.mult)
                        last.then_inc(s_vns, 1)
                        dve.wait_ge(s_vns, 1)
                        for g in range(G):
                            last = dve.tensor_scalar(obs[:, g * P:(g + 1) * P], vns[:, g * P:(g + 1) * P],
                                                     w00[:, g:g + 1], b00[:, g:g + 1], ALU.mult, ALU.add)
                        link(last)
                        dve.tensor_tensor(yas[:, :], yas[:, :], obs[:, :], ALU.mult).then_inc(s_yas, 1)
                    if name == "ga":
                        rstd_wait()
                        link(dve.scalar_tensor_tensor(out=yas[:, :], in0=yas[:, :], scalar=rstd[0:B, 36:37],
                                                      in1=vns[:, :], op0=ALU.mult, op1=ALU.mult))
                elif kind == "sg":
                    t = s[1]
                    n = pa_use[s]
                    wait_full(dve, pa_full, n)
                    for g in range(G):
                        last = dve.scalar_tensor_tensor(
                            out=ya[:, t, g * P:(g + 1) * P], in0=PA[n % 2][:, g * P:(g + 1) * P],
                            scalar=sgub[:, g:g + 1], in1=ya[:, t, g * P:(g + 1) * P], op0=ALU.add, op1=ALU.mult)
                    last.then_inc(pa_free[n % 2], 1)
                elif kind == "qk":
                    h, i = s[1], s[2]
                    a = h * NT + i
                    n = pa_use[s]
                    if a >= 2:
                        wait_full(dve, tp_full, tp_use[("ptr",) + divmod(a - 2, NT)])
                    wait_full(dve, pa_full, n)
                    m = (i + 1) * P
                    dve.scalar_tensor_tensor(out=pr[:, a % 2, 0:m], in0=alibi[:, SEQ - m:SEQ], scalar=SLOPES[h],
                                             in1=PA[n % 2][:, 0:m], op0=ALU.mult, op1=ALU.add).then_inc(pa_free[n % 2], 1)
                    dve.wait_ge(pa_free[n % 2], n // 2 + 1)
                    dve.tensor_reduce(smax[:, a % 2:a % 2 + 1], pr[:, a % 2, 0:m], AX.X, ALU.max,
                                      negate=True).then_inc(s_pmax, 1)
                elif kind == "pv" and s[2] == NT - 1:
                    h = s[1]
                    if h == 0:
                        dve.wait_ge(s_krow_stored, 16 * (NT + 1))
                    dve.wait_ge(s_ptused, NT * (h + 1))
                    dve.wait_ge(s_pexp, NT * (h + 1))
                    link(dve.reciprocal(rinv[:, :], ssum[:, h, :]))
                    dve.tensor_tensor(yb[:, :, h * HD:(h + 1) * HD], PO[:, 0:NT * HD].rearrange("p (t d) -> p t d", t=NT),
                                      rinv[:, :].unsqueeze(2).broadcast_to([P, NT, HD]), ALU.mult).then_inc(po_free, 1)
                elif kind == "yt":
                    t, half = s[1], s[2]
                    n = tp_use[s]
                    wait_full(dve, tp_full, n)
                    dve.tensor_tensor(hT[:, 4 * half:4 * half + 4, t * P:(t + 1) * P],
                                      TP[n % 2][:, :].rearrange("p (k q) -> p k q", k=4),
                                      gab[:, 4 * half:4 * half + 4].unsqueeze(2).broadcast_to([P, 4, P]),
                                      ALU.mult).then_inc(tp_free[n % 2], 1)
                elif kind == "op":
                    t, half = s[1], s[2]
                    n = pa_use[s]
                    stage = (pr[:, :, :] if t % 2 == 0 else pT[:, :, :, :].rearrange("p a j q -> p a (j q)"))
                    dve.wait_ge(s_sq, sq_use[s] + 1)
                    if t == 0 and half == 0:
                        dve.wait_ge(s_xres, 16 * (NT + 1))
                    dve.tensor_tensor(stage[:, half, :], PA[n % 2][:, :], gpost[:, half * W:(half + 1) * W],
                                      ALU.mult).then_inc(pa_free[n % 2], 1)
                    if half == 1:
                        dve.tensor_tensor(msum[:, 41 + 2 * t:42 + 2 * t], msum[:, 40 + 2 * t:41 + 2 * t],
                                          msum[:, 41 + 2 * t:42 + 2 * t], ALU.add).then_inc(s_mso, 1)
                        rstd_wait()
                        dve.wait_ge(pa_free[n % 2], n // 2 + 1)
                        dve.scalar_tensor_tensor(out=xres[t], in0=stage, scalar=rstd[:, 41 + 2 * t:42 + 2 * t],
                                                 in1=xres[t], op0=ALU.mult, op1=ALU.add).then_inc(s_yo, 1)
                elif kind == "sn":
                    dve.wait_ge(dc_full, dc_use[s] + 1)
                    dve.tensor_copy(snT[:, :], DC[0:H, 0:B]).then_inc(dc_free, 1)
                elif kind == "ks":
                    b, n = s[1], s[2]
                    m = NB * b + n
                    if not of_pool(m):
                        if n == 0 or (n == 1 and of_pool(NB * b)):
                            dve.wait_ge(dc_free, dc_use[("qb", b)] + 1)
                        dve.wait_ge(s_k[m % SLOTS], 16 * (m // SLOTS + 1))
                        slot = (m - pool_count(m)) % 2
                        before = [x for x in range(m) if not of_pool(x)][-2:-1]
                        if before:
                            dve.wait_ge(s_red, score_no[before[0]] + 1)
                        dve.tensor_tensor(prod[:, slot, :, :], K[:, m % SLOTS, :, :],
                                          qb[:, b % 2, :].unsqueeze(1).broadcast_to([P, 2, W]), ALU.mult
                                          ).then_inc(s_dmul, 1)
                    for x in scored_at[s]:
                        score(x)
                elif kind == "dg":
                    for x in scored_at[s]:
                        score(x)
                elif kind == "gt":
                    b = s[1]
                    dve.wait_ge(dc_full, dc_use[s] + 1)
                    dve.tensor_tensor(gtmp[:, :, :, :].rearrange("h n r x -> h (n r) x"),
                                      DC[0:H, 0:NB * 2 * H].rearrange("h (a x) -> h a x", x=H),
                                      ident[0:H, 0:H].unsqueeze(1).broadcast_to([H, NB * 2, H]), ALU.mult
                                      ).then_inc(dc_free, 1)
                    dve.wait_ge(dc_free, dc_use[s] + 1)
                    link(dve.tensor_reduce(g16[:, :], gtmp[:, :, :, :].rearrange("h n r x -> h n (r x)"), AX.X, ALU.add))
                    link(dve.max(top8[:, :], g16[:, :]))
                    link(dve.max_index(topi[:, :], top8[:, :], g16[:, :]))
                    link(dve.tensor_copy(vals[:, :, 0], topi[:, 0:TOP]))
                    link(dve.tensor_tensor(oneh[:, :, :], iota16[:, :].unsqueeze(1).broadcast_to([H, TOP, NB]),
                                           vals[:, :, 0:1].broadcast_to([H, TOP, NB]), ALU.is_equal))
                    for j in range(2):
                        last = dve.tensor_tensor(ohp[:, :, j, :], oneh[:, :, :],
                                                 ptbf[0:H, b, :, j].unsqueeze(1).broadcast_to([H, TOP, NB]), ALU.mult)
                    link(last)
                    link(dve.tensor_reduce(vals[:, :, 1:3], ohp[:, :, :, :], AX.X, ALU.add))
                    dve.tensor_tensor(spreado[:, :, :], ident[0:H, 0:H].unsqueeze(2).broadcast_to([H, H, TOP * NB]),
                                      oneh[:, :, :].rearrange("h k n -> h (k n)").unsqueeze(1).broadcast_to([H, H, TOP * NB]),
                                      ALU.mult)
                    dve.tensor_tensor(spread[:, :, :], ident[0:H, 0:H].unsqueeze(2).broadcast_to([H, H, TOP * 3]),
                                      vals[:, :, :].rearrange("h k c -> h (k c)").unsqueeze(1).broadcast_to([H, H, TOP * 3]),
                                      ALU.mult).then_inc(s_spr, 1)
                elif kind == "bc":
                    b = s[1]
                    dve.wait_ge(dc_full, dc_use[s] + 1)
                    got = DC[:, 0:H * TOP * 3].rearrange("p (x c) -> p x c", c=3)
                    if b >= 2:
                        dve.wait_ge(s_v[b % 2], 16 * H * TOP * 2 * (b // 2))
                    if b >= 1:
                        dve.wait_ge(s_pex, b)
                    dve.tensor_copy(selpi[0:1, b % 2, :].rearrange("a (x j) -> a x j", j=2), got[0:1, :, 1:3]).then_inc(s_sel, 1)
                    hot = DC[:, H * TOP * 3:H * TOP * (3 + NB)].rearrange("p (h k n) -> p h k n", h=H, n=NB)
                    slot, sums = product_slot[s]
                    dve.wait_ge(s_red, sums)
                    got_s = prod[:, slot, :, :].rearrange("p a b -> p (a b)")[:, 0:2 * H * TOP * NB]
                    got_s = got_s.rearrange("p (r h k n) -> p r h k n", r=2, h=H, n=NB)
                    for r in range(2):
                        dve.tensor_tensor(got_s[:, r, :, :, :], hot,
                                          sall[:, b % 2, :, r, :].rearrange("p n h -> p h n").unsqueeze(2)
                                          .broadcast_to([P, H, TOP, NB]), ALU.mult)
                    dve.tensor_tensor(sbias[:, :, :], got[:, :, 0].rearrange("p (h k) -> p h k", h=H),
                                      slope256[:, :].unsqueeze(2).broadcast_to([P, H, TOP]), ALU.mult
                                      ).then_inc(dc_free, 1)
                    dve.wait_ge(dc_free, dc_use[s] + 1)
                    last = dve.tensor_reduce(sc[:, :, :, :].rearrange("p h k r -> p r (h k)"),
                                             got_s.rearrange("p r h k n -> p r (h k) n"), AX.X, ALU.add)
                    link(last)
                    link(dve.tensor_tensor(sc[:, :, :, :], sc[:, :, :, :],
                                           calibi[:, :, :].unsqueeze(2).broadcast_to([P, H, TOP, 2]), ALU.add))
                    link(dve.tensor_tensor(sc[:, :, :, :], sc[:, :, :, :],
                                           sbias[:, :, :].unsqueeze(3).broadcast_to([P, H, TOP, 2]), ALU.add))
                    dve.tensor_reduce(mx[:, :], sc[:, :, :, :].rearrange("p h k r -> p h (k r)"), AX.X,
                                      ALU.max).then_inc(s_mxr, 1)
                elif kind == "mt":
                    b = s[1]
                    dve.wait_ge(dc_full, dc_use[s] + 1)
                    dve.tensor_reduce(mrow[:, :], DC[0:H, 0:P], AX.X, ALU.max).then_inc(dc_free, 1)
                    dve.wait_ge(dc_free, dc_use[s] + 1)
                    link(dve.tensor_tensor(MT[:, b:b + 1], mrow[:, :], snT[:, b:b + 1], ALU.max))
                    dve.tensor_scalar(dgm[:, :], ident[0:H, 0:H], MT[:, b:b + 1], None, ALU.mult).then_inc(s_dgm, 1)
                elif kind == "mb":
                    dve.wait_ge(dc_full, dc_use[s] + 1)
                    dve.tensor_tensor(sc[:, :, :, :].rearrange("p h k r -> p h (k r)"),
                                      sc[:, :, :, :].rearrange("p h k r -> p h (k r)"),
                                      DC[:, 0:H].unsqueeze(2).broadcast_to([P, H, TOP * 2]), ALU.subtract
                                      ).then_inc(dc_free, 1)
                elif kind == "pvd":
                    b = s[1]
                    dve.wait_ge(s_pex, b + 1)
                    dve.tensor_reduce(psm[:, :], pex[:, :, :, :].rearrange("p h k r -> p h (k r)"), AX.X,
                                      ALU.add).then_inc(s_psm, 1)
                elif kind == "fin0":
                    dve.tensor_tensor(pnT[:, :], snT[:, :], MT[:, :], ALU.subtract).then_inc(s_fin0, 1)
                    dve.wait_ge(dc_full, dc_use[s] + 1)
                    dve.tensor_copy(pn[:, :], DC[0:B, 0:H]).then_inc(dc_free, 1)
                    dve.wait_ge(dc_free, dc_use[s] + 1)
                    dve.wait_ge(s_obs, 16 * 6)
                    link(dve.tensor_tensor(den[:, :], den[:, :], pn[:, :], ALU.add))
                    link(dve.reciprocal(den[:, :], den[:, :]))
                    o3, v3 = (x[:, :].rearrange("b (h d) -> b h d", h=H) for x in (obs, vs))
                    dve.wait_ge(s_vrow_stored, 16 * (NT + 1))
                    link(dve.tensor_tensor(v3, v3, pn[:, :].unsqueeze(2).broadcast_to([B, H, HD]), ALU.mult))
                    link(dve.tensor_tensor(o3, o3, v3, ALU.add))
                    dve.tensor_tensor(o3, o3, den[:, :].unsqueeze(2).broadcast_to([B, H, HD]), ALU.mult
                                      ).then_inc(s_fin0, 1)
                elif kind == "fin1":
                    n_rs[0] += 1
                    fin_rs = n_rs[0]
                elif kind == "fin2":
                    dve.wait_ge(s_rs, fin_rs)
                    dve.scalar_tensor_tensor(out=obs[:, :], in0=obs[:, :], scalar=rstd[0:B, 37:38], in1=ks[:, :],
                                             op0=ALU.mult, op1=ALU.mult).then_inc(s_fin, 1)
                    n = tp_use[s]
                    wait_full(dve, tp_full, n)
                    dve.tensor_tensor(hTs[:, :, 0:B], TP[n % 2][:, 0:KC * B].rearrange("p (k b) -> p k b", k=KC),
                                      gab[:, :].unsqueeze(2).broadcast_to([P, KC, B]), ALU.mult).then_inc(tp_free[n % 2], 1)
                elif kind == "ffd" and s[1] == 1:
                    dve.wait_ge(s_sq, sq_use[s] + 1)
                    dve.wait_ge(s_xres, 16 * (NT + 1))
                    dve.tensor_tensor(msum[0:B, 39:40], msum[0:B, 38:39], msum[0:B, 39:40], ALU.add).then_inc(s_mso, 1)
                    rstd_wait()
                    for half, y in enumerate((yas, obs)):
                        last = dve.scalar_tensor_tensor(out=y[:, :], in0=y[:, :], scalar=rstd[0:B, 39:40],
                                                        in1=gpost[0:B, half * W:(half + 1) * W], op0=ALU.mult, op1=ALU.mult)
                    link(last)
                    for half, y in enumerate((yas, obs)):
                        x2 = xs2_sb[:, 2 * half:2 * half + 2, :]
                        last = dve.tensor_tensor(x2, x2, y[:, :].rearrange("b (a c) -> b a c", a=2), ALU.add)
                    last.then_inc(s_sout, 1)


_INS = ['x_prompt', 'x_sample', 'cache_k', 'cache_v', 'page_table', 'g_pre', 'w_in', 'sgu_gain', 'sgu_w',
        'sgu_b', 'g_branch_a', 'g_branch_b', 'w_out', 'g_post']
_OUTS = [(1, SEQ, D), (B, 1, D), (1, 1, SEQ, H, HD), (1, 1, SEQ, H, HD), (1, B, 1, H, HD), (1, B, 1, H, HD),
         (1, B, 1, W)]


def kernel(**inputs):
    import numpy as _np
    import concourse.bacc as _bacc
    from concourse import mybir as _mybir
    from concourse.bass_utils import run_bass_kernel_spmd as _run

    nc = _bacc.Bacc("TRN2", target_bir_lowering=False, num_devices=1, dynamic_dma_scratch_size=RING)
    arrays, args = {}, []
    for name in _INS:
        a = _np.ascontiguousarray(inputs[name])
        arrays[f"in_{name}"] = a
        args.append(nc.dram_tensor(f"in_{name}", a.shape, _mybir.dt.from_np(a.dtype), kind="ExternalInput").ap())
    for i, shape in enumerate(_OUTS):
        args.append(nc.dram_tensor(f"out_{i}", shape, F32, kind="ExternalOutput").ap())
    hymba_kernel(nc, *args)
    r = _run(nc, [arrays], core_ids=[0])
    return tuple(r.results[0][f"out_{i}"] for i in range(len(_OUTS)))
```
